# Optimizing a Trainium2 kernel written in Bass

```python
import jax, jax.numpy as jnp
from jax import lax
import numpy as np

D_MODEL = 1024
BATCH = 1
SEQ = 128
DEPTH = 1
DEC_BATCH = 1
DEC_SEQ = 1024
PAST_LEN = 256

GRID_W = 64
HEAD_DIM = 64
N_HEADS = D_MODEL // HEAD_DIM
N_KV_HEADS = N_HEADS // 4
KV_GROUP = N_HEADS // N_KV_HEADS
ROPE_THETA = 10000.0
Q_BLOCK = 128
R_DK = 128
R_HEADS = D_MODEL // R_DK
R_DV = D_MODEL // R_HEADS
CHUNK = 64
D_FF = 2816
EPS = 1e-6
ATT_W = N_HEADS * HEAD_DIM
KV_W = N_KV_HEADS * HEAD_DIM
REC_K = R_HEADS * R_DK
REC_V = R_HEADS * R_DV
IN_WIDTHS = (ATT_W, KV_W, KV_W, REC_K, REC_K, REC_K, REC_V, REC_V, D_MODEL, D_MODEL)
IN_W = sum(IN_WIDTHS)
IN_SPLITS = tuple(int(s) for s in np.cumsum(IN_WIDTHS)[:-1])

kernel_name = "hybrid_gqa_hgrn2_diffusion_step"

def rmsnorm(x, gain):
    xf = x.astype(jnp.float32)
    y = xf * lax.rsqrt(jnp.mean(xf * xf, axis=-1, keepdims=True) + EPS)
    return (y * gain.astype(jnp.float32)).astype(x.dtype)

def axial_angles(n_tokens):
    rows = n_tokens // GRID_W
    row = jnp.repeat(jnp.arange(rows, dtype=jnp.float32), GRID_W)
    col = jnp.tile(jnp.arange(GRID_W, dtype=jnp.float32), rows)
    half = HEAD_DIM // 2
    inv_freq = 1.0 / (ROPE_THETA ** (jnp.arange(0, half, 2, dtype=jnp.float32) / half))
    return row[:, None] * inv_freq, col[:, None] * inv_freq

def _rotate(xa, ang):
    x1, x2 = jnp.split(xa, 2, axis=-1)
    cos = jnp.cos(ang)[None, :, None, :]
    sin = jnp.sin(ang)[None, :, None, :]
    return jnp.concatenate([x1 * cos - x2 * sin, x1 * sin + x2 * cos], axis=-1)

def apply_axial_rope(x, ang_row, ang_col):
    xf = x.astype(jnp.float32)
    half = HEAD_DIM // 2
    return jnp.concatenate([_rotate(xf[..., :half], ang_row), _rotate(xf[..., half:], ang_col)], axis=-1).astype(x.dtype)

def block_attention(q, k, v):
    B, Lq = q.shape[0], q.shape[1]
    nb = Lq // Q_BLOCK
    qb = q.reshape(B, nb, Q_BLOCK, N_KV_HEADS, KV_GROUP, HEAD_DIM).transpose(1, 0, 2, 3, 4, 5)
    kf = k.astype(jnp.float32)
    vf = v.astype(jnp.float32)
    scale = HEAD_DIM ** -0.5

    def one_block(qblk):
        s = jnp.einsum("bqkgd,bskd->bkgqs", qblk.astype(jnp.float32), kf) * scale
        p = jax.nn.softmax(s, axis=-1)
        return jnp.einsum("bkgqs,bskd->bqkgd", p, vf)

    o = lax.map(one_block, qb)
    return o.transpose(1, 0, 2, 3, 4, 5).reshape(B, Lq, ATT_W).astype(q.dtype)

def chunk_recurrence(q, k, v, g, s0):
    B, L, H, _ = q.shape
    DV = v.shape[-1]
    nc = L // CHUNK

    def to_chunks(a):
        return a.reshape(B, nc, CHUNK, H, a.shape[-1]).transpose(1, 0, 3, 2, 4)

    causal = jnp.tril(jnp.ones((CHUNK, CHUNK), jnp.float32))

    def step(S, inp):
        qc, kc, vc, gc = inp
        b = jnp.cumsum(gc, axis=2)
        b_last = b[:, :, -1:, :]
        q_dec = qc * jnp.exp(b)
        k_dec = kc * jnp.exp(-b)
        scores = jnp.einsum("bhtk,bhsk->bhts", q_dec, k_dec) * causal
        o = jnp.einsum("bhts,bhsv->bhtv", scores, vc) + jnp.einsum("bhtk,bhkv->bhtv", q_dec, S)
        S_new = jnp.exp(b_last[:, :, 0, :])[..., None] * S + jnp.einsum("bhsk,bhsv->bhkv", kc * jnp.exp(b_last - b), vc)
        return S_new, o

    S_fin, o = lax.scan(step, s0.astype(jnp.float32), (to_chunks(q), to_chunks(k), to_chunks(v), to_chunks(g)))
    return o.transpose(1, 0, 3, 2, 4).reshape(B, L, H, DV), S_fin

def token_mixer(h, w_in, w_o, q_gain, k_gain, r_gain, lb, ang_row, ang_col, ctx_k, ctx_v, s0_fwd, s0_bwd):
    B, L, _ = h.shape
    f32 = jnp.float32
    aq, ak, av, rq, rf_fwd, rf_bwd, ri, rg, za, zr = jnp.split(h @ w_in, IN_SPLITS, axis=-1)
    q = rmsnorm(aq.reshape(B, L, N_HEADS, HEAD_DIM), q_gain)
    k = rmsnorm(ak.reshape(B, L, N_KV_HEADS, HEAD_DIM), k_gain)
    v = av.reshape(B, L, N_KV_HEADS, HEAD_DIM)
    if ctx_k is None:
        k_all, v_all = k, v
    else:
        q = apply_axial_rope(q, ang_row, ang_col)
        k = apply_axial_rope(k, ang_row, ang_col)
        k_all = jnp.concatenate([k, ctx_k.astype(k.dtype)], axis=1)
        v_all = jnp.concatenate([v, ctx_v.astype(v.dtype)], axis=1)
    attn = block_attention(q, k_all, v_all)
    rqf = jax.nn.silu(rq.astype(f32)).reshape(B, L, R_HEADS, R_DK) * (R_DK ** -0.5)
    rif = ri.astype(f32).reshape(B, L, R_HEADS, R_DV)

    def gates(zf, lb_d):
        f = lb_d + (1.0 - lb_d) * jax.nn.sigmoid(zf.astype(f32).reshape(B, L, R_HEADS, R_DK))
        return 1.0 - f, jnp.log(f)

    k_f, g_f = gates(rf_fwd, lb[0])
    k_b, g_b = gates(rf_bwd, lb[1])
    if s0_fwd is None:
        s0_fwd = jnp.zeros((B, R_HEADS, R_DK, R_DV), f32)
        s0_bwd = jnp.zeros((B, R_HEADS, R_DK, R_DV), f32)
    o_f, S_f = chunk_recurrence(rqf, k_f, rif, g_f, s0_fwd)
    o_b, S_b = chunk_recurrence(rqf[:, ::-1], k_b[:, ::-1], rif[:, ::-1], g_b[:, ::-1], s0_bwd)
    o_rec = rmsnorm(o_f + o_b[:, ::-1], r_gain) * jax.nn.silu(rg.astype(f32)).reshape(B, L, R_HEADS, R_DV)
    rec = o_rec.reshape(B, L, REC_V).astype(h.dtype)
    merged = jax.nn.sigmoid(za) * attn + jax.nn.sigmoid(zr) * rec
    return merged @ w_o, k, v, S_f, S_b

def conv_ffn(h, w_up, conv_w, conv_b, w_down):
    u = h @ w_up
    up = jnp.pad(u, ((0, 0), (1, 1), (0, 0)))
    u = up[:, :-2] * conv_w[0] + up[:, 1:-1] * conv_w[1] + up[:, 2:] * conv_w[2] + conv_b
    a, b = jnp.split(u, 2, axis=-1)
    return (jax.nn.silu(a) * b) @ w_down

def adaln(cond, w, b):
    mod = (jax.nn.silu(cond) @ w + b).reshape(cond.shape[0], 6, D_MODEL)
    return tuple(mod[:, i][:, None, :] for i in range(6))

def setup_inputs(seed: int = 0) -> dict:
    key = jax.random.key(seed)
    ks = jax.random.split(key, 24)
    d = D_MODEL

    def nrm(k, shape, s):
        return jax.random.normal(k, shape, jnp.float32) * s

    return {
        "x_prompt": nrm(ks[0], (BATCH, SEQ, d), 1.0),
        "x_sample": nrm(ks[1], (DEC_BATCH, DEC_SEQ, d), 1.0),
        "c": nrm(ks[2], (DEC_BATCH, d), 1.0),
        "cache_k": nrm(ks[3], (DEC_BATCH, DEPTH, PAST_LEN, N_KV_HEADS, HEAD_DIM), 1.0),
        "cache_v": nrm(ks[4], (DEC_BATCH, DEPTH, PAST_LEN, N_KV_HEADS, HEAD_DIM), 1.0),
        "state_hgrn": nrm(ks[5], (DEC_BATCH, DEPTH, 2, R_HEADS, R_DK, R_DV), 0.5),
        "c_ctx": nrm(ks[6], (d,), 1.0),
        "ada_w": nrm(ks[7], (DEPTH, d, 6 * d), 0.5 * d ** -0.5),
        "ada_b": nrm(ks[8], (DEPTH, 6 * d), 0.02),
        "norm1": 1.0 + nrm(ks[9], (DEPTH, d), 0.02),
        "norm2": 1.0 + nrm(ks[10], (DEPTH, d), 0.02),
        "w_in": nrm(ks[11], (DEPTH, d, IN_W), d ** -0.5),
        "q_norm": 1.0 + nrm(ks[12], (DEPTH, HEAD_DIM), 0.02),
        "k_norm": 1.0 + nrm(ks[13], (DEPTH, HEAD_DIM), 0.02),
        "hgrn_lb_logits": nrm(ks[14], (2, DEPTH + 1, REC_K), 0.1),
        "hgrn_norm": 1.0 + nrm(ks[15], (DEPTH, R_DV), 0.02),
        "w_o": nrm(ks[16], (DEPTH, d, d), d ** -0.5),
        "w_up": nrm(ks[17], (DEPTH, d, 2 * D_FF), d ** -0.5),
        "conv_w": nrm(ks[18], (DEPTH, 3, 2 * D_FF), 3 ** -0.5),
        "conv_b": nrm(ks[19], (DEPTH, 2 * D_FF), 0.02),
        "w_down": nrm(ks[20], (DEPTH, D_FF, d), D_FF ** -0.5),
        "final_norm": 1.0 + nrm(ks[21], (d,), 0.02),
    }

def reference(x_prompt, x_sample, c, cache_k, cache_v, state_hgrn, c_ctx, ada_w, ada_b, norm1, norm2,
              w_in, q_norm, k_norm, hgrn_lb_logits, hgrn_norm, w_o, w_up, conv_w, conv_b, w_down, final_norm):
    lb_all = jnp.cumsum(jax.nn.softmax(hgrn_lb_logits.astype(jnp.float32), axis=1), axis=1)
    ang_row, ang_col = axial_angles(x_sample.shape[1])
    xp, xs = x_prompt, x_sample
    new_k, new_v, new_s = [], [], []
    for l in range(DEPTH):
        lb = lb_all[:, l].reshape(2, R_HEADS, R_DK)
        sh1, sc1, g1, sh2, sc2, g2 = adaln(c_ctx[None, :], ada_w[l], ada_b[l])
        h = rmsnorm(xp, norm1[l]) * (1.0 + sc1) + sh1
        out, k_c, v_c, s_f, s_b = token_mixer(h, w_in[l], w_o[l], q_norm[l], k_norm[l], hgrn_norm[l], lb,
                                              None, None, None, None, None, None)
        xp = xp + g1 * out
        h = rmsnorm(xp, norm2[l]) * (1.0 + sc2) + sh2
        xp = xp + g2 * conv_ffn(h, w_up[l], conv_w[l], conv_b[l], w_down[l])
        new_k.append(k_c)
        new_v.append(v_c)
        new_s.append(jnp.stack([s_f, s_b], axis=1).astype(xp.dtype))
        sh1, sc1, g1, sh2, sc2, g2 = adaln(c, ada_w[l], ada_b[l])
        h = rmsnorm(xs, norm1[l]) * (1.0 + sc1) + sh1
        out, _, _, _, _ = token_mixer(h, w_in[l], w_o[l], q_norm[l], k_norm[l], hgrn_norm[l], lb,
                                      ang_row, ang_col, cache_k[:, l], cache_v[:, l],
                                      state_hgrn[:, l, 0], state_hgrn[:, l, 1])
        xs = xs + g1 * out
        h = rmsnorm(xs, norm2[l]) * (1.0 + sc2) + sh2
        xs = xs + g2 * conv_ffn(h, w_up[l], conv_w[l], conv_b[l], w_down[l])
    y_prompt = rmsnorm(xp, final_norm)
    y_sample = rmsnorm(xs, final_norm)
    new_cache_k = jnp.stack(new_k, axis=1)
    new_cache_v = jnp.stack(new_v, axis=1)
    new_state_hgrn = jnp.stack(new_s, axis=1)
    return (y_prompt, y_sample, new_cache_k, new_cache_v, new_state_hgrn)


_drawn_inputs = setup_inputs


def setup_inputs(seed=0):
    import zlib

    import numpy as np

    out = dict(_drawn_inputs(seed))
    spreads = {}
    factors = {'cache_k': 8.0,
     'cache_v': 8.0,
     'state_hgrn': 8.0,
     'norm1': 2.889,
     'norm2': 8.0,
     'q_norm': 8.0,
     'k_norm': 7.841,
     'hgrn_norm': 8.0,
     'conv_b': 8.0,
     'final_norm': 7.484}
    for name, (base, spread) in spreads.items():
        noise = np.random.default_rng([zlib.crc32(name.encode()), seed]).standard_normal(out[name].shape)
        drawn = base * np.exp(spread * noise) if base else spread * noise
        out[name] = __import__('jax').numpy.asarray(drawn.astype(out[name].dtype))
    for name, factor in factors.items():
        out[name] = (out[name] * factor).astype(out[name].dtype)
    return out
```

```python
from contextlib import ExitStack

import concourse.bass as bass
from concourse import mybir

F32 = mybir.dt.float32
F32R = mybir.dt.float32r
BF16 = mybir.dt.bfloat16
ALU = mybir.AluOpType
ACT = mybir.ActivationFunctionType
AX_X = mybir.AxisListType.X

P = 128
D = 1024
KC = D // P
T_CTX, T_LAT = 128, 1024
T = T_CTX + T_LAT
NT = T // P
G = 384
NG = T // G
HEAD = 64
NKV, GQ = 4, 4
PAST = 256
NKC = NT + PAST // P
CH = 64
NCH = T // CH
RH = 8
D_FF = 2816
FB = D_FF // P
EPS = 1e-6
B_Q, B_K, B_V, B_RQ, B_RFF, B_RFB, B_RI, B_RG, B_ZA, B_ZR = 0, 8, 10, 12, 20, 28, 36, 44, 52, 60
PHASES = 5
CHAIN2 = 28
RANGES = ((0, T_CTX), (T_CTX, T))


class Chain:

    def __init__(self, eng, sem, base):
        self.eng, self.sem, self.base, self.n = eng, sem, base, 0

    def step(self, ins):
        self.n += 1
        ins.then_inc(self.sem, 1)
        return ins

    def wait(self):
        self.eng.wait_ge(self.sem, self.base + self.n)

    def link(self, ins):
        self.step(ins)
        self.wait()


def split_groups(g):
    lo, hi = g * G, (g + 1) * G
    return [(max(lo, a), min(hi, b), n) for n, (a, b) in enumerate(RANGES) if max(lo, a) < min(hi, b)]


def build(nc, a, outs, phases=5):
    y_prompt, y_sample, out_k, out_v, out_state = outs
    rec_dram = nc.dram_tensor("rec_scratch", (RH, P, T), F32, kind="Internal").ap()
    mix_dram = nc.dram_tensor("mix_scratch", (KC, P, T), F32, kind="Internal").ap()
    w_in = a["w_in"][0].rearrange("(k p) (b c) -> b p k c", p=P, c=P)
    w_in64 = a["w_in"][0].rearrange("(k p) (b c) -> b p k c", p=P, c=HEAD)
    w_o = a["w_o"][0].rearrange("(k p) (b c) -> b p k c", p=P, c=P)
    w_up = a["w_up"][0].rearrange("(k p) (b c) -> b p k c", p=P, c=P)
    w_down = a["w_down"][0].rearrange("(f p) (j c) -> f p j c", p=P, c=P)

    with ExitStack() as ctx:
        def sb(name, shape, dt=F32, c=ctx):
            return c.enter_context(nc.sbuf_tensor(name, shape, dt))

        def pb(name, shape, dt=F32, c=ctx):
            return c.enter_context(nc.psum_tensor(name, shape, dt))

        def sem(name, c=ctx):
            return c.enter_context(nc.semaphore(name))

        HH = sb("act_hi", [P, KC, T], F32R)
        HL = sb("act_lo", [P, KC, T], F32R)
        ident = sb("ident", [P, P])
        ones = sb("ones", [P, P])
        VT = sb("vec_t", [P, 112])
        CW = sb("conv_t", [P, 4, 2 * FB])
        MOD = sb("mod", [P, 48, 2])
        A1 = sb("a1", [P, KC, 2])
        A2 = sb("a2", [P, KC, 2])
        lb = sb("lb", [P, 2 * RH])
        lb1 = sb("lb1", [P, 2 * RH])
        lb1n = sb("lb1n", [P, 2 * RH])
        rgain = sb("rgain", [P, 1])

        phase0(nc, a, sb, pb, sem, HH, HL, ident, ones, VT, CW, MOD, A1, A2, lb, lb1, lb1n, rgain)
        if phases >= 1:
            phase1(nc, a, sem, HH, HL, ident, ones, lb, lb1, lb1n, rgain, w_in, rec_dram, out_state)
        if phases >= 2:
            phase2(nc, a, sem, HH, HL, ident, w_in, w_in64, rec_dram, mix_dram, out_k, out_v)
        if phases >= 3:
            X1 = sb("resid_t", [P, KC, T])
            phase3(nc, a, sem, HH, HL, ident, ones, MOD, A2, X1, w_o, mix_dram)
        if phases >= 4:
            phase4(nc, a, sem, HH, HL, MOD, CW, X1, w_up, w_down)
            phase5(nc, a, sem, ident, X1, y_prompt, y_sample)


def phase0(nc, a, sb_, pb_, sem, HH, HL, ident, ones, VT, CW, MOD, A1, A2, lb, lb1, lb1n, rgain):
    with ExitStack() as ctx:
        def sb(name, shape, dt=F32):
            return ctx.enter_context(nc.sbuf_tensor(name, shape, dt))

        V1 = sb("v1", [112, P])
        V2 = sb("v2", [88, P])
        V3 = sb("v3", [88, P])
        X = sb("x0", [P, NT, D])
        AW = sb("ada_w", [P, 3, KC, 512])
        MR = sb("mod_rows", [2, 6 * D])
        HF = sb("h_f32", [P, 2, 512])
        junk = sb("junk0", [P, D])
        CS = sb("cond_silu", [P, 2, KC])
        SG = sb("cond_sig", [P, 2 * KC])
        LD = sb("lb_diff", [P, 2 * RH])
        SS = sb("ss0", [P, NT])
        RS = sb("rs0", [P, NT])
        vps = ctx.enter_context(nc.psum_tensor("vps", [P, 512], F32))
        aps = ctx.enter_context(nc.psum_tensor("ada_ps", [P, 2, 512], F32))
        mps = ctx.enter_context(nc.psum_tensor("mod_ps", [P, 512], F32))
        xps = ctx.enter_context(nc.psum_tensor("x_ps", [P, 4, 512], F32))

        const_in, vec_in, x_in0, x_in1 = sem("const_in"), sem("vec_in"), sem("x_in0"), sem("x_in1")
        ada_in = [sem(f"ada_in{i}") for i in range(3)]
        vec_t, vec_ok, cond_sig, cond_ok = sem("vec_t"), sem("vec_ok"), sem("cond_sig"), sem("cond_ok")
        ada_done, ada_out, mod_t, mod_ok = sem("ada_done"), sem("ada_out"), sem("mod_t"), sem("mod_ok")
        sq_done, ln_done, rs_done, xn_done = sem("sq_done"), sem("ln_done"), sem("rs_done"), sem("xn_done")
        xt_done, hf_done, hi_done, lo_done = sem("xt_done"), sem("hf_done"), sem("hi_done"), sem("lo_done")
        v_ch = sem("v0_chain")
        GR = [(0, 1, 0), (1, 5, 1), (5, 9, 1)]

        with nc.Block() as block:
            @block.sync
            def _(sp):
                sp.dma_start(ident[:, :], a["c_ident"]).then_inc(const_in, 16)
                row = lambda x: x.rearrange("(r c) -> r c", c=P)
                vecs = [(V1[0:48, :], row(a["ada_b"][0])), (V1[48:56, :], row(a["norm1"][0])),
                        (V1[56:64, :], row(a["norm2"][0])), (V1[64:72, :], row(a["c_ctx"])),
                        (V1[72:80, :], row(a["c"][0])),
                        (V1[80:112, :], a["hgrn_lb_logits"].rearrange("a b (r c) -> (a b r) c", c=P)),
                        (V2[0:44, :], row(a["conv_w"][0, 0])), (V2[44:88, :], row(a["conv_w"][0, 1])),
                        (V3[0:44, :], row(a["conv_w"][0, 2])), (V3[44:88, :], row(a["conv_b"][0])),
                        (rgain[:, :], a["hgrn_norm"][0].rearrange("(p o) -> p o", o=1))]
                for dst, src in vecs:
                    sp.dma_start(dst, src).then_inc(vec_in, 16)
                sp.dma_start(X[:, 0, :], a["x_prompt"][0]).then_inc(x_in0, 16)
                sp.dma_start(X[:, 1:NT, :], a["x_sample"][0].rearrange("(t p) d -> p t d", p=P)).then_inc(x_in1, 16)

            @block.scalar
            def _(act):
                for c in range(3):
                    act.dma_start(AW[:, c], a["ada_w"][0].rearrange("(k p) (b c) -> b p k c", p=P, c=512)[c]).then_inc(ada_in[c], 16)
                act.wait_ge(vec_ok, 1)
                nc.scalar.activation(SG[:, :], VT[:, 64:80], ACT.Sigmoid).then_inc(cond_sig, 1)
                act.wait_ge(vec_ok, 2)
                nc.scalar.activation(lb[:, :], LD[:, :], ACT.Sigmoid).then_inc(cond_sig, 1)
                act.wait_ge(x_in0, 16)
                act.wait_ge(x_in1, 16)
                for t in range(NT):
                    if t:
                        act.wait_ge(sq_done, t)
                    nc.scalar.activation(junk[:, :], X[:, t, :], ACT.Square, accum_out=SS[:, t:t + 1]).then_inc(sq_done, 1)
                act.wait_ge(v_ch, 1)
                nc.scalar.activation(RS[:, :], SS[:, :], ACT.Ln).then_inc(ln_done, 1)
                act.wait_ge(ln_done, 1)
                nc.scalar.activation(RS[:, :], RS[:, :], ACT.Exp, scale=-0.5).then_inc(rs_done, 1)
                for c in range(12):
                    act.wait_ge(ada_done, c + 1)
                    nc.scalar.activation(MR[:, c * 512:(c + 1) * 512], aps[0:2, c % 2, :], ACT.Copy).then_inc(ada_out, 1)
                    if c + 3 < 12:
                        act.dma_start(AW[:, c % 3], a["ada_w"][0].rearrange("(k p) (b c) -> b p k c", p=P, c=512)[c + 3]).then_inc(ada_in[c % 3], 16)
                for n in range(3 * KC):
                    j, (t0, t1, _) = n // 3, GR[n % 3]
                    act.wait_ge(hf_done, n + 1)
                    nc.scalar.activation(HH[:, j, t0 * P:t1 * P], HF[:, n % 2, 0:(t1 - t0) * P], ACT.Copy).then_inc(hi_done, 1)

            @block.tensor
            def _(pe):
                pe.wait_ge(const_in, 16)
                pe.wait_ge(vec_in, 16 * 11)
                nc.tensor.transpose(vps[:, 0:112], V1[:, :], ident[0:112, 0:112])
                nc.tensor.transpose(vps[:, 112:200], V2[:, :], ident[0:88, 0:88])
                nc.tensor.transpose(vps[:, 200:288], V3[:, :], ident[0:88, 0:88]).then_inc(vec_t, 1)
                pe.wait_ge(cond_ok, 1)
                for c in range(12):
                    pe.wait_ge(ada_in[c % 3], 16 * (c // 3 + 1))
                    if c >= 2:
                        pe.wait_ge(ada_out, c - 1)
                    for k in range(KC):
                        m = nc.tensor.matmul(aps[0:2, c % 2, :], CS[:, :, k], AW[:, c % 3, k, :], start=(k == 0), stop=(k == KC - 1))
                    m.then_inc(ada_done, 1)
                pe.wait_ge(ada_out, 12)
                for b in range(48):
                    m = nc.tensor.transpose(mps[:, 2 * b:2 * b + 2], MR[:, b * P:(b + 1) * P], ident[0:2, 0:2])
                m.then_inc(mod_t, 1)
                pe.wait_ge(xn_done, NT)
                for n in range(3 * KC):
                    j, (t0, t1, _) = n // 3, GR[n % 3]
                    if n >= 4:
                        pe.wait_ge(hf_done, n - 3)
                    for i, t in enumerate(range(t0, t1)):
                        m = nc.tensor.transpose(xps[:, n % 4, i * P:(i + 1) * P], X[:, t, j * P:(j + 1) * P], ident[:, :])
                    m.then_inc(xt_done, 1)

            @block.vector
            def _(dve):
                nc.vector.memset(ones[:, :], 1.0)
                dve.wait_ge(vec_t, 1)
                nc.vector.tensor_copy(VT[:, :], vps[:, 0:112]).then_inc(vec_ok, 1)
                nc.vector.tensor_copy(CW[:, :, :], vps[:, 112:288].rearrange("p (a b) -> p a b", a=4)).then_inc(lo_done, 1)
                dve.wait_ge(vec_ok, 1)
                lgt = VT[:, 80:112].rearrange("p (d l h) -> p d l h", d=2, l=2)
                nc.vector.tensor_tensor(LD[:, :].rearrange("p (d h) -> p d h", d=2), lgt[:, :, 0, :], lgt[:, :, 1, :], ALU.subtract).then_inc(vec_ok, 1)
                dve.wait_ge(cond_sig, 1)
                nc.vector.tensor_tensor(CS[:, :, :].rearrange("p a k -> p (a k)"), VT[:, 64:80], SG[:, :], ALU.mult).then_inc(cond_ok, 1)
                dve.wait_ge(cond_sig, 2)
                nc.vector.tensor_scalar(lb1[:, :], lb[:, :], -1.0, 1.0, ALU.mult, ALU.add)
                nc.vector.tensor_scalar(lb1n[:, :], lb[:, :], 1.0, -1.0, ALU.mult, ALU.add)
                dve.wait_ge(sq_done, NT)
                nc.vector.tensor_scalar(SS[:, :], SS[:, :], 1.0 / D, EPS, ALU.mult, ALU.add).then_inc(v_ch, 1)
                dve.wait_ge(rs_done, 1)
                for t in range(NT):
                    nc.vector.tensor_scalar(X[:, t, :], X[:, t, :], RS[:, t:t + 1], None, ALU.mult).then_inc(xn_done, 1)
                dve.wait_ge(mod_t, 1)
                nc.vector.tensor_tensor(MOD[:, :, :], mps[:, 0:96].rearrange("p (b g) -> p b g", g=2),
                                        VT[:, 0:48].unsqueeze(2).broadcast_to((P, 48, 2)), ALU.add).then_inc(mod_ok, 1)
                dve.wait_ge(mod_ok, 1)
                nc.vector.scalar_tensor_tensor(A1[:, :, :], MOD[:, 8:16, :], 1.0, VT[:, 48:56].unsqueeze(2).broadcast_to((P, 8, 2)), ALU.add, ALU.mult).then_inc(mod_ok, 1)
                nc.vector.scalar_tensor_tensor(A2[:, :, :], MOD[:, 32:40, :], 1.0, VT[:, 56:64].unsqueeze(2).broadcast_to((P, 8, 2)), ALU.add, ALU.mult).then_inc(mod_ok, 1)
                dve.wait_ge(mod_ok, 3)

                def low_part(n):
                    j, (t0, t1, _) = n // 3, GR[n % 3]
                    dve.wait_ge(hi_done, n + 1)
                    nc.vector.tensor_tensor(HL[:, j, t0 * P:t1 * P], HF[:, n % 2, 0:(t1 - t0) * P],
                                            HH[:, j, t0 * P:t1 * P].bitcast(F32), ALU.subtract).then_inc(lo_done, 1)

                for n in range(3 * KC):
                    j, (t0, t1, grp) = n // 3, GR[n % 3]
                    dve.wait_ge(xt_done, n + 1)
                    if n >= 2:
                        dve.wait_ge(lo_done, n)
                    nc.vector.tensor_scalar(HF[:, n % 2, 0:(t1 - t0) * P], xps[:, n % 4, 0:(t1 - t0) * P],
                                            A1[:, j, grp:grp + 1], MOD[:, j, grp:grp + 1], ALU.mult, ALU.add).then_inc(hf_done, 1)
                    if n:
                        low_part(n - 1)
                low_part(3 * KC - 1)


def three_pass(nc, out, w_hi, w_lo, x_hi, x_lo, k, last):
    nc.tensor.matmul(out, w_hi, x_hi, start=(k == 0), stop=False)
    nc.tensor.matmul(out, w_hi, x_lo, start=False, stop=False)
    return nc.tensor.matmul(out, w_lo, x_hi, start=False, stop=last)


def phase1(nc, a, sem, HH, HL, ident, ones, lb, lb1, lb1n, rgain, w_in, rec_dram, out_state):
    with ExitStack() as ctx:
        def sb(name, shape, dt=F32):
            return ctx.enter_context(nc.sbuf_tensor(name, shape, dt))

        def pb(name, shape):
            return ctx.enter_context(nc.psum_tensor(name, shape, F32))

        WR = sb("w1_raw", [P, 2, KC, P])
        WH = sb("w1_hi", [P, 3, KC, P], F32R)
        WL = sb("w1_lo", [P, 3, KC, P], F32R)
        S = sb("states", [P, 2, NCH + 1, P])
        TK = sb("keys_values_t", [P, NT, 3, P])
        QD = sb("q_dec", [P, 2, T])
        KD = sb("k_dec", [P, 2, T])
        SIG = sb("sig_f", [P, 2, T])
        RQ, RIT, RG, ZR = sb("rq", [P, T]), sb("ri_t", [P, T]), sb("rg", [P, T]), sb("zr", [P, T])
        GB = sb("log_f", [P, T])
        BB = sb("cum_log_f", [P, T])
        RS = sb("rec_rstd", [P, G])
        AM = sb("masked_scores", [P, 2, 2 * P])
        M2 = sb("causal2", [P, 2 * P])
        EL = sb("chunk_decay", [P, 2, NCH])
        MK = sb("chunk_start", [P, T], BF16)
        LBr, LB1r = sb("lb_act", [P, 2]), sb("lb1_act", [P, 2])
        LBk, LBn = sb("lb1_dve", [P, 2]), sb("lb1n_dve", [P, 2])
        EPSB = sb("eps_r", [P, 1])
        OT = RIT

        proj = pb("proj_ps", [P, 2, 512])
        tps = pb("t_o_ps", [P, 2, 512])
        kvps = pb("kv_ps", [P, 2, 512])
        aps = pb("scores_ps", [P, 2, 512])

        raw_in = [sem("r_raw_in0"), sem("r_raw_in1")]
        w_go, w_hi, w_split = sem("r_w_go"), sem("r_w_hi"), sem("r_w_split")
        proj_done, proj_out = sem("r_proj_done"), sem("r_proj_out")
        log_f, cum_f, exp_f = sem("r_log_f"), sem("r_cum_f"), sem("r_exp_f")
        dir_ready, dve_ch = sem("r_dir_ready"), sem("r_dve_chain")
        t_done, t_out, kv_done = sem("r_t_done"), sem("r_t_out"), sem("r_kv_done")
        st = [sem("r_state_f"), sem("r_state_b")]
        a_done, a_out, o_done, o_out = sem("r_a_done"), sem("r_a_out"), sem("r_o_done"), sem("r_o_out")
        ss_done, ss_ln, ss_out = sem("r_ss_done"), sem("r_ss_ln"), sem("r_ss_out")
        rec_t, rec_ready = sem("r_rec_t"), sem("r_rec_ready")
        s0_in, rec_store, st_store = sem("r_s0_in"), sem("r_rec_store"), sem("r_state_store")
        m_in, mk_ok, zero_ok, lb_ok = sem("r_mask_in"), sem("r_mk_ok"), sem("r_zero_ok"), sem("r_lb_ok")

        UNITS = (B_RQ, B_RFF, B_RFB, B_RI, B_RG, B_ZR)
        NU = len(UNITS)
        PG = NU * NG
        C_SPLIT, C_PROJ, C_OUT = 2, 9, 2
        FWD = [(c, 18 if c == 1 else c + 1) for c in range(NCH)]
        BWD = [(c, 18 if c == 0 else c - 1) for c in reversed(range(NCH))]

        def links(d, j):
            return 2 * (j + 1) - (d == 0 and j == NT - 1) - (d == 1 and j >= NT - 2)

        with nc.Block() as block:
            @block.sync
            def _(sp):
                sp.dma_start(M2[:, :], a["c_mask"]).then_inc(m_in, 16)
                with sp.Fori(0, RH) as r:
                    for u, b0 in enumerate(UNITS):
                        sp.wait_ge(w_split, r * NU + (u - 2 + 1 + C_SPLIT))
                        sp.dma_start(WR[:, u % 2], w_in[r + b0]).then_inc(raw_in[u % 2], 16)
                    sp.wait_ge(o_done, r * NT + 1)
                    sp.dma_start(S[:, 0, 2, :], a["state_hgrn"][0, 0, 0][r]).then_inc(s0_in, 16)
                    sp.dma_start(S[:, 1, NCH - 1, :], a["state_hgrn"][0, 0, 1][r]).then_inc(s0_in, 16)

            @block.gpsimd
            def _(pool):
                pool.sem_inc(w_split, C_SPLIT)
                with pool.Fori(0, RH) as r:
                    for u in range(NU):
                        pool.wait_ge(raw_in[u % 2], r * 48 + 16 * (u // 2 + 1))
                        pool.wait_ge(proj_done, r * PG + (NG * (u - 3) + NG + C_PROJ))
                        pool.sem_inc(w_go, 1)
                        nc.gpsimd.tensor_copy(WH[:, u % 3], WR[:, u % 2]).then_inc(w_hi, 1)
                        pool.wait_ge(w_hi, r * NU + u + 1)
                        nc.gpsimd.tensor_tensor(WL[:, u % 3], WR[:, u % 2], WH[:, u % 3].bitcast(F32), ALU.subtract).then_inc(w_split, 1)

            @block.tensor
            def _(pe):
                pe.sem_inc(proj_done, C_PROJ)
                pe.sem_inc(t_done, 1)
                pe.sem_inc(o_done, 1)
                pe.wait_ge(m_in, 16)
                pe.wait_ge(zero_ok, 2)
                with pe.Fori(0, RH) as r:
                    for u in range(NU):
                        pe.wait_ge(w_split, r * NU + (u + 1 + C_SPLIT))
                        for g in range(NG):
                            n = NG * u + g
                            pe.wait_ge(proj_out, r * PG + (n - 2 + 1 + C_OUT))
                            for k in range(KC):
                                m = three_pass(nc, proj[:, n % 2, 0:G], WH[:, u % 3, k], WL[:, u % 3, k],
                                               HH[:, k, g * G:(g + 1) * G], HL[:, k, g * G:(g + 1) * G], k, k == KC - 1)
                            m.then_inc(proj_done, 1)
                    pe.wait_ge(dir_ready, r * 2 + 3)
                    pe.wait_ge(proj_out, r * PG + (12 + C_OUT))
                    for j in range(NT):
                        if j >= 2:
                            pe.wait_ge(t_out, r * NT + j - 1)
                        cols = slice(j * P, (j + 1) * P)
                        nc.tensor.transpose(tps[:, j % 2, 0:P], SIG[:, 0, cols], ident[:, :])
                        nc.tensor.transpose(tps[:, j % 2, P:2 * P], SIG[:, 1, cols], ident[:, :])
                        nc.tensor.transpose(tps[:, j % 2, 2 * P:3 * P], RIT[:, cols], ident[:, :]).then_inc(t_done, 1)
                    for j in range(NT):
                        pe.wait_ge(t_out, r * NT + NT)
                        if j >= 2:
                            for d in range(2):
                                pe.wait_ge(st[d], r * 17 + links(d, j - 2))
                        for q in range(4):
                            c = FWD[2 * j + q][0] if q < 2 else BWD[2 * j + q - 2][0]
                            rows = slice((c % 2) * CH, (c % 2 + 1) * CH)
                            bank = (kvps, aps)[c % 2]
                            m = nc.tensor.matmul(bank[:, j % 2, q // 2 * P:(q // 2 + 1) * P], TK[rows, c // 2, q // 2, :], TK[rows, c // 2, 2, :],
                                                 start=True, stop=True)
                        m.then_inc(kv_done, 1)

                    def scores(j):
                        if j >= 2:
                            pe.wait_ge(a_out, r * NT + j - 1)
                        cols = slice(j * P, (j + 1) * P)
                        for d in range(2):
                            m = nc.tensor.matmul(aps[:, j % 2, d * P:(d + 1) * P], KD[:, d, cols], QD[:, d, cols], start=True, stop=True)
                        m.then_inc(a_done, 1)

                    for s in st:
                        pe.wait_ge(s, r * 17 + 17)
                    scores(0)
                    pe.wait_ge(s0_in, r * 32 + 32)
                    for j in range(NT):
                        if j + 1 < NT:
                            scores(j + 1)
                        pe.wait_ge(a_out, r * NT + j + 1)
                        if j >= 2:
                            pe.wait_ge(o_out, r * 2 * NT + 2 * (j - 1))
                        o = tps[:, j % 2, 0:P]
                        for d in range(2):
                            nc.tensor.matmul(o, TK[:, j, 2, :], AM[:, j % 2, d * P:(d + 1) * P], start=(d == 0), stop=False)
                        for d in range(2):
                            for h in range(2):
                                c = 2 * j + h
                                m = nc.tensor.matmul(o[:, h * CH:(h + 1) * CH], S[:, d, c, :], QD[:, d, c * CH:(c + 1) * CH],
                                                     start=False, stop=(d == 1 and h == 1))
                        m.then_inc(o_done, 1)
                    for g in range(NG):
                        pe.wait_ge(o_out, r * 2 * NT + 6 * (g + 1))
                        if g == 2:
                            pe.wait_ge(ss_ln, r * NG + 1)
                        nc.tensor.matmul(kvps[:, g % 2, 0:G], ones[:, :], BB[:, g * G:(g + 1) * G], start=True, stop=True).then_inc(ss_done, 1)

            @block.scalar
            def _(act):
                act.sem_inc(proj_out, C_OUT)
                act.wait_ge(zero_ok, 2)
                with act.Fori(0, RH) as r:
                    def evacuate(u, dst, func):
                        for g in range(NG):
                            n = NG * u + g
                            act.wait_ge(proj_done, r * PG + (n + 1 + C_PROJ))
                            nc.scalar.activation(dst[:, g * G:(g + 1) * G], proj[:, n % 2, 0:G], func).then_inc(proj_out, 1)

                    def gate_logs(d):
                        act.wait_ge(proj_out, r * PG + (6 + 3 * d + C_OUT))
                        act.wait_ge(dir_ready, r * 2 + d + 1)
                        nc.scalar.activation(GB[:, :], SIG[:, d, :], ACT.Ln, bias=LBr[:, d:d + 1], scale=LB1r[:, d:d + 1]).then_inc(log_f, 1)
                        act.wait_ge(cum_f, r * 2 + d + 1)
                        nc.scalar.activation(GB[:, :], BB[:, :], ACT.Exp)
                        nc.scalar.activation(BB[:, :], BB[:, :], ACT.Exp, scale=-1.0).then_inc(exp_f, 1)

                    lbv = lb[:, :].rearrange("p (d h) -> p h d", d=2)
                    lb1v = lb1[:, :].rearrange("p (d h) -> p h d", d=2)
                    act.wait_ge(dir_ready, r * 2 + 1)
                    nc.scalar.activation(LBr[:, :], lbv[:, bass.ds(r, 1), :].rearrange("p a d -> p (a d)"), ACT.Copy)
                    nc.scalar.activation(LB1r[:, :], lb1v[:, bass.ds(r, 1), :].rearrange("p a d -> p (a d)"), ACT.Copy).then_inc(lb_ok, 1)
                    act.wait_ge(lb_ok, r + 1)
                    evacuate(0, RQ, ACT.Silu)
                    act.wait_ge(t_done, r * NT + 1)
                    evacuate(1, SIG[:, 0], ACT.Sigmoid)
                    act.wait_ge(ss_done, r * NG + 1)
                    gate_logs(0)
                    evacuate(2, SIG[:, 1], ACT.Sigmoid)
                    gate_logs(1)
                    act.wait_ge(rec_store, r * 16 + 1)
                    evacuate(3, RIT, ACT.Copy)
                    evacuate(4, RG, ACT.Silu)
                    evacuate(5, ZR, ACT.Sigmoid)
                    act.wait_ge(o_done, r * NT + 1)
                    for j in range(NT):
                        act.wait_ge(t_done, r * NT + j + 2)
                        nc.scalar.activation(TK[:, j].rearrange("p a b -> p (a b)"), tps[:, j % 2, 0:3 * P], ACT.Copy).then_inc(t_out, 1)
                    for j in range(NT):
                        act.wait_ge(o_done, r * NT + j + 2)
                        nc.scalar.activation(OT[:, j * P:(j + 1) * P], tps[:, j % 2, 0:P], ACT.Copy).then_inc(o_out, 1)
                        nc.scalar.activation(BB[:, j * P:(j + 1) * P], tps[:, j % 2, 0:P], ACT.Square).then_inc(o_out, 1)
                    for g in range(NG):
                        act.wait_ge(ss_done, r * NG + g + 2)
                        if g:
                            act.wait_ge(rec_ready, r * (NG + 0) + g + 1)
                        else:
                            act.wait_ge(rec_ready, r * NG + 1)
                        nc.scalar.activation(RS[:, :], kvps[:, g % 2, 0:G], ACT.Ln, scale=1.0 / P, bias=EPSB[:, 0:1]).then_inc(ss_ln, 1)
                        act.wait_ge(ss_ln, r * NG + g + 1)
                        nc.scalar.activation(RS[:, :], RS[:, :], ACT.Exp, scale=-0.5).then_inc(ss_out, 1)
                    act.wait_ge(rec_ready, r * NG + NG + 1)
                    act.dma_start(rec_dram[r], OT[:, :]).then_inc(rec_store, 16)
                    for d in range(2):
                        act.wait_ge(st[d], r * 17 + 17)
                        act.dma_start(out_state[0, 0, d][r], S[:, d, NCH, :]).then_inc(st_store, 16)
                act.wait_ge(rec_store, 16 * RH + 1)
                act.wait_ge(st_store, 32 * RH + 1)

            @block.vector
            def _(dve):
                dve.sem_inc(dir_ready, 1)
                dve.sem_inc(rec_ready, 1)
                dve.sem_inc(rec_store, 1)
                dve.sem_inc(st_store, 1)
                dve.sem_inc(ss_done, 1)
                nc.vector.memset(EPSB[:, :], EPS)
                nc.vector.memset(S[:, 0, 0, :], 0.0).then_inc(zero_ok, 1)
                nc.vector.memset(S[:, 1, 1, :], 0.0).then_inc(zero_ok, 1)
                nc.vector.memset(MK[:, :], 1.0).then_inc(mk_ok, 1)
                dve.wait_ge(mk_ok, 1)
                nc.vector.memset(MK[:, 0:T:CH], 0.0).then_inc(mk_ok, 1)
                dve.wait_ge(mk_ok, 2)
                dve.wait_ge(m_in, 16)
                with dve.Fori(0, RH) as r:
                    ch = Chain(dve, dve_ch, r * 8)
                    nc.vector.tensor_copy(LBk[:, :], lb1[:, :].rearrange("p (d h) -> p h d", d=2)[:, bass.ds(r, 1), :].rearrange("p a d -> p (a d)"))
                    ch.step(nc.vector.tensor_copy(LBn[:, :], lb1n[:, :].rearrange("p (d h) -> p h d", d=2)[:, bass.ds(r, 1), :].rearrange("p a d -> p (a d)")))
                    for d in range(2):
                        dve.wait_ge(dir_ready, r * 2 + d + 1)
                        dve.wait_ge(log_f, r * 2 + d + 1)
                        rev = slice(None, None, -1) if d else slice(None)
                        nc.vector.tensor_tensor_scan(BB[:, rev], MK[:, :], GB[:, rev], 0.0, ALU.mult, ALU.add).then_inc(cum_f, 1)
                        ch.wait()
                        ch.step(nc.vector.tensor_scalar(SIG[:, d, :], SIG[:, d, :], LBn[:, d:d + 1], LBk[:, d:d + 1], ALU.mult, ALU.add))
                        dve.wait_ge(exp_f, r * 2 + d + 1)
                        last = GB[:, CH - 1:T:CH] if d == 0 else GB[:, 0:T:CH]
                        ch.link(nc.vector.tensor_copy(EL[:, d, :], last))
                        ch.link(nc.vector.tensor_tensor(KD[:, d, :], SIG[:, d, :], BB[:, :], ALU.mult))
                        nc.vector.tensor_tensor(SIG[:, d, :].rearrange("p (c t) -> p c t", t=CH), KD[:, d, :].rearrange("p (c t) -> p c t", t=CH),
                                                EL[:, d, :].unsqueeze(2).broadcast_to((P, NCH, CH)), ALU.mult)
                        nc.vector.scalar_tensor_tensor(QD[:, d, :], RQ[:, :], float(P) ** -0.5, GB[:, :], ALU.mult, ALU.mult).then_inc(dir_ready, 1)
                    dve.wait_ge(proj_out, r * PG + (PG + C_OUT))
                    ch.step(nc.vector.tensor_tensor(RG[:, :], RG[:, :], ZR[:, :], ALU.mult))
                    dve.wait_ge(s0_in, r * 32 + 32)
                    dve.wait_ge(st_store, r * 32 + 1)
                    count = [0, 0]
                    for j in range(NT):
                        dve.wait_ge(kv_done, r * NT + j + 1)
                        for half in range(2):
                            for d, order in enumerate((FWD, BWD)):
                                c, nxt = order[2 * j + half]
                                used = (kvps, aps)[c % 2][:, j % 2, d * P:(d + 1) * P]
                                if (d, c) in ((0, NCH - 1), (1, 2)):
                                    continue
                                if count[d]:
                                    dve.wait_ge(st[d], r * 17 + count[d])
                                ins = nc.vector.scalar_tensor_tensor(S[:, d, nxt, :], S[:, d, c, :], EL[:, d, c:c + 1], used, ALU.mult, ALU.add)
                                ins.then_inc(st[d], 1)
                                count[d] += 1
                        assert count == [links(0, j), links(1, j)]
                    for j in range(NT):
                        dve.wait_ge(a_done, r * NT + j + 1)
                        if j >= 2:
                            dve.wait_ge(o_done, r * NT + j)
                        nc.vector.tensor_tensor(AM[:, j % 2, :], aps[:, j % 2, 0:2 * P], M2[:, :], ALU.mult).then_inc(a_out, 1)
                    ch.wait()
                    for g in range(NG):
                        dve.wait_ge(ss_out, r * NG + g + 1)
                        cols = slice(g * G, (g + 1) * G)
                        nc.vector.scalar_tensor_tensor(OT[:, cols], OT[:, cols], rgain[:, 0:1], RS[:, :], ALU.mult, ALU.mult).then_inc(rec_t, 1)
                        dve.wait_ge(rec_t, r * NG + g + 1)
                        nc.vector.tensor_tensor(OT[:, cols], OT[:, cols], RG[:, cols], ALU.mult).then_inc(rec_ready, 1)
                    assert ch.n == 8, ch.n


def phase2(nc, a, sem, HH, HL, ident, w_in, w_in64, rec_dram, mix_dram, out_k, out_v):
    with ExitStack() as ctx:
        def sb(name, shape, dt=F32):
            return ctx.enter_context(nc.sbuf_tensor(name, shape, dt))

        WR = sb("w2_raw", [P, 2, KC, P])
        WH = sb("w2_hi", [P, 3, KC, P], F32R)
        WL = sb("w2_lo", [P, 3, KC, P], F32R)
        QKV = sb("qkv", [P, NT, G])
        KH = sb("keys_hi2", [P, NKC * P], F32R)
        KL = sb("keys_lo1", [HEAD + 1, NKC * P], F32R)
        KS = sb("key_stage", [P, 2, 3, 3 * HEAD], F32R)
        V1 = sb("values_hi1", [P, NKC, P], F32R)
        V2 = sb("values_lo", [P, NKC, HEAD], F32R)
        PE32 = sb("probs", [P, 2, 512])
        PH = sb("probs_hi", [P, 2, 512], F32R)
        PL = sb("probs_lo", [P, 2, 512], F32R)
        QT1 = sb("q_t_hilo", [P, 2, 512], F32R)
        QT2 = sb("q_t_max", [HEAD + 1, 2, 512], F32R)
        QS1 = sb("q_stage", [P, GQ, P], F32R)
        QS2 = sb("q_stage_max", [P, GQ, HEAD + 2], F32R)
        ATT = sb("attn_t", [P, 2, T])
        ZA = sb("za_gate", [P, 2, T])
        COS, SIN = sb("cos", [P, NT - 1, HEAD]), sb("sin", [P, NT - 1, HEAD])
        R1, R2 = sb("rope_a", [P, 3, 5 * HEAD]), sb("rope_b", [P, 3, 5 * HEAD])
        SS, RST = sb("qk_ss", [P, 15]), sb("qk_rstd", [P, 15])
        M4 = sb("row_max", [P, GQ])
        RR = sb("inv_sum", [HEAD, 512])
        CK, CV = sb("cache_k_in", [P, 2, HEAD]), sb("cache_v_in", [P, 2, HEAD])
        GN = sb("qk_gain", [P, 2, HEAD])
        ps = ctx.enter_context(nc.psum_tensor("att_ps", [P, 8, 512], F32))
        B_S, B_QT, B_ST, B_PV, B_PROJ, B_KT = 0, 3, 4, 7, 4, 0

        raw_in = [sem("a_raw_in0"), sem("a_raw_in1")]
        w_go, w_hi, w_split = sem("a_w_go"), sem("a_w_hi"), sem("a_w_split")
        proj_done, proj_out = sem("a_proj_done"), sem("a_proj_out")
        ss_ok, rst_ln, rst_ok, n_ch = sem("a_ss_ok"), sem("a_rst_ln"), sem("a_rst_ok"), sem("a_norm_chain")
        ks_ok, kt_done, kt_out, v_ok = sem("a_ks_ok"), sem("a_kt_done"), sem("a_kt_out"), sem("a_v_ok")
        qs1_ok, qs2_ok, qt_done, qt_out = sem("a_qs1_ok"), sem("a_qs2_ok"), sem("a_qt_done"), sem("a_qt_out")
        qs_hi = sem("a_qs_hi")
        s_done, m_done = sem("a_s_done"), sem("a_m_done")
        st_done, ex_done, hi_go, hi_done, lo_done, pv_done = (sem("a_st_done"), sem("a_ex_done"), sem("a_hi_go"), sem("a_hi_done"),
                                                             sem("a_lo_done"), sem("a_pv_done"))
        r_ln, r_ok, att_ok = sem("a_r_ln"), sem("a_r_ok"), sem("a_att_ok")
        za_mul, rec_in, mix_ok, mix_store = sem("a_za_mul"), sem("a_rec_in"), sem("a_mix_ok"), sem("a_mix_store")
        ctx_in, kv_store, const_in, set_ok = sem("a_ctx_in"), sem("a_kv_store"), sem("a_const_in"), sem("a_set_ok")

        NU, PG, C_SPLIT, C_PROJ, C_OUT = 5, 15, 2, 7, 2
        NS = 9
        NC = 1 + 10 * (NS - 1)

        def keys(n):
            return range(0, 1) if n == 0 else range(1, NKC)

        def idx(n, i):
            return 0 if n == 0 else 1 + 10 * (n - 1) + i

        def slot(n, i):
            return 1 if n == 0 else i % 2

        def after(n, i):
            nc_ = len(keys(n))
            if n == 0:
                return (1, 1)
            if i + 2 < nc_:
                return (n, i + 2)
            return (n + 1, i + 2 - nc_) if n + 1 < NS else None

        with nc.Block() as block:
            def all_steps(eng, kv, step):
                step(0, 0)
                with eng.Fori(0, 3) as p:
                    step(1, p * 2)
                    step(2, p * 2)
                step(7, 0)
                step(8, 0)

            @block.sync
            def _(sp):
                for dst, src in ((COS[:, :, :], a["c_cos"].rearrange("(t p) d -> p t d", p=P)),
                                 (SIN[:, :, :], a["c_sin"].rearrange("(t p) d -> p t d", p=P)),
                                 (GN[:, 0, :], a["q_norm"][0].partition_broadcast(P)),
                                 (GN[:, 1, :], a["k_norm"][0].partition_broadcast(P))):
                    sp.dma_start(dst, src).then_inc(const_in, 16)
                with sp.Fori(0, NKV) as kv:
                    for u in range(NU):
                        before = (0, -1, 1, 2, 3)[u]
                        sp.wait_ge(w_split, kv * NU + (before + C_SPLIT))
                        if u < 2:
                            sp.dma_start(WR[:, u], w_in[kv * 2 + (B_Q + u)]).then_inc(raw_in[u], 16)
                        elif u == 2:
                            sp.dma_start(WR[:, 0, :, 0:HEAD], w_in64[kv + 2 * B_K]).then_inc(raw_in[0], 16)
                            sp.dma_start(WR[:, 0, :, HEAD:P], w_in64[kv + 2 * B_V]).then_inc(raw_in[0], 16)
                        else:
                            sp.dma_start(WR[:, u % 2], w_in[kv * 2 + (B_ZA + u - 3)]).then_inc(raw_in[u % 2], 16)
                    sp.wait_ge(v_ok, kv + 1)
                    sp.wait_ge(ks_ok, kv * 4 + 1)
                    sp.dma_start(CK[:, :, :], a["cache_k"][0, 0].rearrange("(b p) h d -> h p b d", p=P)[kv]).then_inc(ctx_in, 16)
                    sp.dma_start(CV[:, :, :], a["cache_v"][0, 0].rearrange("(b p) h d -> h p b d", p=P)[kv]).then_inc(ctx_in, 16)
                    sp.wait_ge(ks_ok, kv * 4 + 2)
                    sp.dma_start(out_k[0, 0].rearrange("t h d -> h t d")[kv], QKV[:, 0, 4 * HEAD:5 * HEAD]).then_inc(kv_store, 16)
                    sp.dma_start(out_v[0, 0].rearrange("t h d -> h t d")[kv], QKV[:, 0, 5 * HEAD:6 * HEAD]).then_inc(kv_store, 16)
                sp.wait_ge(kv_store, 32 * NKV + 1)

            @block.gpsimd
            def _(pool):
                pool.sem_inc(w_split, C_SPLIT)
                with pool.Fori(0, NKV) as kv:
                    for u in range(NU):
                        pool.wait_ge(raw_in[u % 2], kv * (64, 32)[u % 2] + (16, 16, 48, 32, 64)[u])
                        pool.wait_ge(proj_done, kv * PG + (4, 7, 1, 16, 16)[u])
                        pool.sem_inc(w_go, 1)
                        nc.gpsimd.tensor_copy(WH[:, u % 3], WR[:, u % 2]).then_inc(w_hi, 1)
                        pool.wait_ge(w_hi, kv * NU + u + 1)
                        nc.gpsimd.tensor_tensor(WL[:, u % 3], WR[:, u % 2], WH[:, u % 3].bitcast(F32), ALU.subtract).then_inc(w_split, 1)

            def key_transposes(pe, kv, g):
                pe.wait_ge(ks_ok, kv * 4 + g + 2)
                pe.wait_ge(kt_out, kv * 8 + (2 * (g - 1) if g >= 2 else 0) + 2)
                n = 3 if g < 3 else 2
                for i in range(n):
                    m = nc.tensor.transpose(ps[:, B_KT + 2 * (g % 2), i * P:(i + 1) * P], KS[:, g % 2, i, 0:P].bitcast(F32), ident[:, :])
                for i in range(n):
                    m = nc.tensor.transpose(ps[0:HEAD, B_KT + 2 * (g % 2) + 1, i * P:(i + 1) * P], KS[:, g % 2, i, P:3 * HEAD].bitcast(F32), ident[:, :])
                m.then_inc(kt_done, 1)

            @block.tensor
            def _(pe):
                pe.sem_inc(proj_done, C_PROJ)
                pe.sem_inc(kt_done, 1)
                pe.wait_ge(set_ok, 2)
                with pe.Fori(0, NKV) as kv:
                    for n in range(PG):
                        if n == 0:
                            pe.wait_ge(w_split, kv * NU + (3 + C_SPLIT))
                            pe.wait_ge(proj_out, kv * PG + C_OUT)
                            pe.wait_ge(att_ok, kv * NS + 1)
                        else:
                            pe.wait_ge(proj_out, kv * PG + (n - 1 + C_OUT))
                        bank = ps[:, B_PROJ + n % 2, 0:G]
                        if n < NT:
                            cols = slice(n * P, (n + 1) * P)
                            for k in range(KC):
                                nc.tensor.matmul(bank, HH[:, k, cols], WH[:, :, k, :], start=(k == 0), stop=False)
                                nc.tensor.matmul(bank, HL[:, k, cols], WH[:, :, k, :], start=False, stop=False)
                                m = nc.tensor.matmul(bank, HH[:, k, cols], WL[:, :, k, :], start=False, stop=(k == KC - 1))
                        else:
                            u, g = 3 + (n - NT) // NG, (n - NT) % NG
                            if g == 0:
                                pe.wait_ge(w_split, kv * NU + (u + 1 + C_SPLIT))
                            for k in range(KC):
                                m = three_pass(nc, bank, WH[:, u % 3, k], WL[:, u % 3, k],
                                               HH[:, k, g * G:(g + 1) * G], HL[:, k, g * G:(g + 1) * G], k, k == KC - 1)
                        m.then_inc(proj_done, 1)
                        if n >= NT + 2:
                            key_transposes(pe, kv, n - NT - 2)

                    def wait_step(sem_, per_kv, count, o, per_step):
                        pe.wait_ge(sem_, kv * per_kv + o * per_step + count)

                    def q_part(n, o):
                        wait_step(qs1_ok, NS, n + 1, o, 1)
                        wait_step(qt_out, 2 * NS, 2 * n + 1, o, 2)
                        for h in range(GQ):
                            m = nc.tensor.transpose(ps[:, B_QT, h * P:(h + 1) * P], QS1[:, h, :].bitcast(F32), ident[:, :])
                        m.then_inc(qt_done, 1)

                    def max_scores(n, o, h):
                        if h == 0:
                            wait_step(qt_out, 2 * NS, 2 * n + 2, o, 2)
                        wait_step(m_done, 4 * NS, 4 * n + h + 1, o, 4)
                        k0, k1 = keys(n)[0] * P, (keys(n)[-1] + 1) * P
                        for i, c in enumerate(range(k0, k1, 512)):
                            w = min(512, k1 - c)
                            m = nc.tensor.matmul(ps[:, B_S + i, 0:w], QT1[:, n % 2, h * P:(h + 1) * P], KH[:, c:c + w], start=True, stop=True)
                        m.then_inc(s_done, 1)

                    def q_max_part(n, o):
                        wait_step(qs2_ok, NS, n + 2, o, 1)
                        for h in range(GQ):
                            m = nc.tensor.transpose(ps[0:HEAD + 1, B_QT, h * P:(h + 1) * P], QS2[:, h, 0:HEAD + 1].bitcast(F32), ident[:, :])
                        m.then_inc(qt_done, 1)

                    def scores_t(n, o, i):
                        g = idx(n, i)
                        if i == 0:
                            wait_step(qt_out, 2 * NS, 2 * n + 3, o, 2)
                        wait_step(ex_done, NC, max(g - 1, 0) + 1, o, 10)
                        c = keys(n)[i] * P
                        bank = ps[:, B_ST + slot(n, i), :]
                        nc.tensor.matmul(bank, KH[:, c:c + P], QT1[:, n % 2, :], start=True, stop=False)
                        nc.tensor.matmul(bank, KL[:, c:c + P], QT2[:, n % 2, :], start=False, stop=True).then_inc(st_done, 1)

                    def weighted(n, o, i):
                        if i == 0:
                            wait_step(att_ok, NS, n + 1, o, 1)
                        wait_step(lo_done, NC, idx(n, i) + 2, o, 10)
                        c, s = keys(n)[i], slot(n, i)
                        last = i == len(keys(n)) - 1
                        nc.tensor.matmul(ps[:, B_PV, :], V1[:, c, :], PH[:, s, :], start=(i == 0), stop=False)
                        nc.tensor.matmul(ps[0:HEAD, B_PV, :], V2[:, c, :], PH[:, s, :], start=False, stop=False)
                        nc.tensor.matmul(ps[:, B_PV, :], V1[:, c, :], PL[:, s, :], start=False, stop=last).then_inc(pv_done, 1)

                    pe.wait_ge(kt_out, kv * 8 + 10)
                    pe.wait_ge(v_ok, kv + 2)
                    q_part(0, 0)
                    for h in range(GQ):
                        max_scores(0, 0, h)
                    q_max_part(0, 0)
                    scores_t(0, 0, 0)

                    def step(n, o):
                        if n == 0:
                            q_part(1, o)
                            for h in range(GQ):
                                max_scores(1, o, h)
                            q_max_part(1, o)
                            scores_t(1, o, 0)
                        for i in range(len(keys(n))):
                            if n and n + 1 < NS:
                                if i == 0:
                                    q_part(n + 1, o)
                                elif i < 5:
                                    max_scores(n + 1, o, i - 1)
                                elif i == 7:
                                    q_max_part(n + 1, o)
                            if after(n, i):
                                scores_t(after(n, i)[0], o, after(n, i)[1])
                            weighted(n, o, i)

                    all_steps(pe, kv, step)

            @block.scalar
            def _(act):
                act.sem_inc(proj_out, C_OUT)
                act.sem_inc(kt_out, 2)
                act.sem_inc(qt_out, 1)
                act.sem_inc(ex_done, 1)
                with act.Fori(0, NKV) as kv:
                    def wait_step(sem_, per_kv, count, o, per_step):
                        act.wait_ge(sem_, kv * per_kv + o * per_step + count)

                    act.wait_ge(kv_store, kv * 32 + 1)
                    act.wait_ge(mix_store, kv * 32 + 1)
                    for n in range(PG):
                        act.wait_ge(proj_done, kv * PG + (n + 1 + C_PROJ))
                        bank = ps[:, B_PROJ + n % 2, 0:G]
                        if n < NT:
                            nc.scalar.activation(QKV[:, n, :], bank, ACT.Copy).then_inc(proj_out, 1)
                        else:
                            g = (n - NT) % NG
                            nc.scalar.activation(ZA[:, (n - NT) // NG, g * G:(g + 1) * G], bank, ACT.Sigmoid).then_inc(proj_out, 1)
                        if n in (3, 6, 9):
                            g = n // 3 - 1
                            act.wait_ge(ss_ok, kv * 3 + g + 1)
                            nc.scalar.activation(RST[:, :], SS[:, :], ACT.Ln).then_inc(rst_ln, 1)
                            act.wait_ge(rst_ln, kv * 3 + g + 1)
                            nc.scalar.activation(RST[:, :], RST[:, :], ACT.Exp, scale=-0.5).then_inc(rst_ok, 1)
                        if n >= NT + 2:
                            g = n - NT - 2
                            w = (3 if g < 3 else 2) * P
                            act.wait_ge(kt_done, kv * 4 + g + 2)
                            nc.scalar.activation(KH[:, 3 * g * P:3 * g * P + w], ps[:, B_KT + 2 * (g % 2), 0:w], ACT.Copy).then_inc(kt_out, 1)
                            nc.scalar.activation(KL[0:HEAD, 3 * g * P:3 * g * P + w], ps[0:HEAD, B_KT + 2 * (g % 2) + 1, 0:w], ACT.Copy).then_inc(kt_out, 1)

                    def q_out(n, o):
                        wait_step(qt_done, 2 * NS, 2 * n + 1, o, 2)
                        nc.scalar.activation(QT1[:, n % 2, :], ps[:, B_QT, :], ACT.Copy).then_inc(qt_out, 1)

                    def q_max_out(n, o):
                        wait_step(qt_done, 2 * NS, 2 * n + 2, o, 2)
                        nc.scalar.activation(QT2[:, n % 2, :], ps[0:HEAD + 1, B_QT, :], ACT.Copy).then_inc(qt_out, 1)

                    def exp(n, o, i):
                        g = idx(n, i)
                        wait_step(st_done, NC, g + 1, o, 10)
                        wait_step(lo_done, NC, max(g - 1, 0) + 1, o, 10)
                        nc.scalar.activation(PE32[:, slot(n, i), :], ps[:, B_ST + slot(n, i), :], ACT.Exp, scale=HEAD ** -0.5).then_inc(ex_done, 1)

                    def inverse_sum(n, o):
                        wait_step(pv_done, NC, idx(n, len(keys(n)) - 1) + 1, o, 10)
                        wait_step(att_ok, NS, n + 1, o, 1)
                        nc.scalar.activation(RR[:, :], ps[HEAD:P, B_PV, :], ACT.Ln).then_inc(r_ln, 1)
                        wait_step(r_ln, NS, n + 1, o, 1)
                        nc.scalar.activation(RR[:, :], RR[:, :], ACT.Exp, scale=-1.0).then_inc(r_ok, 1)

                    q_out(0, 0)
                    q_max_out(0, 0)
                    exp(0, 0, 0)

                    def step(n, o):
                        if n == 0:
                            q_out(1, o)
                            q_max_out(1, o)
                            exp(1, o, 0)
                        if n:
                            inverse_sum(n - 1, o)
                        for i in range(len(keys(n))):
                            if n and n + 1 < NS:
                                if i == 0:
                                    q_out(n + 1, o)
                                elif i == 7:
                                    q_max_out(n + 1, o)
                            if after(n, i):
                                exp(after(n, i)[0], o, after(n, i)[1])

                    all_steps(act, kv, step)
                    inverse_sum(NS - 1, 0)
                    act.wait_ge(za_mul, kv + 1)
                    for j in range(2):
                        act.dma_start(ZA[:, j, :], rec_dram[kv * 2 + j]).then_inc(rec_in, 16)
                    for j in range(2):
                        act.wait_ge(mix_ok, kv * 2 + j + 1)
                        act.dma_start(mix_dram[kv * 2 + j], ATT[:, j, :]).then_inc(mix_store, 16)
                act.wait_ge(mix_store, 32 * NKV + 1)

            @block.vector
            def _(dve):
                nc.vector.memset(KL[HEAD:HEAD + 1, :].bitcast(F32), 1.0).then_inc(set_ok, 1)
                nc.vector.memset(V1[:, :, HEAD:P].bitcast(F32), 1.0).then_inc(set_ok, 1)
                for s in (v_ok, ks_ok, kv_store, mix_store, m_done, lo_done, att_ok, qs2_ok):
                    dve.sem_inc(s, 1)
                dve.wait_ge(const_in, 64)
                with dve.Fori(0, NKV) as kv:
                    def wait_step(sem_, per_kv, count, o, per_step):
                        dve.wait_ge(sem_, kv * per_kv + o * per_step + count)

                    ch = Chain(dve, n_ch, kv * CHAIN2)

                    def stage_keys(g, src, n):
                        dve.wait_ge(kt_done, kv * 4 + (g - 1 if g >= 2 else 0) + 1)
                        ch.wait()
                        st = KS[:, g % 2, 0:n, :]
                        nc.vector.tensor_copy(st[:, :, 0:HEAD], src)
                        ch.link(nc.vector.tensor_copy(st[:, :, HEAD:P], src))
                        nc.vector.tensor_tensor(st[:, :, P:3 * HEAD], src, st[:, :, 0:HEAD].bitcast(F32), ALU.subtract).then_inc(ks_ok, 1)

                    for g in range(3):
                        dve.wait_ge(proj_out, kv * PG + (3 * g + 3 + C_OUT))
                        if g:
                            ch.wait()
                        x = QKV[:, 3 * g:3 * g + 3, 0:5 * HEAD]
                        x4 = x.rearrange("p t (h d) -> p t h d", d=HEAD)
                        ch.link(nc.vector.tensor_tensor(R1[:, :, :], x, x, ALU.mult))
                        ch.link(nc.vector.tensor_reduce(SS[:, :], R1[:, :, :].rearrange("p t (h d) -> p (t h) d", d=HEAD), AX_X, ALU.add))
                        nc.vector.tensor_scalar(SS[:, :], SS[:, :], 1.0 / HEAD, EPS, ALU.mult, ALU.add).then_inc(ss_ok, 1)
                        dve.wait_ge(rst_ok, kv * 3 + g + 1)
                        ch.link(nc.vector.tensor_tensor(x4, x4, RST[:, :].rearrange("p (t h) -> p t h", t=3).unsqueeze(3).broadcast_to((P, 3, 5, HEAD)), ALU.mult))
                        ch.step(nc.vector.tensor_tensor(x4[:, :, 0:4, :], x4[:, :, 0:4, :], GN[:, 0, :].unsqueeze(1).unsqueeze(1).broadcast_to((P, 3, 4, HEAD)), ALU.mult))
                        ch.link(nc.vector.tensor_tensor(x4[:, :, 4, :], x4[:, :, 4, :], GN[:, 1, :].unsqueeze(1).broadcast_to((P, 3, HEAD)), ALU.mult))
                        tiles = [t for t in range(3 * g, 3 * g + 3) if t]
                        for t in tiles:
                            i = t - 3 * g
                            xt = QKV[:, t, 0:5 * HEAD].rearrange("p (h d) -> p h d", d=HEAD)
                            nc.vector.tensor_tensor(R1[:, i, :].rearrange("p (h d) -> p h d", d=HEAD), xt,
                                                    COS[:, t - 1, :].unsqueeze(1).broadcast_to((P, 5, HEAD)), ALU.mult)
                            for half in range(2):
                                v = lambda z: z.rearrange("p h (s b e) -> p h s b e", s=2, b=2)
                                m = nc.vector.tensor_tensor(v(R2[:, i, :].rearrange("p (h d) -> p h d", d=HEAD))[:, :, :, half, :],
                                                            v(xt)[:, :, :, 1 - half, :],
                                                            SIN[:, t - 1, :].rearrange("p (s b e) -> p s b e", s=2, b=2)[:, :, half, :].unsqueeze(1).broadcast_to((P, 5, 2, 16)), ALU.mult)
                        ch.link(m)
                        i0 = tiles[0] - 3 * g
                        ch.link(nc.vector.tensor_tensor(QKV[:, tiles[0]:3 * g + 3, 0:5 * HEAD], R1[:, i0:3, :], R2[:, i0:3, :], ALU.add))
                        stage_keys(g, QKV[:, 3 * g:3 * g + 3, 4 * HEAD:5 * HEAD], 3)
                    dve.wait_ge(ctx_in, kv * 32 + 32)
                    stage_keys(3, CK[:, :, :], 2)
                    val = QKV[:, :, 5 * HEAD:6 * HEAD]
                    ch.step(nc.vector.tensor_copy(V1[:, 0:NT, 0:HEAD], val))
                    ch.link(nc.vector.tensor_copy(V1[:, NT:NKC, 0:HEAD], CV[:, :, :]))
                    ch.link(nc.vector.tensor_tensor(V2[:, 0:NT, :], val, V1[:, 0:NT, 0:HEAD].bitcast(F32), ALU.subtract))
                    nc.vector.tensor_tensor(V2[:, NT:NKC, :], CV[:, :, :], V1[:, NT:NKC, 0:HEAD].bitcast(F32), ALU.subtract).then_inc(v_ok, 1)

                    def stage_q(n, o):
                        wait_step(qt_done, 2 * NS, 2 * n, o, 2) if n else None
                        q = (QKV[:, n, 0:4 * HEAD] if isinstance(o, int) else QKV[:, bass.ds(o + n, 1), 0:4 * HEAD].rearrange("p a d -> p (a d)"))
                        q = q.rearrange("p (h d) -> p h d", d=HEAD)
                        nc.vector.tensor_copy(QS2[:, :, 0:HEAD], q)
                        nc.vector.tensor_copy(QS1[:, :, 0:HEAD], q).then_inc(qs_hi, 1)
                        wait_step(qs_hi, NS, n + 1, o, 1)
                        nc.vector.tensor_tensor(QS1[:, :, HEAD:P], q, QS1[:, :, 0:HEAD].bitcast(F32), ALU.subtract).then_inc(qs1_ok, 1)

                    def row_max(n, o, h):
                        wait_step(s_done, 4 * NS, 4 * n + h + 1, o, 4)
                        if h == 0:
                            wait_step(qs2_ok, NS, n + 1, o, 1)
                        w = len(keys(n)) * P
                        s = ps[:, B_S:B_S + 3, :].rearrange("p a b -> p (a b)")[:, 0:w]
                        nc.vector.tensor_reduce(M4[:, h:h + 1], s, AX_X, ALU.max).then_inc(m_done, 1)

                    def put_max(n, o):
                        wait_step(m_done, 4 * NS, 4 * n + 5, o, 4)
                        nc.vector.tensor_scalar(QS2[:, :, HEAD], M4[:, :], -1.0, None, ALU.mult).then_inc(qs2_ok, 1)

                    def low(n, o, i):
                        g = idx(n, i)
                        wait_step(hi_done, NC, g + 1, o, 10)
                        wait_step(pv_done, NC, g - 1, o, 10) if g >= 2 else None
                        s = slot(n, i)
                        nc.vector.tensor_tensor(PL[:, s, :], PE32[:, s, :], PH[:, s, :].bitcast(F32), ALU.subtract).then_inc(lo_done, 1)

                    def high(n, o, i):
                        g = idx(n, i)
                        wait_step(ex_done, NC, g + 2, o, 10)
                        wait_step(pv_done, NC, g - 1, o, 10) if g >= 2 else None
                        s = slot(n, i)
                        nc.vector.tensor_copy(PH[:, s, :], PE32[:, s, :]).then_inc(hi_done, 1)

                    def normalise(n, o):
                        wait_step(r_ok, NS, n + 1, o, 1)
                        for par in range(2):
                            out = ATT[par * HEAD:(par + 1) * HEAD, :, :]
                            out = out[:, :, n * P:(n + 1) * P] if isinstance(o, int) else out[:, :, bass.ds(o * P + n * P, P)]
                            m = nc.vector.tensor_tensor(out, ps[0:HEAD, B_PV, :].rearrange("p (j b q) -> p b j q", j=2, b=2)[:, par],
                                                        RR[:, :].rearrange("p (j b q) -> p b j q", j=2, b=2)[:, par], ALU.mult)
                        m.then_inc(att_ok, 1)

                    stage_q(0, 0)
                    for h in range(GQ):
                        row_max(0, 0, h)
                    put_max(0, 0)
                    stage_q(1, 0)
                    high(0, 0, 0)
                    low(0, 0, 0)

                    def step(n, o):
                        if n == 0:
                            for h in range(GQ):
                                row_max(1, o, h)
                            put_max(1, o)
                            stage_q(2, o)
                            high(1, o, 0)
                            low(1, o, 0)
                        if n:
                            normalise(n - 1, o)
                        for i in range(len(keys(n))):
                            if n and n + 1 < NS and 1 <= i < 5:
                                row_max(n + 1, o, i - 1)
                                if i == 4:
                                    put_max(n + 1, o)
                            if after(n, i):
                                high(after(n, i)[0], o, after(n, i)[1])
                                low(after(n, i)[0], o, after(n, i)[1])
                            if i == 8 and n and n + 2 < NS:
                                stage_q(n + 2, o)

                    all_steps(dve, kv, step)
                    normalise(NS - 1, 0)
                    dve.wait_ge(att_ok, kv * NS + NS + 1)
                    dve.wait_ge(mix_store, kv * 32 + 1)
                    nc.vector.tensor_tensor(ATT[:, :, :], ATT[:, :, :], ZA[:, :, :], ALU.mult).then_inc(za_mul, 1)
                    dve.wait_ge(za_mul, kv + 1)
                    dve.wait_ge(rec_in, kv * 32 + 32)
                    for j in range(2):
                        nc.vector.tensor_tensor(ATT[:, j, :], ATT[:, j, :], ZA[:, j, :], ALU.add).then_inc(mix_ok, 1)
                    assert ch.n == CHAIN2, ch.n



def phase3(nc, a, sem, HH, HL, ident, ones, MOD, A2, X1, w_o, mix_dram):
    with ExitStack() as ctx:
        def sb(name, shape, dt=F32):
            return ctx.enter_context(nc.sbuf_tensor(name, shape, dt))

        WR = sb("w3_raw", [P, 2, KC, P])
        WH = sb("w3_hi", [P, 2, KC, P], F32R)
        WL = sb("w3_lo", [P, 2, KC, P], F32R)
        X = sb("x3", [P, 2, D])
        MS = sb("mix_in", [P, 2, T])
        SQ = sb("sq3", [P, T])
        RS = sb("rs3", [P, T])
        PRE = sb("pre3", [P, 2, T])
        EPSB = sb("eps3", [P, 1])
        ps = ctx.enter_context(nc.psum_tensor("out_ps", [P, 8, 512], F32))

        raw_in = [sem("o_raw_in0"), sem("o_raw_in1")]
        w_go, w_hi, w_split = sem("o_w_go"), sem("o_w_hi"), sem("o_w_split")
        x_in = [sem("o_x_in0"), sem("o_x_in1")]
        mix_in = [sem("o_mix_in0"), sem("o_mix_in1")]
        xt_done, xt_out = sem("o_xt_done"), sem("o_xt_out")
        mh, ml = sem("o_mix_hi"), sem("o_mix_lo")
        proj_done, res_ok = sem("o_proj_done"), sem("o_res_ok")
        sq_ok, ss_done, ss_ln, rs_ok = sem("o_sq_ok"), sem("o_ss_done"), sem("o_ss_ln"), sem("o_rs_ok")
        pre_ok, hi_ok, lo_ok, set_ok = sem("o_pre_ok"), sem("o_hi_ok"), sem("o_lo_ok"), sem("o_set_ok")
        C_SPLIT, C_PROJ = 2, 6

        def x_rows(t):
            return a["x_prompt"][0] if t == 0 else a["x_sample"][0, (t - 1) * P:t * P, :]

        with nc.Block() as block:
            @block.sync
            def _(sp):
                for t in range(NT):
                    if t >= 2:
                        sp.wait_ge(xt_done, 2 * (t - 1))
                    sp.dma_start(X[:, t % 2, :], x_rows(t)).then_inc(x_in[t % 2], 16)
                    if t < KC:
                        if t >= 2:
                            sp.wait_ge(ml, t - 1)
                        sp.dma_start(MS[:, t % 2, :], mix_dram[t]).then_inc(mix_in[t % 2], 16)
                with sp.Fori(0, KC // 2) as i:
                    for u in range(2):
                        sp.wait_ge(w_split, i * 2 + u + 1)
                        sp.dma_start(WR[:, u], w_o[i * 2 + u]).then_inc(raw_in[u], 16)

            @block.gpsimd
            def _(pool):
                pool.sem_inc(w_split, C_SPLIT)
                with pool.Fori(0, KC // 2) as i:
                    for u in range(2):
                        pool.wait_ge(raw_in[u], i * 16 + 16)
                        pool.wait_ge(proj_done, i * 6 + (NG * (u - 2) + NG + C_PROJ))
                        pool.sem_inc(w_go, 1)
                        nc.gpsimd.tensor_copy(WH[:, u], WR[:, u]).then_inc(w_hi, 1)
                        pool.wait_ge(w_hi, i * 2 + u + 1)
                        nc.gpsimd.tensor_tensor(WL[:, u], WR[:, u], WH[:, u].bitcast(F32), ALU.subtract).then_inc(w_split, 1)

            @block.tensor
            def _(pe):
                pe.sem_inc(proj_done, C_PROJ)
                for t in range(NT):
                    pe.wait_ge(x_in[t % 2], 16 * (t // 2 + 1))
                    for q in range(2):
                        n = 2 * t + q
                        if n >= 4:
                            pe.wait_ge(xt_out, n - 3)
                        for i in range(4):
                            m = nc.tensor.transpose(ps[:, n % 4, i * P:(i + 1) * P], X[:, t % 2, (4 * q + i) * P:(4 * q + i + 1) * P], ident[:, :])
                        m.then_inc(xt_done, 1)
                pe.wait_ge(ml, KC)
                pe.wait_ge(xt_out, 2 * NT)
                with pe.Fori(0, KC // 2) as i:
                    for u in range(2):
                        pe.wait_ge(w_split, i * 2 + u + 1 + C_SPLIT)
                        for g in range(NG):
                            n = NG * u + g
                            pe.wait_ge(res_ok, i * 6 + n + 1)
                            for k in range(KC):
                                m = three_pass(nc, ps[:, n, 0:G], WH[:, u, k], WL[:, u, k],
                                               HH[:, k, g * G:(g + 1) * G], HL[:, k, g * G:(g + 1) * G], k, k == KC - 1)
                            m.then_inc(proj_done, 1)
                pe.wait_ge(res_ok, 6 * (KC // 2) + 6)
                for j in range(KC):
                    pe.wait_ge(sq_ok, j + 1)
                    for g in range(NG):
                        m = nc.tensor.matmul(ps[:, g, 0:G], ones[:, :], SQ[:, g * G:(g + 1) * G], start=(j == 0), stop=(j == KC - 1))
                    m.then_inc(ss_done, 1)

            @block.scalar
            def _(act):
                for t in range(NT):
                    for q in range(2):
                        n = 2 * t + q
                        act.wait_ge(xt_done, n + 1)
                        nc.scalar.activation(X1[:, 4 * q:4 * q + 4, t * P:(t + 1) * P], ps[:, n % 4, :].rearrange("p (j c) -> p j c", j=4), ACT.Copy).then_inc(xt_out, 1)
                    if t < KC:
                        act.wait_ge(mix_in[t % 2], 16 * (t // 2 + 1))
                        nc.scalar.activation(HH[:, t, :], MS[:, t % 2, :], ACT.Copy).then_inc(mh, 1)
                act.wait_ge(res_ok, 6 * (KC // 2) + 6)
                act.wait_ge(set_ok, 1)
                for j in range(KC):
                    if j:
                        act.wait_ge(ss_done, j)
                    nc.scalar.activation(SQ[:, :], X1[:, j, :], ACT.Square).then_inc(sq_ok, 1)
                act.wait_ge(ss_done, KC)
                for g in range(NG):
                    nc.scalar.activation(RS[:, g * G:(g + 1) * G], ps[:, g, 0:G], ACT.Ln, scale=1.0 / D, bias=EPSB[:, 0:1]).then_inc(ss_ln, 1)
                act.wait_ge(ss_ln, NG)
                nc.scalar.activation(RS[:, :], RS[:, :], ACT.Exp, scale=-0.5).then_inc(rs_ok, 1)
                for j in range(KC):
                    act.wait_ge(pre_ok, 2 * j + 2)
                    for grp, (t0, t1) in enumerate(RANGES):
                        nc.scalar.activation(HH[:, j, t0:t1], PRE[:, j % 2, t0:t1], ACT.Identity, bias=MOD[:, 24 + j, grp:grp + 1]).then_inc(hi_ok, 1)

            @block.vector
            def _(dve):
                nc.vector.memset(EPSB[:, :], EPS).then_inc(set_ok, 1)
                dve.sem_inc(res_ok, 6)
                for k in range(KC):
                    dve.wait_ge(mh, k + 1)
                    nc.vector.tensor_tensor(HL[:, k, :], MS[:, k % 2, :], HH[:, k, :].bitcast(F32), ALU.subtract).then_inc(ml, 1)
                dve.wait_ge(xt_out, 2 * NT)
                with dve.Fori(0, KC // 2) as i:
                    for u in range(2):
                        for g in range(NG):
                            n = NG * u + g
                            dve.wait_ge(proj_done, i * 6 + n + 1 + C_PROJ)
                            for t0, t1, grp in split_groups(g):
                                x = X1[:, bass.ds(i * 2 + u, 1), t0:t1].rearrange("p a t -> p (a t)")
                                gate = MOD[:, bass.ds(i * 2 + (16 + u), 1), grp:grp + 1].rearrange("p a t -> p (a t)")
                                m = nc.vector.scalar_tensor_tensor(x, ps[:, n, t0 - g * G:t1 - g * G], gate, x, ALU.mult, ALU.add)
                            m.then_inc(res_ok, 1)
                dve.wait_ge(rs_ok, 1)
                def low(j):
                    for grp, (t0, t1) in enumerate(RANGES):
                        dve.wait_ge(hi_ok, 2 * j + grp + 1)
                        nc.vector.scalar_tensor_tensor(HL[:, j, t0:t1], PRE[:, j % 2, t0:t1], MOD[:, 24 + j, grp:grp + 1],
                                                       HH[:, j, t0:t1].bitcast(F32), ALU.add, ALU.subtract).then_inc(lo_ok, 1)
                for j in range(KC):
                    if j >= 2:
                        dve.wait_ge(lo_ok, 2 * (j - 1))
                    for grp, (t0, t1) in enumerate(RANGES):
                        nc.vector.scalar_tensor_tensor(PRE[:, j % 2, t0:t1], X1[:, j, t0:t1], A2[:, j, grp:grp + 1], RS[:, t0:t1],
                                                       ALU.mult, ALU.mult).then_inc(pre_ok, 1)
                    if j:
                        low(j - 1)
                low(KC - 1)


def phase4(nc, a, sem, HH, HL, MOD, CW, X1, w_up, w_down):
    with ExitStack() as ctx:
        def sb(name, shape, dt=F32):
            return ctx.enter_context(nc.sbuf_tensor(name, shape, dt))

        WR = sb("w4_raw", [P, 3, KC, P])
        WH = sb("w4_hi", [P, 3, KC, P], F32R)
        WL = sb("w4_lo", [P, 3, KC, P], F32R)
        U = sb("up", [P, 2, T])
        C = sb("conv", [P, 2, T])
        GF = sb("gated", [P, T])
        GH = sb("gated_hi", [P, T], F32R)
        GL = sb("gated_lo", [P, T], F32R)
        up = ctx.enter_context(nc.psum_tensor("up_ps", [P, 4, 512], F32))
        dn = ctx.enter_context(nc.psum_tensor("down_ps", [P, 4, 512], F32))

        raw_in = [sem(f"f_raw_in{i}") for i in range(3)]
        w_go, w_hi = sem("f_w_go"), sem("f_w_hi")
        w_split = [sem(f"f_w_split{i}") for i in range(3)]
        up_done, up_out, taps = sem("f_up_done"), sem("f_up_out"), sem("f_taps")
        silu_ok, g_ok, gh_ok, gl_ok = sem("f_silu_ok"), sem("f_g_ok"), sem("f_gh_ok"), sem("f_gl_ok")
        dn_done, dn_out = sem("f_dn_done"), sem("f_dn_out")
        ND = KC * NG
        C_UP, C_DN = 6, 4

        with nc.Block() as block:
            @block.sync
            def _(sp):
                with sp.Fori(0, FB) as f:
                    for s, src in enumerate((w_up[f], w_up[f + FB], w_down[f])):
                        sp.wait_ge(w_split[s], f + 1)
                        sp.dma_start(WR[:, s], src).then_inc(raw_in[s], 16)

            @block.gpsimd
            def _(pool):
                for s in w_split:
                    pool.sem_inc(s, 1)
                with pool.Fori(0, FB) as f:
                    for s in range(3):
                        pool.wait_ge(raw_in[s], f * 16 + 16)
                        if s < 2:
                            pool.wait_ge(up_done, f * 6 + (3 * s - 3 + C_UP))
                        else:
                            pool.wait_ge(dn_done, f * ND + 1)
                        pool.sem_inc(w_go, 1)
                        nc.gpsimd.tensor_copy(WH[:, s], WR[:, s]).then_inc(w_hi, 1)
                        pool.wait_ge(w_hi, f * 3 + s + 1)
                        nc.gpsimd.tensor_tensor(WL[:, s], WR[:, s], WH[:, s].bitcast(F32), ALU.subtract).then_inc(w_split[s], 1)

            @block.tensor
            def _(pe):
                pe.sem_inc(up_done, C_UP)
                pe.sem_inc(dn_done, 1)

                def up_part(f):
                    for s in range(2):
                        pe.wait_ge(w_split[s], f + 2)
                        for g in range(NG):
                            n = NG * s + g
                            pe.wait_ge(up_out, f * 6 + n + 3)
                            for k in range(KC):
                                m = three_pass(nc, up[:, n % 2, 0:G], WH[:, s, k], WL[:, s, k],
                                               HH[:, k, g * G:(g + 1) * G], HL[:, k, g * G:(g + 1) * G], k, k == KC - 1)
                            m.then_inc(up_done, 1)

                def down_part(f):
                    pe.wait_ge(w_split[2], f + 2)
                    pe.wait_ge(gl_ok, f + 2)
                    for j in range(KC):
                        for g in range(NG):
                            n = NG * j + g
                            pe.wait_ge(dn_out, f * ND + (n - 4 + 1 + C_DN))
                            three_pass(nc, dn[:, n % 4, 0:G], WH[:, 2, j], WL[:, 2, j],
                                       GH[:, g * G:(g + 1) * G], GL[:, g * G:(g + 1) * G], 0, True).then_inc(dn_done, 1)

                up_part(0)
                with pe.Fori(0, FB - 1) as f:
                    up_part(f + 1)
                    down_part(f)
                down_part(FB - 1)

            @block.scalar
            def _(act):
                act.sem_inc(up_out, 4)
                with act.Fori(0, FB) as f:
                    for s in range(2):
                        act.wait_ge(g_ok, f + 1)
                        for g in range(NG):
                            n = NG * s + g
                            act.wait_ge(up_done, f * 6 + n + 1 + C_UP)
                            cols = slice(g * G, (g + 1) * G)
                            tap = CW[:, 1, bass.ds(f + s * FB, 1)]
                            bias = CW[:, 3, bass.ds(f + s * FB, 1)]
                            nc.scalar.activation(U[:, s, cols], up[:, n % 2, 0:G], ACT.Copy)
                            nc.scalar.activation(C[:, s, cols], up[:, n % 2, 0:G], ACT.Identity, scale=tap, bias=bias).then_inc(up_out, 1)
                        if s == 0:
                            act.wait_ge(taps, f * 8 + 4)
                            nc.scalar.activation(C[:, 0, :], C[:, 0, :], ACT.Silu).then_inc(silu_ok, 1)
                    act.wait_ge(g_ok, f + 2)
                    act.wait_ge(dn_done, f * ND + 1)
                    nc.scalar.activation(GH[:, :], GF[:, :], ACT.Copy).then_inc(gh_ok, 1)

            @block.vector
            def _(dve):
                dve.sem_inc(g_ok, 1)
                dve.sem_inc(gl_ok, 1)
                dve.sem_inc(dn_out, C_DN)

                def conv(f):
                    for s in range(2):
                        dve.wait_ge(up_out, f * 6 + NG * (s + 1) + 4)
                        n = 0
                        for tap, src, dst in ((0, 0, 1), (2, 1, 0)):
                            for t0, t1 in RANGES:
                                w = t1 - t0 - 1
                                if n >= 2:
                                    dve.wait_ge(taps, f * 8 + 4 * s + n - 1)
                                c = C[:, s, t0 + dst:t0 + dst + w]
                                nc.vector.scalar_tensor_tensor(c, U[:, s, t0 + src:t0 + src + w], CW[:, tap, bass.ds(f + s * FB, 1)],
                                                               c, ALU.mult, ALU.add).then_inc(taps, 1)
                                n += 1
                    dve.wait_ge(silu_ok, f + 1)
                    dve.wait_ge(taps, f * 8 + 8)
                    dve.wait_ge(gl_ok, f + 1)
                    nc.vector.tensor_tensor(GF[:, :], C[:, 0, :], C[:, 1, :], ALU.mult).then_inc(g_ok, 1)

                def low(f):
                    dve.wait_ge(gh_ok, f + 1)
                    nc.vector.tensor_tensor(GL[:, :], GF[:, :], GH[:, :].bitcast(F32), ALU.subtract).then_inc(gl_ok, 1)

                def add_down(f):
                    dve.wait_ge(dn_out, f * ND + C_DN)
                    for j in range(KC):
                        for g in range(NG):
                            n = NG * j + g
                            dve.wait_ge(dn_done, f * ND + n + 2)
                            for t0, t1, grp in split_groups(g):
                                x = X1[:, j, t0:t1]
                                m = nc.vector.scalar_tensor_tensor(x, dn[:, n % 4, t0 - g * G:t1 - g * G], MOD[:, 40 + j, grp:grp + 1], x, ALU.mult, ALU.add)
                            m.then_inc(dn_out, 1)

                conv(0)
                low(0)
                with dve.Fori(0, FB - 1) as f:
                    conv(f + 1)
                    add_down(f)
                    low(f + 1)
                add_down(FB - 1)


def phase5(nc, a, sem, ident, X1, y_prompt, y_sample):
    with ExitStack() as ctx:
        def sb(name, shape, dt=F32):
            return ctx.enter_context(nc.sbuf_tensor(name, shape, dt))

        Y = sb("y", [P, NT, D])
        junk = sb("junk5", [P, 2, D])
        FN = sb("final_gain", [P, D])
        SS, RS = sb("ss5", [P, NT]), sb("rs5", [P, NT])
        EPSB = sb("eps5", [P, 1])
        ps = ctx.enter_context(nc.psum_tensor("y_ps", [P, 4, 1024], F32))
        fn_in, yt, sq, yc, ln, rs, st = (sem("y_gain_in"), sem("y_t"), sem("y_sq"), sem("y_copy"), sem("y_ln"),
                                                   sem("y_rs"), sem("y_store"))
        set_ok = sem("y_set_ok")
        with nc.Block() as block:
            @block.sync
            def _(sp):
                sp.dma_start(FN[:, :], a["final_norm"].partition_broadcast(P)).then_inc(fn_in, 16)
                for t in range(NT):
                    sp.wait_ge(yc, t + 1)
                    sp.dma_start(y_prompt[0] if t == 0 else y_sample[0, (t - 1) * P:t * P, :], Y[:, t, :]).then_inc(st, 16)
                sp.wait_ge(st, 16 * NT)

            @block.tensor
            def _(pe):
                for t in range(NT):
                    if t >= 4:
                        pe.wait_ge(yc, t - 3)
                    for j in range(KC):
                        m = nc.tensor.transpose(ps[:, t % 4, j * P:(j + 1) * P], X1[:, j, t * P:(t + 1) * P], ident[:, :])
                    m.then_inc(yt, 1)

            @block.scalar
            def _(act):
                act.wait_ge(set_ok, 1)
                for t in range(NT):
                    act.wait_ge(yt, t + 1)
                    if t >= 2:
                        act.wait_ge(sq, t - 1)
                    nc.scalar.activation(junk[:, t % 2, :], ps[:, t % 4, :], ACT.Square, accum_out=SS[:, t:t + 1]).then_inc(sq, 1)
                    act.wait_ge(sq, t + 1)
                    nc.scalar.activation(RS[:, t:t + 1], SS[:, t:t + 1], ACT.Ln, scale=1.0 / D, bias=EPSB[:, 0:1]).then_inc(ln, 1)
                    act.wait_ge(ln, t + 1)
                    nc.scalar.activation(RS[:, t:t + 1], RS[:, t:t + 1], ACT.Exp, scale=-0.5).then_inc(rs, 1)

            @block.vector
            def _(dve):
                nc.vector.memset(EPSB[:, :], EPS).then_inc(set_ok, 1)
                dve.wait_ge(fn_in, 16)
                for t in range(NT):
                    dve.wait_ge(rs, t + 1)
                    nc.vector.scalar_tensor_tensor(Y[:, t, :], ps[:, t % 4, :], RS[:, t:t + 1], FN[:, :], ALU.mult, ALU.mult).then_inc(yc, 1)



_INS = ["x_prompt", "x_sample", "c", "cache_k", "cache_v", "state_hgrn", "c_ctx", "ada_w", "ada_b", "norm1", "norm2",
        "w_in", "q_norm", "k_norm", "hgrn_lb_logits", "hgrn_norm", "w_o", "w_up", "conv_w", "conv_b", "w_down", "final_norm"]
_OUTS = [(1, T_CTX, D), (1, T_LAT, D), (1, 1, T_CTX, NKV, HEAD), (1, 1, T_CTX, NKV, HEAD), (1, 1, 2, RH, P, P)]


def shape_constants():
    import numpy as np
    s, t = np.arange(P)[:, None], np.arange(P)[None, :]
    same = s // CH == t // CH
    mask = np.concatenate([same & (s <= t), same & (s >= t)], axis=1).astype(np.float32)
    half, grid_w = HEAD // 2, 64
    inv = (1.0 / (10000.0 ** (np.arange(0, half, 2, dtype=np.float32) / np.float32(half)))).astype(np.float32)
    n = np.arange(T_LAT)
    row, col = (n // grid_w).astype(np.float32)[:, None] * inv, (n % grid_w).astype(np.float32)[:, None] * inv
    cos = np.concatenate([np.cos(row), np.cos(row), np.cos(col), np.cos(col)], axis=1).astype(np.float32)
    sin = np.concatenate([-np.sin(row), np.sin(row), -np.sin(col), np.sin(col)], axis=1).astype(np.float32)
    return {"c_ident": np.eye(P, dtype=np.float32), "c_mask": mask, "c_cos": cos, "c_sin": sin}


def kernel(**inputs):
    import numpy as np
    import concourse.bacc as bacc
    from concourse.bass_utils import run_bass_kernel_spmd

    nc = bacc.Bacc("TRN2", target_bir_lowering=False, num_devices=1)
    arrays, aps = {}, {}
    given = {n: np.ascontiguousarray(inputs[n]) for n in _INS}
    given.update(shape_constants())
    for n, v in given.items():
        arrays["in_" + n] = v
        aps[n] = nc.dram_tensor("in_" + n, v.shape, F32, kind="ExternalInput").ap()
    outs = [nc.dram_tensor(f"out_{i}", s, F32, kind="ExternalOutput").ap() for i, s in enumerate(_OUTS)]
    build(nc, aps, outs, PHASES)
    r = run_bass_kernel_spmd(nc, [arrays], core_ids=[0])
    return tuple(r.results[0][f"out_{i}"] for i in range(len(_OUTS)))
```

```python
from contextlib import ExitStack

import concourse.bass as bass
from concourse import mybir

F32 = mybir.dt.float32
F32R = mybir.dt.float32r
BF16 = mybir.dt.bfloat16
ALU = mybir.AluOpType
ACT = mybir.ActivationFunctionType
LN_EXP = "natural_log_exp_and_others"
AX_X = mybir.AxisListType.X

P = 128
D = 1024
KC = D // P
T_CTX, T_LAT = 128, 1024
T = T_CTX + T_LAT
NT = T // P
G = 384
NG = T // G
HEAD = 64
NKV, GQ = 4, 4
PAST = 256
NKC = NT + PAST // P
CH = 64
NCH = T // CH
RH = 8
D_FF = 2816
FB = D_FF // P
EPS = 1e-6
B_Q, B_K, B_V, B_RQ, B_RFF, B_RFB, B_RI, B_RG, B_ZA, B_ZR = 0, 8, 10, 12, 20, 28, 36, 44, 52, 60
PHASES = 5
CHAIN2 = 28
RANGES = ((0, T_CTX), (T_CTX, T))


class Chain:

    def __init__(self, eng, sem, base):
        self.eng, self.sem, self.base, self.n = eng, sem, base, 0

    def step(self, ins):
        self.n += 1
        ins.then_inc(self.sem, 1)
        return ins

    def wait(self):
        self.eng.wait_ge(self.sem, self.base + self.n)

    def link(self, ins):
        self.step(ins)
        self.wait()


def split_groups(g):
    lo, hi = g * G, (g + 1) * G
    return [(max(lo, a), min(hi, b), n) for n, (a, b) in enumerate(RANGES) if max(lo, a) < min(hi, b)]


def build(nc, a, outs, phases=5):
    y_prompt, y_sample, out_k, out_v, out_state = outs
    rec_dram = nc.dram_tensor("rec_scratch", (RH, P, T), F32, kind="Internal").ap()
    mix_dram = nc.dram_tensor("mix_scratch", (KC, P, T), F32, kind="Internal").ap()
    w_in = a["w_in"][0].rearrange("(k p) (b c) -> b p k c", p=P, c=P)
    w_in64 = a["w_in"][0].rearrange("(k p) (b c) -> b p k c", p=P, c=HEAD)
    w_o = a["w_o"][0].rearrange("(k p) (b c) -> b p k c", p=P, c=P)
    w_up = a["w_up"][0].rearrange("(k p) (b c) -> b p k c", p=P, c=P)
    w_down = a["w_down"][0].rearrange("(f p) (j c) -> f p j c", p=P, c=P)

    with ExitStack() as ctx:
        def sb(name, shape, dt=F32, c=ctx):
            return c.enter_context(nc.sbuf_tensor(name, shape, dt))

        def pb(name, shape, dt=F32, c=ctx):
            return c.enter_context(nc.psum_tensor(name, shape, dt))

        def sem(name, c=ctx):
            return c.enter_context(nc.semaphore(name))

        HH = sb("act_hi", [P, KC, T], F32R)
        HL = sb("act_lo", [P, KC, T], F32R)
        ident = sb("ident", [P, P])
        ones = sb("ones", [P, P])
        VT = sb("vec_t", [P, 112])
        CW = sb("conv_t", [P, 4, 2 * FB])
        MOD = sb("mod", [P, 48, 2])
        A1 = sb("a1", [P, KC, 2])
        A2 = sb("a2", [P, KC, 2])
        lb = sb("lb", [P, 2 * RH])
        lb1 = sb("lb1", [P, 2 * RH])
        lb1n = sb("lb1n", [P, 2 * RH])
        rgain = sb("rgain", [P, 1])

        phase0(nc, a, sb, pb, sem, HH, HL, ident, ones, VT, CW, MOD, A1, A2, lb, lb1, lb1n, rgain)
        W = (sb("w_raw", [P, 2, KC, P]), sb("w_hi", [P, 3, KC, P], F32R), sb("w_lo", [P, 3, KC, P], F32R))
        if phases >= 1:
            phase1(nc, a, sem, W, w_in64, HH, HL, ident, ones, lb, lb1, lb1n, rgain, w_in, rec_dram, out_state)
        if phases >= 2:
            phase2(nc, a, sem, W, w_o, HH, HL, ident, w_in, w_in64, rec_dram, mix_dram, out_k, out_v)
        if phases >= 3:
            X1 = sb("resid_t", [P, KC, T])
            phase3(nc, a, sem, W, w_up, HH, HL, ident, ones, MOD, A2, X1, w_o, mix_dram)
        if phases >= 4:
            phase4(nc, a, sem, W, HH, HL, MOD, CW, X1, w_up, w_down)
            phase5(nc, a, sem, ident, X1, y_prompt, y_sample)


def phase0(nc, a, sb_, pb_, sem, HH, HL, ident, ones, VT, CW, MOD, A1, A2, lb, lb1, lb1n, rgain):
    with ExitStack() as ctx:
        def sb(name, shape, dt=F32):
            return ctx.enter_context(nc.sbuf_tensor(name, shape, dt))

        V1 = sb("v1", [112, P])
        V2 = sb("v2", [88, P])
        V3 = sb("v3", [88, P])
        X = sb("x0", [P, NT, D])
        AW = sb("ada_w", [P, 3, KC, 512])
        MR = sb("mod_rows", [2, 6 * D])
        HF = sb("h_f32", [P, 2, 512])
        junk = sb("junk0", [P, D])
        CS = sb("cond_silu", [P, 2, KC])
        SG = sb("cond_sig", [P, 2 * KC])
        LD = sb("lb_diff", [P, 2 * RH])
        SS = sb("ss0", [P, NT])
        RS = sb("rs0", [P, NT])
        vps = ctx.enter_context(nc.psum_tensor("vps", [P, 512], F32))
        aps = ctx.enter_context(nc.psum_tensor("ada_ps", [P, 2, 512], F32))
        mps = ctx.enter_context(nc.psum_tensor("mod_ps", [P, 512], F32))
        xps = ctx.enter_context(nc.psum_tensor("x_ps", [P, 4, 512], F32))

        const_in, vec_in, x_in0, x_in1 = sem("const_in"), sem("vec_in"), sem("x_in0"), sem("x_in1")
        ada_in = [sem(f"ada_in{i}") for i in range(3)]
        vec_t, vec_ok, cond_sig, cond_ok = sem("vec_t"), sem("vec_ok"), sem("cond_sig"), sem("cond_ok")
        ada_done, ada_out, mod_t, mod_ok = sem("ada_done"), sem("ada_out"), sem("mod_t"), sem("mod_ok")
        sq_done, ln_done, rs_done, xn_done = sem("sq_done"), sem("ln_done"), sem("rs_done"), sem("xn_done")
        xt_done, hf_done, hi_done, lo_done = sem("xt_done"), sem("hf_done"), sem("hi_done"), sem("lo_done")
        v_ch = sem("v0_chain")
        GR = [(0, 1, 0), (1, 5, 1), (5, 9, 1)]

        with nc.Block() as block:
            @block.sync
            def _(sp):
                sp.dma_start(ident[:, :], a["c_ident"]).then_inc(const_in, 16)
                row = lambda x: x.rearrange("(r c) -> r c", c=P)
                vecs = [(V1[0:48, :], row(a["ada_b"][0])), (V1[48:56, :], row(a["norm1"][0])),
                        (V1[56:64, :], row(a["norm2"][0])), (V1[64:72, :], row(a["c_ctx"])),
                        (V1[72:80, :], row(a["c"][0])),
                        (V1[80:112, :], a["hgrn_lb_logits"].rearrange("a b (r c) -> (a b r) c", c=P)),
                        (V2[0:44, :], row(a["conv_w"][0, 0])), (V2[44:88, :], row(a["conv_w"][0, 1])),
                        (V3[0:44, :], row(a["conv_w"][0, 2])), (V3[44:88, :], row(a["conv_b"][0])),
                        (rgain[:, :], a["hgrn_norm"][0].rearrange("(p o) -> p o", o=1))]
                for dst, src in vecs:
                    sp.dma_start(dst, src).then_inc(vec_in, 16)
                sp.dma_start(X[:, 0, :], a["x_prompt"][0]).then_inc(x_in0, 16)
                sp.dma_start(X[:, 1:NT, :], a["x_sample"][0].rearrange("(t p) d -> p t d", p=P)).then_inc(x_in1, 16)

            @block.scalar
            def _(act):
                for c in range(3):
                    act.dma_start(AW[:, c], a["ada_w"][0].rearrange("(k p) (b c) -> b p k c", p=P, c=512)[c]).then_inc(ada_in[c], 16)
                act.wait_ge(vec_ok, 1)
                nc.scalar.activation(SG[:, :], VT[:, 64:80], ACT.Sigmoid).then_inc(cond_sig, 1)
                act.wait_ge(vec_ok, 2)
                nc.scalar.activation(lb[:, :], LD[:, :], ACT.Sigmoid).then_inc(cond_sig, 1)
                act.wait_ge(x_in0, 16)
                act.wait_ge(x_in1, 16)
                for t in range(NT):
                    if t:
                        act.wait_ge(sq_done, t)
                    nc.scalar.activation(junk[:, :], X[:, t, :], ACT.Square, accum_out=SS[:, t:t + 1]).then_inc(sq_done, 1)
                nc.scalar.preload_act_table_set(LN_EXP)
                act.wait_ge(v_ch, 1)
                nc.scalar.activation(RS[:, :], SS[:, :], ACT.Ln).then_inc(ln_done, 1)
                act.wait_ge(ln_done, 1)
                nc.scalar.activation(RS[:, :], RS[:, :], ACT.Exp, scale=-0.5).then_inc(rs_done, 1)
                for c in range(12):
                    act.wait_ge(ada_done, c + 1)
                    nc.scalar.activation(MR[:, c * 512:(c + 1) * 512], aps[0:2, c % 2, :], ACT.Copy).then_inc(ada_out, 1)
                    if c + 3 < 12:
                        act.dma_start(AW[:, c % 3], a["ada_w"][0].rearrange("(k p) (b c) -> b p k c", p=P, c=512)[c + 3]).then_inc(ada_in[c % 3], 16)
                for n in range(3 * KC):
                    j, (t0, t1, _) = n // 3, GR[n % 3]
                    act.wait_ge(hf_done, n + 1)
                    nc.scalar.activation(HH[:, j, t0 * P:t1 * P], HF[:, n % 2, 0:(t1 - t0) * P], ACT.Copy).then_inc(hi_done, 1)

            @block.tensor
            def _(pe):
                pe.wait_ge(const_in, 16)
                pe.wait_ge(vec_in, 16 * 11)
                nc.tensor.transpose(vps[:, 0:112], V1[:, :], ident[0:112, 0:112])
                nc.tensor.transpose(vps[:, 112:200], V2[:, :], ident[0:88, 0:88])
                nc.tensor.transpose(vps[:, 200:288], V3[:, :], ident[0:88, 0:88]).then_inc(vec_t, 1)
                pe.wait_ge(cond_ok, 1)
                for c in range(12):
                    pe.wait_ge(ada_in[c % 3], 16 * (c // 3 + 1))
                    if c >= 2:
                        pe.wait_ge(ada_out, c - 1)
                    for k in range(KC):
                        m = nc.tensor.matmul(aps[0:2, c % 2, :], CS[:, :, k], AW[:, c % 3, k, :], start=(k == 0), stop=(k == KC - 1))
                    m.then_inc(ada_done, 1)
                pe.wait_ge(ada_out, 12)
                for b in range(48):
                    m = nc.tensor.transpose(mps[:, 2 * b:2 * b + 2], MR[:, b * P:(b + 1) * P], ident[0:2, 0:2])
                m.then_inc(mod_t, 1)
                pe.wait_ge(xn_done, NT)
                for n in range(3 * KC):
                    j, (t0, t1, _) = n // 3, GR[n % 3]
                    if n >= 4:
                        pe.wait_ge(hf_done, n - 3)
                    for i, t in enumerate(range(t0, t1)):
                        m = nc.tensor.transpose(xps[:, n % 4, i * P:(i + 1) * P], X[:, t, j * P:(j + 1) * P], ident[:, :])
                    m.then_inc(xt_done, 1)

            @block.vector
            def _(dve):
                nc.vector.memset(ones[:, :], 1.0)
                dve.wait_ge(vec_t, 1)
                nc.vector.tensor_copy(VT[:, :], vps[:, 0:112]).then_inc(vec_ok, 1)
                nc.vector.tensor_copy(CW[:, :, :], vps[:, 112:288].rearrange("p (a b) -> p a b", a=4)).then_inc(lo_done, 1)
                dve.wait_ge(vec_ok, 1)
                lgt = VT[:, 80:112].rearrange("p (d l h) -> p d l h", d=2, l=2)
                nc.vector.tensor_tensor(LD[:, :].rearrange("p (d h) -> p d h", d=2), lgt[:, :, 0, :], lgt[:, :, 1, :], ALU.subtract).then_inc(vec_ok, 1)
                dve.wait_ge(cond_sig, 1)
                nc.vector.tensor_tensor(CS[:, :, :].rearrange("p a k -> p (a k)"), VT[:, 64:80], SG[:, :], ALU.mult).then_inc(cond_ok, 1)
                dve.wait_ge(cond_sig, 2)
                nc.vector.tensor_scalar(lb1[:, :], lb[:, :], -1.0, 1.0, ALU.mult, ALU.add)
                nc.vector.tensor_scalar(lb1n[:, :], lb[:, :], 1.0, -1.0, ALU.mult, ALU.add)
                dve.wait_ge(sq_done, NT)
                nc.vector.tensor_scalar(SS[:, :], SS[:, :], 1.0 / D, EPS, ALU.mult, ALU.add).then_inc(v_ch, 1)
                dve.wait_ge(rs_done, 1)
                for t in range(NT):
                    nc.vector.tensor_scalar(X[:, t, :], X[:, t, :], RS[:, t:t + 1], None, ALU.mult).then_inc(xn_done, 1)
                dve.wait_ge(mod_t, 1)
                nc.vector.tensor_tensor(MOD[:, :, :], mps[:, 0:96].rearrange("p (b g) -> p b g", g=2),
                                        VT[:, 0:48].unsqueeze(2).broadcast_to((P, 48, 2)), ALU.add).then_inc(mod_ok, 1)
                dve.wait_ge(mod_ok, 1)
                nc.vector.scalar_tensor_tensor(A1[:, :, :], MOD[:, 8:16, :], 1.0, VT[:, 48:56].unsqueeze(2).broadcast_to((P, 8, 2)), ALU.add, ALU.mult).then_inc(mod_ok, 1)
                nc.vector.scalar_tensor_tensor(A2[:, :, :], MOD[:, 32:40, :], 1.0, VT[:, 56:64].unsqueeze(2).broadcast_to((P, 8, 2)), ALU.add, ALU.mult).then_inc(mod_ok, 1)
                dve.wait_ge(mod_ok, 3)

                def low_part(n):
                    j, (t0, t1, _) = n // 3, GR[n % 3]
                    dve.wait_ge(hi_done, n + 1)
                    nc.vector.tensor_tensor(HL[:, j, t0 * P:t1 * P], HF[:, n % 2, 0:(t1 - t0) * P],
                                            HH[:, j, t0 * P:t1 * P].bitcast(F32), ALU.subtract).then_inc(lo_done, 1)

                for n in range(3 * KC):
                    j, (t0, t1, grp) = n // 3, GR[n % 3]
                    dve.wait_ge(xt_done, n + 1)
                    if n >= 2:
                        dve.wait_ge(lo_done, n)
                    nc.vector.tensor_scalar(HF[:, n % 2, 0:(t1 - t0) * P], xps[:, n % 4, 0:(t1 - t0) * P],
                                            A1[:, j, grp:grp + 1], MOD[:, j, grp:grp + 1], ALU.mult, ALU.add).then_inc(hf_done, 1)
                    if n:
                        low_part(n - 1)
                low_part(3 * KC - 1)


def three_pass(nc, out, w_hi, w_lo, x_hi, x_lo, k, last):
    nc.tensor.matmul(out, w_hi, x_hi, start=(k == 0), stop=False)
    nc.tensor.matmul(out, w_hi, x_lo, start=False, stop=False)
    return nc.tensor.matmul(out, w_lo, x_hi, start=False, stop=last)


def load_qkv(sp, WR, w_in, w_in64, kv, u, done):
    if u < 2:
        sp.dma_start(WR[:, u], w_in[kv * 2 + (B_Q + u)]).then_inc(done, 16)
    else:
        sp.dma_start(WR[:, 0, :, 0:HEAD], w_in64[kv + 2 * B_K]).then_inc(done, 16)
        sp.dma_start(WR[:, 0, :, HEAD:P], w_in64[kv + 2 * B_V]).then_inc(done, 16)


def phase1(nc, a, sem, W, w_in64, HH, HL, ident, ones, lb, lb1, lb1n, rgain, w_in, rec_dram, out_state):
    with ExitStack() as ctx:
        def sb(name, shape, dt=F32):
            return ctx.enter_context(nc.sbuf_tensor(name, shape, dt))

        def pb(name, shape):
            return ctx.enter_context(nc.psum_tensor(name, shape, F32))

        WR, WH, WL = W
        S = sb("states", [P, 2, NCH + 1, P])
        TK = sb("keys_values_t", [P, NT, 3, P])
        QD = sb("q_dec", [P, 2, T])
        KD = sb("k_dec", [P, 2, T])
        SIG = sb("sig_f", [P, 2, T])
        RQ, RIT, RG, ZR = sb("rq", [P, T]), sb("ri_t", [P, T]), sb("rg", [P, T]), sb("zr", [P, T])
        GB = sb("log_f", [P, T])
        BB = sb("cum_log_f", [P, T])
        RS = sb("rec_rstd", [P, G])
        AM = sb("masked_scores", [P, 2, 2 * P])
        M2 = sb("causal2", [P, 2 * P])
        EL = sb("chunk_decay", [P, 2, NCH])
        MK = sb("chunk_start", [P, T], BF16)
        LBr, LB1r = sb("lb_act", [P, 2]), sb("lb1_act", [P, 2])
        LBk, LBn = sb("lb1_dve", [P, 2]), sb("lb1n_dve", [P, 2])
        EPSB = sb("eps_r", [P, 1])
        OT = RIT

        proj = pb("proj_ps", [P, 2, 512])
        tps = pb("t_o_ps", [P, 2, 512])
        kvps = pb("kv_ps", [P, 2, 512])
        aps = pb("scores_ps", [P, 2, 512])

        raw_in = [sem("r_raw_in0"), sem("r_raw_in1")]
        w_go, w_hi, w_split = sem("r_w_go"), sem("r_w_hi"), sem("r_w_split")
        proj_done, proj_out = sem("r_proj_done"), sem("r_proj_out")
        log_f, cum_f, exp_f = sem("r_log_f"), sem("r_cum_f"), sem("r_exp_f")
        dir_ready, dve_ch = sem("r_dir_ready"), sem("r_dve_chain")
        t_done, t_out, kv_done = sem("r_t_done"), sem("r_t_out"), sem("r_kv_done")
        st = [sem("r_state_f"), sem("r_state_b")]
        a_done, a_out, o_done, o_out = sem("r_a_done"), sem("r_a_out"), sem("r_o_done"), sem("r_o_out")
        ss_done, ss_ln, ss_out = sem("r_ss_done"), sem("r_ss_ln"), sem("r_ss_out")
        rec_t, rec_ready = sem("r_rec_t"), sem("r_rec_ready")
        s0_in, rec_store, st_store = sem("r_s0_in"), sem("r_rec_store"), sem("r_state_store")
        m_in, mk_ok, zero_ok, lb_ok = sem("r_mask_in"), sem("r_mk_ok"), sem("r_zero_ok"), sem("r_lb_ok")

        UNITS = (B_RQ, B_RFF, B_RFB, B_RI, B_RG, B_ZR)
        NU = len(UNITS)
        PG = NU * NG
        C_SPLIT, C_PROJ, C_OUT = 2, 9, 2
        FWD = [(c, 18 if c == 1 else c + 1) for c in range(NCH)]
        BWD = [(c, 18 if c == 0 else c - 1) for c in reversed(range(NCH))]

        def links(d, j):
            return 2 * (j + 1) - (d == 0 and j == NT - 1) - (d == 1 and j >= NT - 2)

        with nc.Block() as block:
            @block.sync
            def _(sp):
                sp.dma_start(M2[:, :], a["c_mask"]).then_inc(m_in, 16)
                with sp.Fori(0, RH) as r:
                    for u, b0 in enumerate(UNITS):
                        sp.wait_ge(w_split, r * NU + (u - 2 + 1 + C_SPLIT))
                        sp.dma_start(WR[:, u % 2], w_in[r + b0]).then_inc(raw_in[u % 2], 16)
                    sp.wait_ge(o_done, r * NT + 1)
                    sp.dma_start(S[:, 0, 2, :], a["state_hgrn"][0, 0, 0][r]).then_inc(s0_in, 16)
                    sp.dma_start(S[:, 1, NCH - 1, :], a["state_hgrn"][0, 0, 1][r]).then_inc(s0_in, 16)
                for u in range(3):
                    sp.wait_ge(w_split, RH * NU + (u - 2 + 1 + C_SPLIT))
                    load_qkv(sp, WR, w_in, w_in64, 0, u, raw_in[u % 2])

            @block.gpsimd
            def _(pool):
                pool.sem_inc(w_split, C_SPLIT)
                def split(u, n0, raw, used):
                    pool.wait_ge(raw_in[u % 2], raw)
                    pool.wait_ge(proj_done, used)
                    pool.sem_inc(w_go, 1)
                    nc.gpsimd.tensor_copy(WH[:, u % 3], WR[:, u % 2]).then_inc(w_hi, 1)
                    pool.wait_ge(w_hi, n0 + (u + 1))
                    nc.gpsimd.tensor_tensor(WL[:, u % 3], WR[:, u % 2], WH[:, u % 3].bitcast(F32), ALU.subtract).then_inc(w_split, 1)

                with pool.Fori(0, RH) as r:
                    for u in range(NU):
                        split(u, r * NU, r * 48 + 16 * (u // 2 + 1), r * PG + (NG * (u - 3) + NG + C_PROJ))
                for u in range(3):
                    split(u, RH * NU, RH * 48 + (16, 16, 48)[u], RH * PG + NG * (u - 3) + NG + C_PROJ)

            @block.tensor
            def _(pe):
                pe.sem_inc(proj_done, C_PROJ)
                pe.sem_inc(t_done, 1)
                pe.sem_inc(o_done, 1)
                pe.wait_ge(m_in, 16)
                pe.wait_ge(zero_ok, 3)
                with pe.Fori(0, RH) as r:
                    for u in range(NU):
                        pe.wait_ge(w_split, r * NU + (u + 1 + C_SPLIT))
                        for g in range(NG):
                            n = NG * u + g
                            pe.wait_ge(proj_out, r * PG + (n - 2 + 1 + C_OUT))
                            for k in range(KC):
                                m = three_pass(nc, proj[:, n % 2, 0:G], WH[:, u % 3, k], WL[:, u % 3, k],
                                               HH[:, k, g * G:(g + 1) * G], HL[:, k, g * G:(g + 1) * G], k, k == KC - 1)
                            m.then_inc(proj_done, 1)
                    pe.wait_ge(dir_ready, r * 2 + 3)
                    pe.wait_ge(proj_out, r * PG + (12 + C_OUT))
                    for j in range(NT):
                        if j >= 2:
                            pe.wait_ge(t_out, r * NT + j - 1)
                        cols = slice(j * P, (j + 1) * P)
                        nc.tensor.transpose(tps[:, j % 2, 0:P], SIG[:, 0, cols], ident[:, :])
                        nc.tensor.transpose(tps[:, j % 2, P:2 * P], SIG[:, 1, cols], ident[:, :])
                        nc.tensor.transpose(tps[:, j % 2, 2 * P:3 * P], RIT[:, cols], ident[:, :]).then_inc(t_done, 1)
                    for j in range(NT):
                        pe.wait_ge(t_out, r * NT + NT)
                        if j >= 2:
                            for d in range(2):
                                pe.wait_ge(st[d], r * 17 + links(d, j - 2))
                        for q in range(4):
                            c = FWD[2 * j + q][0] if q < 2 else BWD[2 * j + q - 2][0]
                            rows = slice((c % 2) * CH, (c % 2 + 1) * CH)
                            bank = (kvps, aps)[c % 2]
                            m = nc.tensor.matmul(bank[:, j % 2, q // 2 * P:(q // 2 + 1) * P], TK[rows, c // 2, q // 2, :], TK[rows, c // 2, 2, :],
                                                 start=True, stop=True)
                        m.then_inc(kv_done, 1)

                    def scores(j):
                        if j >= 2:
                            pe.wait_ge(a_out, r * NT + j - 1)
                        cols = slice(j * P, (j + 1) * P)
                        for d in range(2):
                            m = nc.tensor.matmul(aps[:, j % 2, d * P:(d + 1) * P], KD[:, d, cols], QD[:, d, cols], start=True, stop=True)
                        m.then_inc(a_done, 1)

                    for s in st:
                        pe.wait_ge(s, r * 17 + 17)
                    scores(0)
                    pe.wait_ge(s0_in, r * 32 + 32)
                    for j in range(NT):
                        if j + 1 < NT:
                            scores(j + 1)
                        pe.wait_ge(a_out, r * NT + j + 1)
                        if j >= 2:
                            pe.wait_ge(o_out, r * 2 * NT + 2 * (j - 1))
                        o = tps[:, j % 2, 0:P]
                        for d in range(2):
                            nc.tensor.matmul(o, TK[:, j, 2, :], AM[:, j % 2, d * P:(d + 1) * P], start=(d == 0), stop=False)
                        for d in range(2):
                            for h in range(2):
                                c = 2 * j + h
                                m = nc.tensor.matmul(o[:, h * CH:(h + 1) * CH], S[:, d, c, :], QD[:, d, c * CH:(c + 1) * CH],
                                                     start=False, stop=(d == 1 and h == 1))
                        m.then_inc(o_done, 1)
                    for g in range(NG):
                        pe.wait_ge(o_out, r * 2 * NT + 6 * (g + 1))
                        if g == 2:
                            pe.wait_ge(ss_ln, r * NG + 1)
                        nc.tensor.matmul(kvps[:, g % 2, 0:G], ones[:, :], BB[:, g * G:(g + 1) * G], start=True, stop=True).then_inc(ss_done, 1)

            @block.scalar
            def _(act):
                act.sem_inc(proj_out, C_OUT)
                act.wait_ge(zero_ok, 3)
                with act.Fori(0, RH) as r:
                    def evacuate(u, dst, func):
                        for g in range(NG):
                            n = NG * u + g
                            act.wait_ge(proj_done, r * PG + (n + 1 + C_PROJ))
                            nc.scalar.activation(dst[:, g * G:(g + 1) * G], proj[:, n % 2, 0:G], func).then_inc(proj_out, 1)

                    def gate_logs(d):
                        nc.scalar.preload_act_table_set(LN_EXP)
                        if d == 0:
                            act.wait_ge(ss_done, r * NG + 1)
                        act.wait_ge(proj_out, r * PG + (6 + 3 * d + C_OUT))
                        act.wait_ge(dir_ready, r * 2 + d + 1)
                        nc.scalar.activation(GB[:, :], SIG[:, d, :], ACT.Ln, bias=LBr[:, d:d + 1], scale=LB1r[:, d:d + 1]).then_inc(log_f, 1)
                        act.wait_ge(cum_f, r * 2 + d + 1)
                        nc.scalar.activation(GB[:, :], BB[:, :], ACT.Exp)
                        nc.scalar.activation(BB[:, :], BB[:, :], ACT.Exp, scale=-1.0).then_inc(exp_f, 1)

                    lbv = lb[:, :].rearrange("p (d h) -> p h d", d=2)
                    lb1v = lb1[:, :].rearrange("p (d h) -> p h d", d=2)
                    act.wait_ge(dir_ready, r * 2 + 1)
                    nc.scalar.activation(LBr[:, :], lbv[:, bass.ds(r, 1), :].rearrange("p a d -> p (a d)"), ACT.Copy)
                    nc.scalar.activation(LB1r[:, :], lb1v[:, bass.ds(r, 1), :].rearrange("p a d -> p (a d)"), ACT.Copy).then_inc(lb_ok, 1)
                    act.wait_ge(lb_ok, r + 1)
                    evacuate(0, RQ, ACT.Silu)
                    act.wait_ge(t_done, r * NT + 1)
                    evacuate(1, SIG[:, 0], ACT.Sigmoid)
                    gate_logs(0)
                    evacuate(2, SIG[:, 1], ACT.Sigmoid)
                    gate_logs(1)
                    act.wait_ge(rec_store, r * 16 + 1)
                    evacuate(3, RIT, ACT.Copy)
                    evacuate(4, RG, ACT.Silu)
                    evacuate(5, ZR, ACT.Sigmoid)
                    act.wait_ge(o_done, r * NT + 1)
                    for j in range(NT):
                        act.wait_ge(t_done, r * NT + j + 2)
                        nc.scalar.activation(TK[:, j].rearrange("p a b -> p (a b)"), tps[:, j % 2, 0:3 * P], ACT.Copy).then_inc(t_out, 1)
                    for j in range(NT):
                        act.wait_ge(o_done, r * NT + j + 2)
                        nc.scalar.activation(OT[:, j * P:(j + 1) * P], tps[:, j % 2, 0:P], ACT.Copy).then_inc(o_out, 1)
                        nc.scalar.activation(BB[:, j * P:(j + 1) * P], tps[:, j % 2, 0:P], ACT.Square).then_inc(o_out, 1)
                    nc.scalar.preload_act_table_set(LN_EXP)
                    for g in range(NG):
                        act.wait_ge(ss_done, r * NG + g + 2)
                        act.wait_ge(rec_ready, r * NG + g + 1)
                        nc.scalar.activation(RS[:, :], kvps[:, g % 2, 0:G], ACT.Ln, scale=1.0 / P, bias=EPSB[:, 0:1]).then_inc(ss_ln, 1)
                        act.wait_ge(ss_ln, r * NG + g + 1)
                        nc.scalar.activation(RS[:, :], RS[:, :], ACT.Exp, scale=-0.5).then_inc(ss_out, 1)
                    act.wait_ge(rec_ready, r * NG + NG + 1)
                    act.dma_start(rec_dram[r], OT[:, :]).then_inc(rec_store, 16)
                    for d in range(2):
                        act.wait_ge(st[d], r * 17 + 17)
                        act.dma_start(out_state[0, 0, d][r], S[:, d, NCH, :]).then_inc(st_store, 16)
                act.wait_ge(rec_store, 16 * RH + 1)
                act.wait_ge(st_store, 32 * RH + 1)

            @block.vector
            def _(dve):
                dve.sem_inc(dir_ready, 1)
                dve.sem_inc(rec_ready, 1)
                dve.sem_inc(rec_store, 1)
                dve.sem_inc(st_store, 1)
                dve.sem_inc(ss_done, 1)
                nc.vector.memset(EPSB[:, :], EPS).then_inc(zero_ok, 1)
                nc.vector.memset(S[:, 0, 0, :], 0.0).then_inc(zero_ok, 1)
                nc.vector.memset(S[:, 1, 1, :], 0.0).then_inc(zero_ok, 1)
                nc.vector.memset(MK[:, :], 1.0).then_inc(mk_ok, 1)
                dve.wait_ge(mk_ok, 1)
                nc.vector.memset(MK[:, 0:T:CH], 0.0).then_inc(mk_ok, 1)
                dve.wait_ge(mk_ok, 2)
                dve.wait_ge(m_in, 16)
                with dve.Fori(0, RH) as r:
                    ch = Chain(dve, dve_ch, r * 8)
                    nc.vector.tensor_copy(LBk[:, :], lb1[:, :].rearrange("p (d h) -> p h d", d=2)[:, bass.ds(r, 1), :].rearrange("p a d -> p (a d)"))
                    ch.step(nc.vector.tensor_copy(LBn[:, :], lb1n[:, :].rearrange("p (d h) -> p h d", d=2)[:, bass.ds(r, 1), :].rearrange("p a d -> p (a d)")))
                    for d in range(2):
                        dve.wait_ge(dir_ready, r * 2 + d + 1)
                        dve.wait_ge(log_f, r * 2 + d + 1)
                        rev = slice(None, None, -1) if d else slice(None)
                        nc.vector.tensor_tensor_scan(BB[:, rev], MK[:, :], GB[:, rev], 0.0, ALU.mult, ALU.add).then_inc(cum_f, 1)
                        ch.wait()
                        ch.step(nc.vector.tensor_scalar(SIG[:, d, :], SIG[:, d, :], LBn[:, d:d + 1], LBk[:, d:d + 1], ALU.mult, ALU.add))
                        dve.wait_ge(exp_f, r * 2 + d + 1)
                        last = GB[:, CH - 1:T:CH] if d == 0 else GB[:, 0:T:CH]
                        ch.link(nc.vector.tensor_copy(EL[:, d, :], last))
                        ch.link(nc.vector.tensor_tensor(KD[:, d, :], SIG[:, d, :], BB[:, :], ALU.mult))
                        nc.vector.tensor_tensor(SIG[:, d, :].rearrange("p (c t) -> p c t", t=CH), KD[:, d, :].rearrange("p (c t) -> p c t", t=CH),
                                                EL[:, d, :].unsqueeze(2).broadcast_to((P, NCH, CH)), ALU.mult)
                        nc.vector.scalar_tensor_tensor(QD[:, d, :], RQ[:, :], float(P) ** -0.5, GB[:, :], ALU.mult, ALU.mult).then_inc(dir_ready, 1)
                    dve.wait_ge(proj_out, r * PG + (PG + C_OUT))
                    ch.step(nc.vector.tensor_tensor(RG[:, :], RG[:, :], ZR[:, :], ALU.mult))
                    dve.wait_ge(s0_in, r * 32 + 32)
                    dve.wait_ge(st_store, r * 32 + 1)
                    count = [0, 0]
                    for j in range(NT):
                        dve.wait_ge(kv_done, r * NT + j + 1)
                        for half in range(2):
                            for d, order in enumerate((FWD, BWD)):
                                c, nxt = order[2 * j + half]
                                used = (kvps, aps)[c % 2][:, j % 2, d * P:(d + 1) * P]
                                if (d, c) in ((0, NCH - 1), (1, 2)):
                                    continue
                                if count[d]:
                                    dve.wait_ge(st[d], r * 17 + count[d])
                                ins = nc.vector.scalar_tensor_tensor(S[:, d, nxt, :], S[:, d, c, :], EL[:, d, c:c + 1], used, ALU.mult, ALU.add)
                                ins.then_inc(st[d], 1)
                                count[d] += 1
                        assert count == [links(0, j), links(1, j)]
                    for j in range(NT):
                        dve.wait_ge(a_done, r * NT + j + 1)
                        if j >= 2:
                            dve.wait_ge(o_done, r * NT + j)
                        nc.vector.tensor_tensor(AM[:, j % 2, :], aps[:, j % 2, 0:2 * P], M2[:, :], ALU.mult).then_inc(a_out, 1)
                    ch.wait()
                    for g in range(NG):
                        dve.wait_ge(ss_out, r * NG + g + 1)
                        cols = slice(g * G, (g + 1) * G)
                        nc.vector.scalar_tensor_tensor(OT[:, cols], OT[:, cols], rgain[:, 0:1], RS[:, :], ALU.mult, ALU.mult).then_inc(rec_t, 1)
                        dve.wait_ge(rec_t, r * NG + g + 1)
                        nc.vector.tensor_tensor(OT[:, cols], OT[:, cols], RG[:, cols], ALU.mult).then_inc(rec_ready, 1)
                    assert ch.n == 8, ch.n


def phase2(nc, a, sem, W, w_o, HH, HL, ident, w_in, w_in64, rec_dram, mix_dram, out_k, out_v):
    with ExitStack() as ctx:
        def sb(name, shape, dt=F32):
            return ctx.enter_context(nc.sbuf_tensor(name, shape, dt))

        WR, W_HI, W_LO = W
        WX_HI, WX_LO = sb("w2_hi", [P, KC, P], F32R), sb("w2_lo", [P, KC, P], F32R)
        WH = [W_HI[:, 0], W_HI[:, 1], W_HI[:, 2], WX_HI[:, :, :]]
        WL = [W_LO[:, 0], W_LO[:, 1], W_LO[:, 2], WX_LO[:, :, :]]
        QKV = sb("qkv", [P, NT, G])
        KH = sb("keys_hi2", [P, NKC * P], F32R)
        KL = sb("keys_lo1", [HEAD + 1, NKC * P], F32R)
        V1 = sb("values_hi1", [P, NKC, P], F32R)
        V2 = sb("values_lo", [P, NKC, HEAD], F32R)
        PE32 = sb("probs", [P, 2, 512])
        PH = sb("probs_hi", [P, 4, 512], F32R)
        PL = sb("probs_lo", [P, 4, 512], F32R)
        KS = PH[:, :, :].rearrange("p a b -> p (a b)")[:, 0:2 * 3 * 3 * HEAD].rearrange("p (s i c) -> p s i c", s=2, i=3)
        QT1 = sb("q_t_hilo", [P, 2, 512], F32R)
        QT2 = sb("q_t_max", [HEAD + 1, 2, 512], F32R)
        QS1 = sb("q_stage", [P, GQ, P], F32R)
        QS2 = sb("q_stage_max", [P, GQ, HEAD + 2], F32R)
        ATT = sb("attn_t", [P, 2, T])
        ZA = sb("za_gate", [P, 2, T])
        COS, SIN = sb("cos", [P, NT - 1, HEAD]), sb("sin", [P, NT - 1, HEAD])
        R1, R2 = (ATT[:, :, :].rearrange("p a t -> p (a t)")[:, i * 15 * HEAD:(i + 1) * 15 * HEAD].rearrange("p (t c) -> p t c", t=3)
                  for i in range(2))
        SS, RST = sb("qk_ss", [P, 15]), sb("qk_rstd", [P, 15])
        M4 = sb("row_max", [P, GQ])
        RR = sb("inv_sum", [HEAD, 512])
        CK, CV = sb("cache_k_in", [P, 2, HEAD]), sb("cache_v_in", [P, 2, HEAD])
        GN = sb("qk_gain", [P, 2, HEAD])
        ps = ctx.enter_context(nc.psum_tensor("att_ps", [P, 8, 512], F32))
        B_S, B_QT, B_ST, B_PV, B_PROJ, B_KT = 0, 3, 4, 6, 4, 0

        raw_in = [sem("a_raw_in0"), sem("a_raw_in1")]
        w_go, w_hi, w_split = sem("a_w_go"), sem("a_w_hi"), sem("a_w_split")
        proj_done, proj_out = sem("a_proj_done"), sem("a_proj_out")
        ss_ok, rst_ln, rst_ok, n_ch = sem("a_ss_ok"), sem("a_rst_ln"), sem("a_rst_ok"), sem("a_norm_chain")
        ks_ok, kt_done, kt_out, v_ok = sem("a_ks_ok"), sem("a_kt_done"), sem("a_kt_out"), sem("a_v_ok")
        qs1_ok, qs2_ok, qt_done, qt_out = sem("a_qs1_ok"), sem("a_qs2_ok"), sem("a_qt_done"), sem("a_qt_out")
        qs_hi = sem("a_qs_hi")
        s_done, m_done = sem("a_s_done"), sem("a_m_done")
        st_done, ex_done, lo_done, pv_done = sem("a_st_done"), sem("a_ex_done"), sem("a_lo_done"), sem("a_pv_done")
        r_ln, r_ok, att_ok = sem("a_r_ln"), sem("a_r_ok"), sem("a_att_ok")
        za_mul, rec_in, mix_ok, mix_store = sem("a_za_mul"), sem("a_rec_in"), sem("a_mix_ok"), sem("a_mix_store")
        ctx_in, kv_store, const_in, set_ok = sem("a_ctx_in"), sem("a_kv_store"), sem("a_const_in"), sem("a_set_ok")

        NU, PG, C_SPLIT, C_PROJ, C_OUT = 5, 15, 2, 7, 2
        NS = 9
        NC = 1 + 10 * (NS - 1)

        MAX_AT = (1, 3, 5, 6)

        def keys(n):
            return range(0, 1) if n == 0 else range(1, NKC)

        def idx(n, i):
            return 0 if n == 0 else 1 + 10 * (n - 1) + i

        def slot(n, i):
            return 1 if n == 0 else i % 2

        def split_slot(n, i):
            return (idx(n, i) - 1) % 4

        def after(n, i):
            nc_ = len(keys(n))
            if n == 0:
                return (1, 1)
            if i + 2 < nc_:
                return (n, i + 2)
            return (n + 1, i + 2 - nc_) if n + 1 < NS else None

        with nc.Block() as block:
            def all_steps(eng, kv, step):
                step(0, 0)
                with eng.Fori(0, 3) as p:
                    step(1, p * 2)
                    step(2, p * 2)
                step(7, 0)
                step(8, 0)

            @block.sync
            def _(sp):
                for dst, src in ((COS[:, :, :], a["c_cos"].rearrange("(t p) d -> p t d", p=P)),
                                 (SIN[:, :, :], a["c_sin"].rearrange("(t p) d -> p t d", p=P)),
                                 (GN[:, 0, :], a["q_norm"][0].partition_broadcast(P)),
                                 (GN[:, 1, :], a["k_norm"][0].partition_broadcast(P))):
                    sp.dma_start(dst, src).then_inc(const_in, 16)
                def load(kv, u):
                    before = (0, -1, 1, 2, 3)[u]
                    sp.wait_ge(w_split, kv * NU + (before + C_SPLIT))
                    if u < 3:
                        load_qkv(sp, WR, w_in, w_in64, kv, u, raw_in[u % 2])
                    else:
                        sp.dma_start(WR[:, u % 2], w_in[kv * 2 + (B_ZA + u - 3)]).then_inc(raw_in[u % 2], 16)

                def load_head(kv):
                    load(kv, 3)
                    load(kv, 4)
                    sp.wait_ge(v_ok, kv + 1)
                    sp.wait_ge(ks_ok, kv * 4 + 1)
                    sp.dma_start(CK[:, :, :], a["cache_k"][0, 0].rearrange("(b p) h d -> h p b d", p=P)[kv]).then_inc(ctx_in, 16)
                    sp.dma_start(CV[:, :, :], a["cache_v"][0, 0].rearrange("(b p) h d -> h p b d", p=P)[kv]).then_inc(ctx_in, 16)
                    sp.wait_ge(ks_ok, kv * 4 + 2)
                    sp.dma_start(out_k[0, 0].rearrange("t h d -> h t d")[kv], QKV[:, 0, 4 * HEAD:5 * HEAD]).then_inc(kv_store, 16)
                    sp.dma_start(out_v[0, 0].rearrange("t h d -> h t d")[kv], QKV[:, 0, 5 * HEAD:6 * HEAD]).then_inc(kv_store, 16)

                with sp.Fori(0, NKV - 1) as kv:
                    load_head(kv)
                    for u in range(3):
                        load(kv + 1, u)
                load_head(NKV - 1)
                for u in range(2):
                    sp.wait_ge(w_split, (NKV - 1) * NU + (5 if u == 0 else 4) + C_SPLIT)
                    sp.dma_start(WR[:, u], w_o[u]).then_inc(raw_in[u], 16)
                sp.wait_ge(kv_store, 32 * NKV + 1)

            @block.gpsimd
            def _(pool):
                pool.sem_inc(w_split, C_SPLIT + 3)
                pool.sem_inc(w_hi, 3)
                pool.sem_inc(raw_in[0], 48)
                pool.sem_inc(raw_in[1], 16)

                def split(u, n0, raw, used):
                    pool.wait_ge(raw_in[u % 2], raw)
                    pool.wait_ge(proj_done, used)
                    pool.sem_inc(w_go, 1)
                    nc.gpsimd.tensor_copy(WH[u % 4], WR[:, u % 2]).then_inc(w_hi, 1)
                    pool.wait_ge(w_hi, n0 + (u + 1))
                    nc.gpsimd.tensor_tensor(WL[u % 4], WR[:, u % 2], WH[u % 4].bitcast(F32), ALU.subtract).then_inc(w_split, 1)

                def split_unit(kv, u):
                    split(u, kv * NU, kv * (64, 32)[u % 2] + (16, 16, 48, 32, 64)[u], kv * PG + (7, 1, 1, 4, 16)[u])

                with pool.Fori(0, NKV - 1) as kv:
                    split_unit(kv, 3)
                    split_unit(kv, 4)
                    for u in range(3):
                        split_unit(kv + 1, u)
                split_unit(NKV - 1, 3)
                split_unit(NKV - 1, 4)
                for u in range(2):
                    split(u, NKV * NU, NKV * (64, 32)[u] + 16, NKV * PG + C_PROJ)

            def key_transposes(pe, kv, g):
                pe.wait_ge(ks_ok, kv * 4 + g + 2)
                pe.wait_ge(kt_out, kv * 8 + (2 * (g - 1) if g >= 2 else 0) + 2)
                n = 3 if g < 3 else 2
                for i in range(n):
                    m = nc.tensor.transpose(ps[:, B_KT + 2 * (g % 2), i * P:(i + 1) * P], KS[:, g % 2, i, 0:P].bitcast(F32), ident[:, :])
                for i in range(n):
                    m = nc.tensor.transpose(ps[0:HEAD, B_KT + 2 * (g % 2) + 1, i * P:(i + 1) * P], KS[:, g % 2, i, P:3 * HEAD].bitcast(F32), ident[:, :])
                m.then_inc(kt_done, 1)

            @block.tensor
            def _(pe):
                pe.sem_inc(proj_done, C_PROJ)
                pe.sem_inc(kt_done, 1)
                pe.wait_ge(set_ok, 2)
                with pe.Fori(0, NKV) as kv:
                    for n in range(PG):
                        if n == 0:
                            pe.wait_ge(w_split, kv * NU + (3 + C_SPLIT))
                            pe.wait_ge(proj_out, kv * PG + C_OUT)
                            pe.wait_ge(att_ok, kv * NS + 1)
                        else:
                            pe.wait_ge(proj_out, kv * PG + (n - 1 + C_OUT))
                        bank = ps[:, B_PROJ + n % 2, 0:G]
                        if n < NT:
                            cols = slice(n * P, (n + 1) * P)
                            for k in range(KC):
                                nc.tensor.matmul(bank, HH[:, k, cols], W_HI[:, :, k, :], start=(k == 0), stop=False)
                                nc.tensor.matmul(bank, HL[:, k, cols], W_HI[:, :, k, :], start=False, stop=False)
                                m = nc.tensor.matmul(bank, HH[:, k, cols], W_LO[:, :, k, :], start=False, stop=(k == KC - 1))
                        else:
                            u, g = 3 + (n - NT) // NG, (n - NT) % NG
                            if g == 0:
                                pe.wait_ge(w_split, kv * NU + (u + 1 + C_SPLIT))
                            for k in range(KC):
                                m = three_pass(nc, bank, WH[u % 4][:, k], WL[u % 4][:, k],
                                               HH[:, k, g * G:(g + 1) * G], HL[:, k, g * G:(g + 1) * G], k, k == KC - 1)
                        m.then_inc(proj_done, 1)
                        if n >= NT + 2:
                            key_transposes(pe, kv, n - NT - 2)

                    def wait_step(sem_, per_kv, count, o, per_step):
                        pe.wait_ge(sem_, kv * per_kv + o * per_step + count)

                    def q_part(n, o):
                        wait_step(qs1_ok, NS, n + 1, o, 1)
                        wait_step(qt_out, 2 * NS, 2 * n + 1, o, 2)
                        for h in range(GQ):
                            m = nc.tensor.transpose(ps[:, B_QT, h * P:(h + 1) * P], QS1[:, h, :].bitcast(F32), ident[:, :])
                        m.then_inc(qt_done, 1)

                    def max_scores(n, o, h):
                        if h == 0:
                            wait_step(qt_out, 2 * NS, 2 * n + 2, o, 2)
                        wait_step(m_done, 4 * NS, 4 * n + h + 1, o, 4)
                        k0, k1 = keys(n)[0] * P, (keys(n)[-1] + 1) * P
                        for i, c in enumerate(range(k0, k1, 512)):
                            w = min(512, k1 - c)
                            m = nc.tensor.matmul(ps[:, B_S + i, 0:w], QT1[:, n % 2, h * P:(h + 1) * P], KH[:, c:c + w], start=True, stop=True)
                        m.then_inc(s_done, 1)

                    def q_max_part(n, o):
                        wait_step(qs2_ok, NS, n + 2, o, 1)
                        for h in range(GQ):
                            m = nc.tensor.transpose(ps[0:HEAD + 1, B_QT, h * P:(h + 1) * P], QS2[:, h, 0:HEAD + 1].bitcast(F32), ident[:, :])
                        m.then_inc(qt_done, 1)

                    def scores_t(n, o, i):
                        g = idx(n, i)
                        if i == 0:
                            wait_step(qt_out, 2 * NS, 2 * n + 3, o, 2)
                        wait_step(ex_done, NC, max(g - 1, 0) + 1, o, 10)
                        c = keys(n)[i] * P
                        bank = ps[:, B_ST + slot(n, i), :]
                        nc.tensor.matmul(bank, KH[:, c:c + P], QT1[:, n % 2, :], start=True, stop=False)
                        nc.tensor.matmul(bank, KL[:, c:c + P], QT2[:, n % 2, :], start=False, stop=True).then_inc(st_done, 1)

                    def weighted(n, o, i):
                        if i == 0:
                            wait_step(att_ok, NS, max(n, 1), o, 1)
                        wait_step(lo_done, NC, idx(n, i) + 2, o, 10)
                        c, s = keys(n)[i], split_slot(n, i)
                        last = i == len(keys(n)) - 1
                        nc.tensor.matmul(ps[:, B_PV + n % 2, :], V1[:, c, :], PH[:, s, :], start=(i == 0), stop=False)
                        nc.tensor.matmul(ps[0:HEAD, B_PV + n % 2, :], V2[:, c, :], PH[:, s, :], start=False, stop=False)
                        nc.tensor.matmul(ps[:, B_PV + n % 2, :], V1[:, c, :], PL[:, s, :], start=False, stop=last).then_inc(pv_done, 1)

                    pe.wait_ge(kt_out, kv * 8 + 10)
                    pe.wait_ge(v_ok, kv + 2)
                    q_part(0, 0)
                    for h in range(GQ):
                        max_scores(0, 0, h)
                    q_max_part(0, 0)
                    scores_t(0, 0, 0)

                    def step(n, o):
                        if n == 0:
                            q_part(1, o)
                            for h in range(GQ):
                                max_scores(1, o, h)
                            q_max_part(1, o)
                            scores_t(1, o, 0)
                        for i in range(len(keys(n))):
                            if n and n + 1 < NS:
                                if i == 0:
                                    q_part(n + 1, o)
                                elif i in MAX_AT:
                                    max_scores(n + 1, o, MAX_AT.index(i))
                            if after(n, i):
                                scores_t(after(n, i)[0], o, after(n, i)[1])
                            if i == 7 and n and n + 1 < NS:
                                q_max_part(n + 1, o)
                            weighted(n, o, i)

                    all_steps(pe, kv, step)

            @block.scalar
            def _(act):
                act.sem_inc(proj_out, C_OUT)
                act.sem_inc(kt_out, 2)
                act.sem_inc(qt_out, 1)
                act.sem_inc(ex_done, 1)
                with act.Fori(0, NKV) as kv:
                    def wait_step(sem_, per_kv, count, o, per_step):
                        act.wait_ge(sem_, kv * per_kv + o * per_step + count)

                    act.wait_ge(kv_store, kv * 32 + 1)
                    act.wait_ge(mix_store, kv * 32 + 1)
                    for n in range(PG):
                        act.wait_ge(proj_done, kv * PG + (n + 1 + C_PROJ))
                        bank = ps[:, B_PROJ + n % 2, 0:G]
                        if n < NT:
                            nc.scalar.activation(QKV[:, n, :], bank, ACT.Copy).then_inc(proj_out, 1)
                        else:
                            g = (n - NT) % NG
                            nc.scalar.activation(ZA[:, (n - NT) // NG, g * G:(g + 1) * G], bank, ACT.Sigmoid).then_inc(proj_out, 1)
                        if n == 3:
                            nc.scalar.preload_act_table_set(LN_EXP)
                        if n in (3, 6, 9):
                            g = n // 3 - 1
                            act.wait_ge(ss_ok, kv * 3 + g + 1)
                            nc.scalar.activation(RST[:, :], SS[:, :], ACT.Ln).then_inc(rst_ln, 1)
                            act.wait_ge(rst_ln, kv * 3 + g + 1)
                            nc.scalar.activation(RST[:, :], RST[:, :], ACT.Exp, scale=-0.5).then_inc(rst_ok, 1)
                        if n >= NT + 2:
                            g = n - NT - 2
                            w = (3 if g < 3 else 2) * P
                            act.wait_ge(kt_done, kv * 4 + g + 2)
                            nc.scalar.activation(KH[:, 3 * g * P:3 * g * P + w], ps[:, B_KT + 2 * (g % 2), 0:w], ACT.Copy).then_inc(kt_out, 1)
                            nc.scalar.activation(KL[0:HEAD, 3 * g * P:3 * g * P + w], ps[0:HEAD, B_KT + 2 * (g % 2) + 1, 0:w], ACT.Copy).then_inc(kt_out, 1)

                    nc.scalar.preload_act_table_set(LN_EXP)

                    def q_out(n, o):
                        wait_step(qt_done, 2 * NS, 2 * n + 1, o, 2)
                        nc.scalar.activation(QT1[:, n % 2, :], ps[:, B_QT, :], ACT.Copy).then_inc(qt_out, 1)

                    def q_max_out(n, o):
                        wait_step(qt_done, 2 * NS, 2 * n + 2, o, 2)
                        nc.scalar.activation(QT2[:, n % 2, :], ps[0:HEAD + 1, B_QT, :], ACT.Copy).then_inc(qt_out, 1)

                    def exp(n, o, i):
                        g = idx(n, i)
                        wait_step(st_done, NC, g + 1, o, 10)
                        wait_step(lo_done, NC, max(g - 1, 0) + 1, o, 10)
                        nc.scalar.activation(PE32[:, slot(n, i), :], ps[:, B_ST + slot(n, i), :], ACT.Exp, scale=HEAD ** -0.5)
                        if g >= 4:
                            wait_step(pv_done, NC, g - 3, o, 10)
                        nc.scalar.activation(PH[:, split_slot(n, i), :], ps[:, B_ST + slot(n, i), :], ACT.Exp, scale=HEAD ** -0.5).then_inc(ex_done, 1)

                    def inverse_sum(n, o):
                        wait_step(pv_done, NC, idx(n, len(keys(n)) - 1) + 1, o, 10)
                        wait_step(att_ok, NS, n + 1, o, 1)
                        nc.scalar.activation(RR[:, :], ps[HEAD:P, B_PV + n % 2, :], ACT.Ln).then_inc(r_ln, 1)
                        wait_step(r_ln, NS, n + 1, o, 1)
                        nc.scalar.activation(RR[:, :], RR[:, :], ACT.Exp, scale=-1.0).then_inc(r_ok, 1)

                    q_out(0, 0)
                    q_max_out(0, 0)
                    exp(0, 0, 0)

                    def step(n, o):
                        if n == 0:
                            q_out(1, o)
                            q_max_out(1, o)
                            exp(1, o, 0)
                        for i in range(len(keys(n))):
                            if i == 0 and n and n + 1 < NS:
                                q_out(n + 1, o)
                            if after(n, i):
                                exp(after(n, i)[0], o, after(n, i)[1])
                            if i == 0 and n:
                                inverse_sum(n - 1, o)
                            if i == 7 and n and n + 1 < NS:
                                q_max_out(n + 1, o)

                    all_steps(act, kv, step)
                    inverse_sum(NS - 1, 0)
                    act.wait_ge(za_mul, kv + 1)
                    for j in range(2):
                        act.dma_start(ZA[:, j, :], rec_dram[kv * 2 + j]).then_inc(rec_in, 16)
                    for j in range(2):
                        act.wait_ge(mix_ok, kv * 2 + j + 1)
                        act.dma_start(mix_dram[kv * 2 + j], ATT[:, j, :]).then_inc(mix_store, 16)
                act.wait_ge(mix_store, 32 * NKV + 1)

            @block.vector
            def _(dve):
                nc.vector.memset(KL[HEAD:HEAD + 1, :].bitcast(F32), 1.0).then_inc(set_ok, 1)
                nc.vector.memset(V1[:, :, HEAD:P].bitcast(F32), 1.0).then_inc(set_ok, 1)
                for s in (v_ok, ks_ok, kv_store, mix_store, m_done, lo_done, att_ok, qs2_ok):
                    dve.sem_inc(s, 1)
                dve.wait_ge(const_in, 64)
                with dve.Fori(0, NKV) as kv:
                    def wait_step(sem_, per_kv, count, o, per_step):
                        dve.wait_ge(sem_, kv * per_kv + o * per_step + count)

                    ch = Chain(dve, n_ch, kv * CHAIN2)

                    def stage_keys(g, src, n):
                        dve.wait_ge(kt_done, kv * 4 + (g - 1 if g >= 2 else 0) + 1)
                        ch.wait()
                        st = KS[:, g % 2, 0:n, :]
                        nc.vector.tensor_copy(st[:, :, 0:HEAD], src)
                        ch.link(nc.vector.tensor_copy(st[:, :, HEAD:P], src))
                        nc.vector.tensor_tensor(st[:, :, P:3 * HEAD], src, st[:, :, 0:HEAD].bitcast(F32), ALU.subtract).then_inc(ks_ok, 1)

                    for g in range(3):
                        dve.wait_ge(proj_out, kv * PG + (3 * g + 3 + C_OUT))
                        if g:
                            ch.wait()
                        x = QKV[:, 3 * g:3 * g + 3, 0:5 * HEAD]
                        x4 = x.rearrange("p t (h d) -> p t h d", d=HEAD)
                        ch.link(nc.vector.tensor_tensor(R1[:, :, :], x, x, ALU.mult))
                        ch.link(nc.vector.tensor_reduce(SS[:, :], R1[:, :, :].rearrange("p t (h d) -> p (t h) d", d=HEAD), AX_X, ALU.add))
                        nc.vector.tensor_scalar(SS[:, :], SS[:, :], 1.0 / HEAD, EPS, ALU.mult, ALU.add).then_inc(ss_ok, 1)
                        dve.wait_ge(rst_ok, kv * 3 + g + 1)
                        ch.link(nc.vector.tensor_tensor(x4, x4, RST[:, :].rearrange("p (t h) -> p t h", t=3).unsqueeze(3).broadcast_to((P, 3, 5, HEAD)), ALU.mult))
                        ch.step(nc.vector.tensor_tensor(x4[:, :, 0:4, :], x4[:, :, 0:4, :], GN[:, 0, :].unsqueeze(1).unsqueeze(1).broadcast_to((P, 3, 4, HEAD)), ALU.mult))
                        ch.link(nc.vector.tensor_tensor(x4[:, :, 4, :], x4[:, :, 4, :], GN[:, 1, :].unsqueeze(1).broadcast_to((P, 3, HEAD)), ALU.mult))
                        tiles = [t for t in range(3 * g, 3 * g + 3) if t]
                        for t in tiles:
                            i = t - 3 * g
                            xt = QKV[:, t, 0:5 * HEAD].rearrange("p (h d) -> p h d", d=HEAD)
                            nc.vector.tensor_tensor(R1[:, i, :].rearrange("p (h d) -> p h d", d=HEAD), xt,
                                                    COS[:, t - 1, :].unsqueeze(1).broadcast_to((P, 5, HEAD)), ALU.mult)
                            for half in range(2):
                                v = lambda z: z.rearrange("p h (s b e) -> p h s b e", s=2, b=2)
                                m = nc.vector.tensor_tensor(v(R2[:, i, :].rearrange("p (h d) -> p h d", d=HEAD))[:, :, :, half, :],
                                                            v(xt)[:, :, :, 1 - half, :],
                                                            SIN[:, t - 1, :].rearrange("p (s b e) -> p s b e", s=2, b=2)[:, :, half, :].unsqueeze(1).broadcast_to((P, 5, 2, 16)), ALU.mult)
                        ch.link(m)
                        i0 = tiles[0] - 3 * g
                        ch.link(nc.vector.tensor_tensor(QKV[:, tiles[0]:3 * g + 3, 0:5 * HEAD], R1[:, i0:3, :], R2[:, i0:3, :], ALU.add))
                        stage_keys(g, QKV[:, 3 * g:3 * g + 3, 4 * HEAD:5 * HEAD], 3)
                    dve.wait_ge(ctx_in, kv * 32 + 32)
                    stage_keys(3, CK[:, :, :], 2)
                    val = QKV[:, :, 5 * HEAD:6 * HEAD]
                    ch.step(nc.vector.tensor_copy(V1[:, 0:NT, 0:HEAD], val))
                    ch.link(nc.vector.tensor_copy(V1[:, NT:NKC, 0:HEAD], CV[:, :, :]))
                    ch.link(nc.vector.tensor_tensor(V2[:, 0:NT, :], val, V1[:, 0:NT, 0:HEAD].bitcast(F32), ALU.subtract))
                    nc.vector.tensor_tensor(V2[:, NT:NKC, :], CV[:, :, :], V1[:, NT:NKC, 0:HEAD].bitcast(F32), ALU.subtract).then_inc(v_ok, 1)

                    def stage_q(n, o):
                        if n:
                            wait_step(qt_done, 2 * NS, 2 * n, o, 2)
                        q = (QKV[:, n, 0:4 * HEAD] if isinstance(o, int) else QKV[:, bass.ds(o + n, 1), 0:4 * HEAD].rearrange("p a d -> p (a d)"))
                        q = q.rearrange("p (h d) -> p h d", d=HEAD)
                        nc.vector.tensor_copy(QS2[:, :, 0:HEAD], q)
                        nc.vector.tensor_copy(QS1[:, :, 0:HEAD], q).then_inc(qs_hi, 1)
                        wait_step(qs_hi, NS, n + 1, o, 1)
                        nc.vector.tensor_tensor(QS1[:, :, HEAD:P], q, QS1[:, :, 0:HEAD].bitcast(F32), ALU.subtract).then_inc(qs1_ok, 1)

                    def row_max(n, o, h):
                        wait_step(s_done, 4 * NS, 4 * n + h + 1, o, 4)
                        if h == 0:
                            wait_step(qs2_ok, NS, n + 1, o, 1)
                        w = len(keys(n)) * P
                        s = ps[:, B_S:B_S + 3, :].rearrange("p a b -> p (a b)")[:, 0:w]
                        nc.vector.tensor_reduce(M4[:, h:h + 1], s, AX_X, ALU.max).then_inc(m_done, 1)

                    def put_max(n, o):
                        wait_step(m_done, 4 * NS, 4 * n + 5, o, 4)
                        nc.vector.tensor_scalar(QS2[:, :, HEAD], M4[:, :], -1.0, None, ALU.mult).then_inc(qs2_ok, 1)

                    def low(n, o, i):
                        g = idx(n, i)
                        wait_step(ex_done, NC, g + 2, o, 10)
                        if g >= 4:
                            wait_step(pv_done, NC, g - 3, o, 10)
                        s = split_slot(n, i)
                        nc.vector.tensor_tensor(PL[:, s, :], PE32[:, slot(n, i), :], PH[:, s, :].bitcast(F32), ALU.subtract).then_inc(lo_done, 1)

                    def normalise(n, o):
                        wait_step(r_ok, NS, n + 1, o, 1)
                        for par in range(2):
                            out = ATT[par * HEAD:(par + 1) * HEAD, :, :]
                            out = out[:, :, n * P:(n + 1) * P] if isinstance(o, int) else out[:, :, bass.ds(o * P + n * P, P)]
                            m = nc.vector.tensor_tensor(out, ps[0:HEAD, B_PV + n % 2, :].rearrange("p (j b q) -> p b j q", j=2, b=2)[:, par],
                                                        RR[:, :].rearrange("p (j b q) -> p b j q", j=2, b=2)[:, par], ALU.mult)
                        m.then_inc(att_ok, 1)

                    stage_q(0, 0)
                    for h in range(GQ):
                        row_max(0, 0, h)
                    put_max(0, 0)
                    stage_q(1, 0)
                    low(0, 0, 0)

                    def step(n, o):
                        if n == 0:
                            for h in range(GQ):
                                row_max(1, o, h)
                            put_max(1, o)
                            stage_q(2, o)
                            low(1, o, 0)
                        for i in range(len(keys(n))):
                            if n and n + 1 < NS and i in MAX_AT:
                                row_max(n + 1, o, MAX_AT.index(i))
                                if i == MAX_AT[-1]:
                                    put_max(n + 1, o)
                            if i == 8 and n and n + 2 < NS:
                                stage_q(n + 2, o)
                            if after(n, i):
                                low(after(n, i)[0], o, after(n, i)[1])
                            if i == 0 and n:
                                normalise(n - 1, o)

                    all_steps(dve, kv, step)
                    normalise(NS - 1, 0)
                    dve.wait_ge(att_ok, kv * NS + NS + 1)
                    dve.wait_ge(mix_store, kv * 32 + 1)
                    nc.vector.tensor_tensor(ATT[:, :, :], ATT[:, :, :], ZA[:, :, :], ALU.mult).then_inc(za_mul, 1)
                    dve.wait_ge(za_mul, kv + 1)
                    dve.wait_ge(rec_in, kv * 32 + 32)
                    for j in range(2):
                        nc.vector.tensor_tensor(ATT[:, j, :], ATT[:, j, :], ZA[:, j, :], ALU.add).then_inc(mix_ok, 1)
                    assert ch.n == CHAIN2, ch.n



def phase3(nc, a, sem, W, w_up, HH, HL, ident, ones, MOD, A2, X1, w_o, mix_dram):
    with ExitStack() as ctx:
        def sb(name, shape, dt=F32):
            return ctx.enter_context(nc.sbuf_tensor(name, shape, dt))

        WR, WH, WL = W
        X = sb("x3", [P, 2, D])
        MS = sb("mix_in", [P, 2, T])
        SQ = sb("sq3", [P, T])
        RS = sb("rs3", [P, T])
        PRE = sb("pre3", [P, 2, T])
        EPSB = sb("eps3", [P, 1])
        ps = ctx.enter_context(nc.psum_tensor("out_ps", [P, 8, 512], F32))

        raw_in = [sem("o_raw_in0"), sem("o_raw_in1")]
        w_go, w_hi, w_split = sem("o_w_go"), sem("o_w_hi"), sem("o_w_split")
        x_in = [sem("o_x_in0"), sem("o_x_in1")]
        mix_in = [sem("o_mix_in0"), sem("o_mix_in1")]
        xt_done, xt_out = sem("o_xt_done"), sem("o_xt_out")
        mh, ml = sem("o_mix_hi"), sem("o_mix_lo")
        proj_done, res_ok = sem("o_proj_done"), sem("o_res_ok")
        sq_ok, ss_done, ss_ln, rs_ok = sem("o_sq_ok"), sem("o_ss_done"), sem("o_ss_ln"), sem("o_rs_ok")
        pre_ok, hi_ok, lo_ok, set_ok = sem("o_pre_ok"), sem("o_hi_ok"), sem("o_lo_ok"), sem("o_set_ok")
        C_SPLIT, C_PROJ = 2, 6

        def x_rows(t):
            return a["x_prompt"][0] if t == 0 else a["x_sample"][0, (t - 1) * P:t * P, :]

        with nc.Block() as block:
            @block.sync
            def _(sp):
                for t in range(NT):
                    if t >= 2:
                        sp.wait_ge(xt_done, 2 * (t - 1))
                    sp.dma_start(X[:, t % 2, :], x_rows(t)).then_inc(x_in[t % 2], 16)
                    if t < KC:
                        if t >= 2:
                            sp.wait_ge(ml, t - 1)
                        sp.dma_start(MS[:, t % 2, :], mix_dram[t]).then_inc(mix_in[t % 2], 16)
                with sp.Fori(1, KC // 2) as i:
                    for u in range(2):
                        sp.wait_ge(w_split, i * 2 + u + 1)
                        sp.dma_start(WR[:, u], w_o[i * 2 + u]).then_inc(raw_in[u], 16)
                for u in range(2):
                    sp.wait_ge(w_split, KC + u + 1)
                    sp.dma_start(WR[:, u], w_up[u * FB]).then_inc(raw_in[u], 16)

            @block.gpsimd
            def _(pool):
                pool.sem_inc(w_split, C_SPLIT + 2)
                pool.sem_inc(w_hi, 2)
                for s in raw_in:
                    pool.sem_inc(s, 16)

                def split(i, u):
                    pool.wait_ge(raw_in[u], i * 16 + 16)
                    pool.wait_ge(proj_done, i * 6 + (NG * (u - 2) + NG + C_PROJ))
                    pool.sem_inc(w_go, 1)
                    nc.gpsimd.tensor_copy(WH[:, u], WR[:, u]).then_inc(w_hi, 1)
                    pool.wait_ge(w_hi, i * 2 + u + 1)
                    nc.gpsimd.tensor_tensor(WL[:, u], WR[:, u], WH[:, u].bitcast(F32), ALU.subtract).then_inc(w_split, 1)

                with pool.Fori(1, KC // 2) as i:
                    for u in range(2):
                        split(i, u)
                for u in range(2):
                    split(KC // 2, u)

            @block.tensor
            def _(pe):
                pe.sem_inc(proj_done, C_PROJ)
                for t in range(NT):
                    pe.wait_ge(x_in[t % 2], 16 * (t // 2 + 1))
                    for q in range(2):
                        n = 2 * t + q
                        if n >= 4:
                            pe.wait_ge(xt_out, n - 3)
                        for i in range(4):
                            m = nc.tensor.transpose(ps[:, n % 4, i * P:(i + 1) * P], X[:, t % 2, (4 * q + i) * P:(4 * q + i + 1) * P], ident[:, :])
                        m.then_inc(xt_done, 1)
                pe.wait_ge(ml, KC)
                pe.wait_ge(xt_out, 2 * NT)
                with pe.Fori(0, KC // 2) as i:
                    for u in range(2):
                        pe.wait_ge(w_split, i * 2 + u + 1 + C_SPLIT)
                        for g in range(NG):
                            n = NG * u + g
                            pe.wait_ge(res_ok, i * 6 + n + 1)
                            for k in range(KC):
                                m = three_pass(nc, ps[:, n, 0:G], WH[:, u, k], WL[:, u, k],
                                               HH[:, k, g * G:(g + 1) * G], HL[:, k, g * G:(g + 1) * G], k, k == KC - 1)
                            m.then_inc(proj_done, 1)
                pe.wait_ge(res_ok, 6 * (KC // 2) + 6)
                for j in range(KC):
                    pe.wait_ge(sq_ok, j + 1)
                    for g in range(NG):
                        m = nc.tensor.matmul(ps[:, g, 0:G], ones[:, :], SQ[:, g * G:(g + 1) * G], start=(j == 0), stop=(j == KC - 1))
                    m.then_inc(ss_done, 1)

            @block.scalar
            def _(act):
                for t in range(NT):
                    for q in range(2):
                        n = 2 * t + q
                        act.wait_ge(xt_done, n + 1)
                        nc.scalar.activation(X1[:, 4 * q:4 * q + 4, t * P:(t + 1) * P], ps[:, n % 4, :].rearrange("p (j c) -> p j c", j=4), ACT.Copy).then_inc(xt_out, 1)
                    if t < KC:
                        act.wait_ge(mix_in[t % 2], 16 * (t // 2 + 1))
                        nc.scalar.activation(HH[:, t, :], MS[:, t % 2, :], ACT.Copy).then_inc(mh, 1)
                nc.scalar.preload_act_table_set(LN_EXP)
                act.wait_ge(res_ok, 6 * (KC // 2) + 6)
                act.wait_ge(set_ok, 1)
                for j in range(KC):
                    if j:
                        act.wait_ge(ss_done, j)
                    nc.scalar.activation(SQ[:, :], X1[:, j, :], ACT.Square).then_inc(sq_ok, 1)
                act.wait_ge(ss_done, KC)
                for g in range(NG):
                    nc.scalar.activation(RS[:, g * G:(g + 1) * G], ps[:, g, 0:G], ACT.Ln, scale=1.0 / D, bias=EPSB[:, 0:1]).then_inc(ss_ln, 1)
                act.wait_ge(ss_ln, NG)
                nc.scalar.activation(RS[:, :], RS[:, :], ACT.Exp, scale=-0.5).then_inc(rs_ok, 1)
                for j in range(KC):
                    act.wait_ge(pre_ok, 2 * j + 2)
                    for grp, (t0, t1) in enumerate(RANGES):
                        nc.scalar.activation(HH[:, j, t0:t1], PRE[:, j % 2, t0:t1], ACT.Identity, bias=MOD[:, 24 + j, grp:grp + 1]).then_inc(hi_ok, 1)

            @block.vector
            def _(dve):
                nc.vector.memset(EPSB[:, :], EPS).then_inc(set_ok, 1)
                dve.sem_inc(res_ok, 6)
                for k in range(KC):
                    dve.wait_ge(mh, k + 1)
                    nc.vector.tensor_tensor(HL[:, k, :], MS[:, k % 2, :], HH[:, k, :].bitcast(F32), ALU.subtract).then_inc(ml, 1)
                dve.wait_ge(xt_out, 2 * NT)
                with dve.Fori(0, KC // 2) as i:
                    for u in range(2):
                        for g in range(NG):
                            n = NG * u + g
                            dve.wait_ge(proj_done, i * 6 + n + 1 + C_PROJ)
                            for t0, t1, grp in split_groups(g):
                                x = X1[:, bass.ds(i * 2 + u, 1), t0:t1].rearrange("p a t -> p (a t)")
                                gate = MOD[:, bass.ds(i * 2 + (16 + u), 1), grp:grp + 1].rearrange("p a t -> p (a t)")
                                m = nc.vector.scalar_tensor_tensor(x, ps[:, n, t0 - g * G:t1 - g * G], gate, x, ALU.mult, ALU.add)
                            m.then_inc(res_ok, 1)
                dve.wait_ge(rs_ok, 1)
                def low(j):
                    for grp, (t0, t1) in enumerate(RANGES):
                        dve.wait_ge(hi_ok, 2 * j + grp + 1)
                        nc.vector.scalar_tensor_tensor(HL[:, j, t0:t1], PRE[:, j % 2, t0:t1], MOD[:, 24 + j, grp:grp + 1],
                                                       HH[:, j, t0:t1].bitcast(F32), ALU.add, ALU.subtract).then_inc(lo_ok, 1)
                for j in range(KC):
                    if j >= 2:
                        dve.wait_ge(lo_ok, 2 * (j - 1))
                    for grp, (t0, t1) in enumerate(RANGES):
                        nc.vector.scalar_tensor_tensor(PRE[:, j % 2, t0:t1], X1[:, j, t0:t1], A2[:, j, grp:grp + 1], RS[:, t0:t1],
                                                       ALU.mult, ALU.mult).then_inc(pre_ok, 1)
                    if j:
                        low(j - 1)
                low(KC - 1)


def phase4(nc, a, sem, W, HH, HL, MOD, CW, X1, w_up, w_down):
    with ExitStack() as ctx:
        def sb(name, shape, dt=F32):
            return ctx.enter_context(nc.sbuf_tensor(name, shape, dt))

        W_RAW, WH, WL = W
        WX_RAW = sb("w4_raw", [P, KC, P])
        WR = [W_RAW[:, 0], W_RAW[:, 1], WX_RAW[:, :, :]]
        U = sb("up", [P, 2, T])
        C = sb("conv", [P, 2, T])
        GF = sb("gated", [P, T])
        GH = sb("gated_hi", [P, T], F32R)
        GL = sb("gated_lo", [P, T], F32R)
        RING = 6
        up = ctx.enter_context(nc.psum_tensor("up_ps", [P, 2, 512], F32))
        dn = ctx.enter_context(nc.psum_tensor("down_ps", [P, RING, 512], F32))

        raw_in = [sem(f"f_raw_in{i}") for i in range(3)]
        w_go, w_hi = sem("f_w_go"), sem("f_w_hi")
        w_split = [sem(f"f_w_split{i}") for i in range(3)]
        up_done, up_out, taps = sem("f_up_done"), sem("f_up_out"), sem("f_taps")
        silu_ok, g_ok, gh_ok, gl_ok = sem("f_silu_ok"), sem("f_g_ok"), sem("f_gh_ok"), sem("f_gl_ok")
        dn_done, dn_out = sem("f_dn_done"), sem("f_dn_out")
        ND = KC * NG
        C_UP, C_UO, C_DN = 6, 2, RING

        with nc.Block() as block:
            @block.sync
            def _(sp):
                def load(s, f):
                    sp.wait_ge(w_split[s], f + 1)
                    sp.dma_start(WR[s], (w_up[f], w_up[f + FB], w_down[f])[s]).then_inc(raw_in[s], 16)

                with sp.Fori(0, FB - 1) as f:
                    load(0, f + 1)
                    load(1, f + 1)
                    load(2, f)
                load(2, FB - 1)

            @block.gpsimd
            def _(pool):
                for s, credit in zip(w_split, (2, 2, 1)):
                    pool.sem_inc(s, credit)
                pool.sem_inc(w_hi, 2)
                pool.sem_inc(raw_in[0], 16)
                pool.sem_inc(raw_in[1], 16)

                def split(s, f, n):
                    pool.wait_ge(raw_in[s], f * 16 + 16)
                    if s < 2:
                        pool.wait_ge(up_done, f * 6 + (3 * s - 3 + C_UP))
                    else:
                        pool.wait_ge(dn_done, f * ND + 1)
                    pool.sem_inc(w_go, 1)
                    nc.gpsimd.tensor_copy(WH[:, s], WR[s]).then_inc(w_hi, 1)
                    pool.wait_ge(w_hi, n)
                    nc.gpsimd.tensor_tensor(WL[:, s], WR[s], WH[:, s].bitcast(F32), ALU.subtract).then_inc(w_split[s], 1)

                with pool.Fori(0, FB - 1) as f:
                    split(0, f + 1, f * 3 + 3)
                    split(1, f + 1, f * 3 + 4)
                    split(2, f, f * 3 + 5)
                split(2, FB - 1, 3 * FB)

            @block.tensor
            def _(pe):
                pe.sem_inc(up_done, C_UP)
                pe.sem_inc(dn_done, 1)

                def up_part(f):
                    for s in range(2):
                        pe.wait_ge(w_split[s], f + 2)
                        for g in range(NG):
                            n = NG * s + g
                            pe.wait_ge(up_out, f * 6 + (n - 2 + 1 + C_UO))
                            for k in range(KC):
                                m = three_pass(nc, up[:, n % 2, 0:G], WH[:, s, k], WL[:, s, k],
                                               HH[:, k, g * G:(g + 1) * G], HL[:, k, g * G:(g + 1) * G], k, k == KC - 1)
                            m.then_inc(up_done, 1)

                def down_part(f):
                    pe.wait_ge(w_split[2], f + 2)
                    pe.wait_ge(gl_ok, f + 2)
                    for j in range(KC):
                        for g in range(NG):
                            n = NG * j + g
                            pe.wait_ge(dn_out, f * ND + (n - RING + 1 + C_DN))
                            three_pass(nc, dn[:, n % RING, 0:G], WH[:, 2, j], WL[:, 2, j],
                                       GH[:, g * G:(g + 1) * G], GL[:, g * G:(g + 1) * G], 0, True).then_inc(dn_done, 1)

                up_part(0)
                with pe.Fori(0, FB - 1) as f:
                    up_part(f + 1)
                    down_part(f)
                down_part(FB - 1)

            @block.scalar
            def _(act):
                act.sem_inc(up_out, C_UO)
                with act.Fori(0, FB) as f:
                    for s in range(2):
                        act.wait_ge(g_ok, f + 1)
                        for g in range(NG):
                            n = NG * s + g
                            act.wait_ge(up_done, f * 6 + n + 1 + C_UP)
                            cols = slice(g * G, (g + 1) * G)
                            tap = CW[:, 1, bass.ds(f + s * FB, 1)]
                            bias = CW[:, 3, bass.ds(f + s * FB, 1)]
                            nc.scalar.activation(U[:, s, cols], up[:, n % 2, 0:G], ACT.Copy)
                            nc.scalar.activation(C[:, s, cols], up[:, n % 2, 0:G], ACT.Identity, scale=tap, bias=bias).then_inc(up_out, 1)
                        if s == 0:
                            act.wait_ge(taps, f * 8 + 4)
                            nc.scalar.activation(C[:, 0, :], C[:, 0, :], ACT.Silu).then_inc(silu_ok, 1)
                    act.wait_ge(g_ok, f + 2)
                    act.wait_ge(dn_done, f * ND + 1)
                    nc.scalar.activation(GH[:, :], GF[:, :], ACT.Copy).then_inc(gh_ok, 1)

            @block.vector
            def _(dve):
                dve.sem_inc(g_ok, 1)
                dve.sem_inc(gl_ok, 1)
                dve.sem_inc(dn_out, C_DN)

                def conv(s, f):
                    dve.wait_ge(up_out, f * 6 + (NG * (s + 1) + C_UO))
                    n = 0
                    for tap, src, dst in ((0, 0, 1), (2, 1, 0)):
                        for t0, t1 in RANGES:
                            w = t1 - t0 - 1
                            if n >= 2:
                                dve.wait_ge(taps, f * 8 + 4 * s + n - 1)
                            c = C[:, s, t0 + dst:t0 + dst + w]
                            nc.vector.scalar_tensor_tensor(c, U[:, s, t0 + src:t0 + src + w], CW[:, tap, bass.ds(f + s * FB, 1)],
                                                           c, ALU.mult, ALU.add).then_inc(taps, 1)
                            n += 1

                def gate(f):
                    dve.wait_ge(silu_ok, f + 1)
                    dve.wait_ge(taps, f * 8 + 8)
                    dve.wait_ge(gl_ok, f + 1)
                    nc.vector.tensor_tensor(GF[:, :], C[:, 0, :], C[:, 1, :], ALU.mult).then_inc(g_ok, 1)

                def low(f):
                    dve.wait_ge(gh_ok, f + 1)
                    nc.vector.tensor_tensor(GL[:, :], GF[:, :], GH[:, :].bitcast(F32), ALU.subtract).then_inc(gl_ok, 1)

                def add_down(f):
                    dve.wait_ge(dn_out, f * ND + C_DN)
                    for j in range(KC):
                        for g in range(NG):
                            n = NG * j + g
                            dve.wait_ge(dn_done, f * ND + n + 2)
                            for t0, t1, grp in split_groups(g):
                                x = X1[:, j, t0:t1]
                                m = nc.vector.scalar_tensor_tensor(x, dn[:, n % RING, t0 - g * G:t1 - g * G], MOD[:, 40 + j, grp:grp + 1], x, ALU.mult, ALU.add)
                            m.then_inc(dn_out, 1)

                conv(0, 0)
                conv(1, 0)
                gate(0)
                low(0)
                with dve.Fori(0, FB - 1) as f:
                    conv(0, f + 1)
                    add_down(f)
                    conv(1, f + 1)
                    gate(f + 1)
                    low(f + 1)
                add_down(FB - 1)


def phase5(nc, a, sem, ident, X1, y_prompt, y_sample):
    with ExitStack() as ctx:
        def sb(name, shape, dt=F32):
            return ctx.enter_context(nc.sbuf_tensor(name, shape, dt))

        Y = sb("y", [P, NT, D])
        junk = sb("junk5", [P, 2, D])
        FN = sb("final_gain", [P, D])
        SS, RS = sb("ss5", [P, NT]), sb("rs5", [P, NT])
        EPSB = sb("eps5", [P, 1])
        ps = ctx.enter_context(nc.psum_tensor("y_ps", [P, 4, 1024], F32))
        fn_in, yt, sq, yc, ln, rs, st = (sem("y_gain_in"), sem("y_t"), sem("y_sq"), sem("y_copy"), sem("y_ln"),
                                                   sem("y_rs"), sem("y_store"))
        set_ok = sem("y_set_ok")
        with nc.Block() as block:
            @block.sync
            def _(sp):
                sp.dma_start(FN[:, :], a["final_norm"].partition_broadcast(P)).then_inc(fn_in, 16)
                for t in range(NT):
                    sp.wait_ge(yc, t + 1)
                    sp.dma_start(y_prompt[0] if t == 0 else y_sample[0, (t - 1) * P:t * P, :], Y[:, t, :]).then_inc(st, 16)
                sp.wait_ge(st, 16 * NT)

            @block.tensor
            def _(pe):
                for t in range(NT):
                    if t >= 4:
                        pe.wait_ge(yc, t - 3)
                    for j in range(KC):
                        m = nc.tensor.transpose(ps[:, t % 4, j * P:(j + 1) * P], X1[:, j, t * P:(t + 1) * P], ident[:, :])
                    m.then_inc(yt, 1)

            @block.scalar
            def _(act):
                nc.scalar.preload_act_table_set(LN_EXP)
                act.wait_ge(set_ok, 1)
                for t in range(NT):
                    act.wait_ge(yt, t + 1)
                    if t >= 2:
                        act.wait_ge(sq, t - 1)
                    nc.scalar.activation(junk[:, t % 2, :], ps[:, t % 4, :], ACT.Square, accum_out=SS[:, t:t + 1]).then_inc(sq, 1)
                    act.wait_ge(sq, t + 1)
                    nc.scalar.activation(RS[:, t:t + 1], SS[:, t:t + 1], ACT.Ln, scale=1.0 / D, bias=EPSB[:, 0:1]).then_inc(ln, 1)
                    act.wait_ge(ln, t + 1)
                    nc.scalar.activation(RS[:, t:t + 1], RS[:, t:t + 1], ACT.Exp, scale=-0.5).then_inc(rs, 1)

            @block.vector
            def _(dve):
                nc.vector.memset(EPSB[:, :], EPS).then_inc(set_ok, 1)
                dve.wait_ge(fn_in, 16)
                for t in range(NT):
                    dve.wait_ge(rs, t + 1)
                    nc.vector.scalar_tensor_tensor(Y[:, t, :], ps[:, t % 4, :], RS[:, t:t + 1], FN[:, :], ALU.mult, ALU.mult).then_inc(yc, 1)



_INS = ["x_prompt", "x_sample", "c", "cache_k", "cache_v", "state_hgrn", "c_ctx", "ada_w", "ada_b", "norm1", "norm2",
        "w_in", "q_norm", "k_norm", "hgrn_lb_logits", "hgrn_norm", "w_o", "w_up", "conv_w", "conv_b", "w_down", "final_norm"]
_OUTS = [(1, T_CTX, D), (1, T_LAT, D), (1, 1, T_CTX, NKV, HEAD), (1, 1, T_CTX, NKV, HEAD), (1, 1, 2, RH, P, P)]


def shape_constants():
    import numpy as np
    s, t = np.arange(P)[:, None], np.arange(P)[None, :]
    same = s // CH == t // CH
    mask = np.concatenate([same & (s <= t), same & (s >= t)], axis=1).astype(np.float32)
    half, grid_w = HEAD // 2, 64
    inv = (1.0 / (10000.0 ** (np.arange(0, half, 2, dtype=np.float32) / np.float32(half)))).astype(np.float32)
    n = np.arange(T_LAT)
    row, col = (n // grid_w).astype(np.float32)[:, None] * inv, (n % grid_w).astype(np.float32)[:, None] * inv
    cos = np.concatenate([np.cos(row), np.cos(row), np.cos(col), np.cos(col)], axis=1).astype(np.float32)
    sin = np.concatenate([-np.sin(row), np.sin(row), -np.sin(col), np.sin(col)], axis=1).astype(np.float32)
    return {"c_ident": np.eye(P, dtype=np.float32), "c_mask": mask, "c_cos": cos, "c_sin": sin}


def kernel(**inputs):
    import numpy as np
    import concourse.bacc as bacc
    from concourse.bass_utils import run_bass_kernel_spmd

    nc = bacc.Bacc("TRN2", target_bir_lowering=False, num_devices=1)
    arrays, aps = {}, {}
    given = {n: np.ascontiguousarray(inputs[n]) for n in _INS}
    given.update(shape_constants())
    for n, v in given.items():
        arrays["in_" + n] = v
        aps[n] = nc.dram_tensor("in_" + n, v.shape, F32, kind="ExternalInput").ap()
    outs = [nc.dram_tensor(f"out_{i}", s, F32, kind="ExternalOutput").ap() for i, s in enumerate(_OUTS)]
    build(nc, aps, outs, PHASES)
    r = run_bass_kernel_spmd(nc, [arrays], core_ids=[0])
    return tuple(r.results[0][f"out_{i}"] for i in range(len(_OUTS)))
```

```python
from contextlib import ExitStack

import concourse.bass as bass
from concourse import mybir

F32 = mybir.dt.float32
F32R = mybir.dt.float32r
BF16 = mybir.dt.bfloat16
ALU = mybir.AluOpType
ACT = mybir.ActivationFunctionType
LN_EXP = "natural_log_exp_and_others"
AX_X = mybir.AxisListType.X

P = 128
D = 1024
KC = D // P
T_CTX, T_LAT = 128, 1024
T = T_CTX + T_LAT
NT = T // P
G = 384
NG = T // G
HEAD = 64
NKV, GQ = 4, 4
PAST = 256
NKC = NT + PAST // P
CH = 64
NCH = T // CH
RH = 8
D_FF = 2816
FB = D_FF // P
EPS = 1e-6
B_Q, B_K, B_V, B_RQ, B_RFF, B_RFB, B_RI, B_RG, B_ZA, B_ZR = 0, 8, 10, 12, 20, 28, 36, 44, 52, 60
CHAIN2 = 31
RANGES = ((0, T_CTX), (T_CTX, T))


class Chain:

    def __init__(self, eng, sem, base):
        self.eng, self.sem, self.base, self.n = eng, sem, base, 0

    def step(self, ins):
        self.n += 1
        ins.then_inc(self.sem, 1)
        return ins

    def wait(self):
        self.eng.wait_ge(self.sem, self.base + self.n)

    def link(self, ins):
        self.step(ins)
        self.wait()


def split_groups(g):
    lo, hi = g * G, (g + 1) * G
    return [(max(lo, a), min(hi, b), n) for n, (a, b) in enumerate(RANGES) if max(lo, a) < min(hi, b)]


def build(nc, a, outs):
    y_prompt, y_sample, out_k, out_v, out_state = outs
    rec_dram = nc.dram_tensor("rec_scratch", (RH, P, T), F32, kind="Internal").ap()
    mix_dram = nc.dram_tensor("mix_scratch", (KC, P, T), F32, kind="Internal").ap()
    w_in = a["w_in"][0].rearrange("(k p) (b c) -> b p k c", p=P, c=P)
    w_in64 = a["w_in"][0].rearrange("(k p) (b c) -> b p k c", p=P, c=HEAD)
    w_o = a["w_o"][0].rearrange("(k p) (b c) -> b p k c", p=P, c=P)
    w_up = a["w_up"][0].rearrange("(k p) (b c) -> b p k c", p=P, c=P)
    w_down = a["w_down"][0].rearrange("(f p) (j c) -> f p j c", p=P, c=P)

    with ExitStack() as ctx:
        def sb(name, shape, dt=F32, c=ctx):
            return c.enter_context(nc.sbuf_tensor(name, shape, dt))

        def pb(name, shape, dt=F32, c=ctx):
            return c.enter_context(nc.psum_tensor(name, shape, dt))

        def sem(name, c=ctx):
            return c.enter_context(nc.semaphore(name))

        HH = sb("act_hi", [P, KC, T], F32R)
        HL = sb("act_lo", [P, KC, T], F32R)
        ident = sb("ident", [P, P])
        ones = sb("ones", [P, P])
        VT = sb("vec_t", [P, 112])
        CW = sb("conv_t", [P, 4, 2 * FB])
        MOD = sb("mod", [P, 48, 2])
        A1 = sb("a1", [P, KC, 2])
        A2 = sb("a2", [P, KC, 2])
        lb = sb("lb", [P, 2 * RH])
        lb1 = sb("lb1", [P, 2 * RH])
        lb1n = sb("lb1n", [P, 2 * RH])
        rgain = sb("rgain", [P, 1])

        phase0(nc, a, sb, pb, sem, HH, HL, ident, ones, VT, CW, MOD, A1, A2, lb, lb1, lb1n, rgain)
        W = (sb("w_raw", [P, 2, KC, P]), sb("w_hi", [P, 3, KC, P], F32R), sb("w_lo", [P, 3, KC, P], F32R))
        phase1(nc, a, sem, W, w_in64, HH, HL, ident, ones, lb, lb1, lb1n, rgain, w_in, rec_dram, out_state)
        phase2(nc, a, sem, W, w_o, HH, HL, ident, w_in, w_in64, rec_dram, mix_dram, out_k, out_v)
        X1 = sb("resid_t", [P, KC, T])
        phase3(nc, a, sem, W, w_up, HH, HL, ident, ones, MOD, A2, X1, w_o, mix_dram)
        phase4(nc, a, sem, W, HH, HL, MOD, CW, X1, w_up, w_down)
        phase5(nc, a, sem, ident, X1, y_prompt, y_sample)


def phase0(nc, a, sb_, pb_, sem, HH, HL, ident, ones, VT, CW, MOD, A1, A2, lb, lb1, lb1n, rgain):
    with ExitStack() as ctx:
        def sb(name, shape, dt=F32):
            return ctx.enter_context(nc.sbuf_tensor(name, shape, dt))

        V1 = sb("v1", [112, P])
        V2 = sb("v2", [88, P])
        V3 = sb("v3", [88, P])
        X = sb("x0", [P, NT, D])
        AW = sb("ada_w", [P, 3, KC, 512])
        MR = sb("mod_rows", [2, 6 * D])
        HF = sb("h_f32", [P, 2, 512])
        junk = sb("junk0", [P, D])
        CS = sb("cond_silu", [P, 2, KC])
        SG = sb("cond_sig", [P, 2 * KC])
        LD = sb("lb_diff", [P, 2 * RH])
        SS = sb("ss0", [P, NT])
        RS = sb("rs0", [P, NT])
        vps = ctx.enter_context(nc.psum_tensor("vps", [P, 512], F32))
        aps = ctx.enter_context(nc.psum_tensor("ada_ps", [P, 2, 512], F32))
        mps = ctx.enter_context(nc.psum_tensor("mod_ps", [P, 512], F32))
        xps = ctx.enter_context(nc.psum_tensor("x_ps", [P, 4, 512], F32))

        const_in, vec_in, x_in0, x_in1 = sem("const_in"), sem("vec_in"), sem("x_in0"), sem("x_in1")
        ada_in = [sem(f"ada_in{i}") for i in range(3)]
        vec_t, vec_ok, cond_sig, cond_ok = sem("vec_t"), sem("vec_ok"), sem("cond_sig"), sem("cond_ok")
        ada_done, ada_out, mod_t, mod_ok = sem("ada_done"), sem("ada_out"), sem("mod_t"), sem("mod_ok")
        sq_done, sqrt_done, rs_done, xn_done = sem("sq_done"), sem("sqrt_done"), sem("rs_done"), sem("xn_done")
        xt_done, hf_done, hi_done, lo_done = sem("xt_done"), sem("hf_done"), sem("hi_done"), sem("lo_done")
        v_ch = sem("v0_chain")
        GR = [(0, 1, 0), (1, 5, 1), (5, 9, 1)]

        with nc.Block() as block:
            @block.sync
            def _(sp):
                sp.dma_start(ident[:, :], a["c_ident"]).then_inc(const_in, 16)
                row = lambda x: x.rearrange("(r c) -> r c", c=P)
                vecs = [(V1[0:48, :], row(a["ada_b"][0])), (V1[48:56, :], row(a["norm1"][0])),
                        (V1[56:64, :], row(a["norm2"][0])), (V1[64:72, :], row(a["c_ctx"])),
                        (V1[72:80, :], row(a["c"][0])),
                        (V1[80:112, :], a["hgrn_lb_logits"].rearrange("a b (r c) -> (a b r) c", c=P)),
                        (V2[0:44, :], row(a["conv_w"][0, 0])), (V2[44:88, :], row(a["conv_w"][0, 1])),
                        (V3[0:44, :], row(a["conv_w"][0, 2])), (V3[44:88, :], row(a["conv_b"][0])),
                        (rgain[:, :], a["hgrn_norm"][0].rearrange("(p o) -> p o", o=1))]
                for dst, src in vecs:
                    sp.dma_start(dst, src).then_inc(vec_in, 16)
                sp.dma_start(X[:, 0, :], a["x_prompt"][0]).then_inc(x_in0, 16)
                sp.dma_start(X[:, 1:NT, :], a["x_sample"][0].rearrange("(t p) d -> p t d", p=P)).then_inc(x_in1, 16)

            @block.scalar
            def _(act):
                for c in range(3):
                    act.dma_start(AW[:, c], a["ada_w"][0].rearrange("(k p) (b c) -> b p k c", p=P, c=512)[c]).then_inc(ada_in[c], 16)
                act.wait_ge(vec_ok, 1)
                nc.scalar.activation(SG[:, :], VT[:, 64:80], ACT.Sigmoid).then_inc(cond_sig, 1)
                act.wait_ge(vec_ok, 2)
                nc.scalar.activation(lb[:, :], LD[:, :], ACT.Sigmoid).then_inc(cond_sig, 1)
                act.wait_ge(x_in0, 16)
                act.wait_ge(x_in1, 16)
                for t in range(NT):
                    if t:
                        act.wait_ge(sq_done, t)
                    nc.scalar.activation(junk[:, :], X[:, t, :], ACT.Square, accum_out=SS[:, t:t + 1]).then_inc(sq_done, 1)
                act.wait_ge(v_ch, 1)
                nc.scalar.activation(RS[:, :], SS[:, :], ACT.Sqrt).then_inc(sqrt_done, 1)
                for c in range(12):
                    act.wait_ge(ada_done, c + 1)
                    nc.scalar.activation(MR[:, c * 512:(c + 1) * 512], aps[0:2, c % 2, :], ACT.Copy).then_inc(ada_out, 1)
                    if c + 3 < 12:
                        act.dma_start(AW[:, c % 3], a["ada_w"][0].rearrange("(k p) (b c) -> b p k c", p=P, c=512)[c + 3]).then_inc(ada_in[c % 3], 16)
                for n in range(3 * KC):
                    j, (t0, t1, _) = n // 3, GR[n % 3]
                    act.wait_ge(hf_done, n + 1)
                    nc.scalar.activation(HH[:, j, t0 * P:t1 * P], HF[:, n % 2, 0:(t1 - t0) * P], ACT.Copy).then_inc(hi_done, 1)

            @block.tensor
            def _(pe):
                pe.wait_ge(const_in, 16)
                pe.wait_ge(vec_in, 16 * 11)
                nc.tensor.transpose(vps[:, 0:112], V1[:, :], ident[0:112, 0:112])
                nc.tensor.transpose(vps[:, 112:200], V2[:, :], ident[0:88, 0:88])
                nc.tensor.transpose(vps[:, 200:288], V3[:, :], ident[0:88, 0:88]).then_inc(vec_t, 1)
                pe.wait_ge(cond_ok, 1)
                for c in range(12):
                    pe.wait_ge(ada_in[c % 3], 16 * (c // 3 + 1))
                    if c >= 2:
                        pe.wait_ge(ada_out, c - 1)
                    for k in range(KC):
                        m = nc.tensor.matmul(aps[0:2, c % 2, :], CS[:, :, k], AW[:, c % 3, k, :], start=(k == 0), stop=(k == KC - 1))
                    m.then_inc(ada_done, 1)
                pe.wait_ge(ada_out, 12)
                for b in range(48):
                    m = nc.tensor.transpose(mps[:, 2 * b:2 * b + 2], MR[:, b * P:(b + 1) * P], ident[0:2, 0:2])
                m.then_inc(mod_t, 1)
                pe.wait_ge(xn_done, NT)
                for n in range(3 * KC):
                    j, (t0, t1, _) = n // 3, GR[n % 3]
                    if n >= 4:
                        pe.wait_ge(hf_done, n - 3)
                    for i, t in enumerate(range(t0, t1)):
                        m = nc.tensor.transpose(xps[:, n % 4, i * P:(i + 1) * P], X[:, t, j * P:(j + 1) * P], ident[:, :])
                    m.then_inc(xt_done, 1)

            @block.vector
            def _(dve):
                nc.vector.memset(ones[:, :], 1.0)
                dve.wait_ge(vec_t, 1)
                nc.vector.tensor_copy(VT[:, :], vps[:, 0:112]).then_inc(vec_ok, 1)
                nc.vector.tensor_copy(CW[:, :, :], vps[:, 112:288].rearrange("p (a b) -> p a b", a=4)).then_inc(lo_done, 1)
                dve.wait_ge(vec_ok, 1)
                lgt = VT[:, 80:112].rearrange("p (d l h) -> p d l h", d=2, l=2)
                nc.vector.tensor_tensor(LD[:, :].rearrange("p (d h) -> p d h", d=2), lgt[:, :, 0, :], lgt[:, :, 1, :], ALU.subtract).then_inc(vec_ok, 1)
                dve.wait_ge(cond_sig, 1)
                nc.vector.tensor_tensor(CS[:, :, :].rearrange("p a k -> p (a k)"), VT[:, 64:80], SG[:, :], ALU.mult).then_inc(cond_ok, 1)
                dve.wait_ge(cond_sig, 2)
                nc.vector.tensor_scalar(lb1[:, :], lb[:, :], -1.0, 1.0, ALU.mult, ALU.add)
                nc.vector.tensor_scalar(lb1n[:, :], lb[:, :], 1.0, -1.0, ALU.mult, ALU.add)
                dve.wait_ge(sq_done, NT)
                nc.vector.tensor_scalar(SS[:, :], SS[:, :], 1.0 / D, EPS, ALU.mult, ALU.add).then_inc(v_ch, 1)
                dve.wait_ge(sqrt_done, 1)
                nc.vector.reciprocal(RS[:, :], RS[:, :]).then_inc(rs_done, 1)
                dve.wait_ge(rs_done, 1)
                for t in range(NT):
                    nc.vector.tensor_scalar(X[:, t, :], X[:, t, :], RS[:, t:t + 1], None, ALU.mult).then_inc(xn_done, 1)
                dve.wait_ge(mod_t, 1)
                nc.vector.tensor_tensor(MOD[:, :, :], mps[:, 0:96].rearrange("p (b g) -> p b g", g=2),
                                        VT[:, 0:48].unsqueeze(2).broadcast_to((P, 48, 2)), ALU.add).then_inc(mod_ok, 1)
                dve.wait_ge(mod_ok, 1)
                nc.vector.scalar_tensor_tensor(A1[:, :, :], MOD[:, 8:16, :], 1.0, VT[:, 48:56].unsqueeze(2).broadcast_to((P, 8, 2)), ALU.add, ALU.mult).then_inc(mod_ok, 1)
                nc.vector.scalar_tensor_tensor(A2[:, :, :], MOD[:, 32:40, :], 1.0, VT[:, 56:64].unsqueeze(2).broadcast_to((P, 8, 2)), ALU.add, ALU.mult).then_inc(mod_ok, 1)
                dve.wait_ge(mod_ok, 3)

                def low_part(n):
                    j, (t0, t1, _) = n // 3, GR[n % 3]
                    dve.wait_ge(hi_done, n + 1)
                    nc.vector.tensor_tensor(HL[:, j, t0 * P:t1 * P], HF[:, n % 2, 0:(t1 - t0) * P],
                                            HH[:, j, t0 * P:t1 * P].bitcast(F32), ALU.subtract).then_inc(lo_done, 1)

                for n in range(3 * KC):
                    j, (t0, t1, grp) = n // 3, GR[n % 3]
                    dve.wait_ge(xt_done, n + 1)
                    if n >= 2:
                        dve.wait_ge(lo_done, n)
                    nc.vector.tensor_scalar(HF[:, n % 2, 0:(t1 - t0) * P], xps[:, n % 4, 0:(t1 - t0) * P],
                                            A1[:, j, grp:grp + 1], MOD[:, j, grp:grp + 1], ALU.mult, ALU.add).then_inc(hf_done, 1)
                    if n:
                        low_part(n - 1)
                low_part(3 * KC - 1)


def three_pass(nc, out, w_hi, w_lo, x_hi, x_lo, k, last):
    nc.tensor.matmul(out, w_hi, x_hi, start=(k == 0), stop=False)
    nc.tensor.matmul(out, w_hi, x_lo, start=False, stop=False)
    return nc.tensor.matmul(out, w_lo, x_hi, start=False, stop=last)


def load_qkv(sp, WR, w_in, w_in64, kv, u, done):
    if u < 2:
        sp.dma_start(WR[:, u], w_in[kv * 2 + (B_Q + u)]).then_inc(done, 16)
    else:
        sp.dma_start(WR[:, 0, :, 0:HEAD], w_in64[kv + 2 * B_K]).then_inc(done, 16)
        sp.dma_start(WR[:, 0, :, HEAD:P], w_in64[kv + 2 * B_V]).then_inc(done, 16)


def phase1(nc, a, sem, W, w_in64, HH, HL, ident, ones, lb, lb1, lb1n, rgain, w_in, rec_dram, out_state):
    with ExitStack() as ctx:
        def sb(name, shape, dt=F32):
            return ctx.enter_context(nc.sbuf_tensor(name, shape, dt))

        def pb(name, shape):
            return ctx.enter_context(nc.psum_tensor(name, shape, F32))

        WR, WH, WL = W
        S = sb("states", [P, 2, NCH + 1, P])
        TK = sb("keys_values_t", [P, NT, 3, P])
        QD = sb("q_dec", [P, 2, T])
        KD = sb("k_dec", [P, 2, T])
        SIG = sb("sig_f", [P, 2, T])
        RQ, RIT, RG, ZR = sb("rq", [P, T]), sb("ri_t", [P, T]), sb("rg", [P, T]), sb("zr", [P, T])
        GB = sb("log_f", [P, 2, T])
        BB = sb("cum_log_f", [P, T])
        AM = sb("masked_scores", [P, 2, 2 * P])
        M2 = sb("causal2", [P, 2 * P])
        EL = sb("chunk_decay", [P, 2, NCH])
        MK = sb("chunk_start", [P, T], BF16)
        LBr, LB1r = sb("lb_act", [P, 2]), sb("lb1_act", [P, 2])
        LBk, LBn = sb("lb1_dve", [P, 2]), sb("lb1n_dve", [P, 2])
        EPSB = sb("eps_r", [P, 1])
        RS = GB[:, 0]
        OT = RIT

        proj = pb("proj_ps", [P, 2, 512])
        tps = pb("t_o_ps", [P, 2, 512])
        kvps = pb("kv_ps", [P, 2, 512])
        aps = pb("scores_ps", [P, 2, 512])

        raw_in = [sem("r_raw_in0"), sem("r_raw_in1")]
        w_go, w_hi, w_split = sem("r_w_go"), sem("r_w_hi"), sem("r_w_split")
        proj_done, proj_out = sem("r_proj_done"), sem("r_proj_out")
        log_f, cum_f, exp_f = sem("r_log_f"), sem("r_cum_f"), sem("r_exp_f")
        dir_ready, dve_ch = sem("r_dir_ready"), sem("r_dve_chain")
        t_done, t_out, t_out_v, kv_done = sem("r_t_done"), sem("r_t_out"), sem("r_t_out_dve"), sem("r_kv_done")
        st = [sem("r_state_f"), sem("r_state_b")]
        a_done, a_out, o_done, o_out = sem("r_a_done"), sem("r_a_out"), sem("r_o_done"), sem("r_o_out")
        ss_done, ss_out, ss_inv = sem("r_ss_done"), sem("r_ss_out"), sem("r_ss_inv")
        rec_t, rec_ready = sem("r_rec_t"), sem("r_rec_ready")
        s0_in, rec_store, st_store = sem("r_s0_in"), sem("r_rec_store"), sem("r_state_store")
        m_in, mk_ok, zero_ok, lb_ok = sem("r_mask_in"), sem("r_mk_ok"), sem("r_zero_ok"), sem("r_lb_ok")

        UNITS = (B_RQ, B_RG, B_RFF, B_RFB, B_RI, B_ZR)
        NU = len(UNITS)
        PG = NU * NG
        C_SPLIT, C_PROJ, C_OUT = 2, 9, 2
        FWD = [(c, 18 if c == 1 else c + 1) for c in range(NCH)]
        BWD = [(c, 18 if c == 0 else c - 1) for c in reversed(range(NCH))]

        def t_bank(j):
            return (tps, kvps)[j // 2 % 2][:, j % 2]

        def links(d, j):
            return 2 * (j + 1) - (d == 0 and j == NT - 1) - (d == 1 and j >= NT - 2)

        with nc.Block() as block:
            @block.sync
            def _(sp):
                sp.dma_start(M2[:, :], a["c_mask"]).then_inc(m_in, 16)
                def load(r, u):
                    sp.wait_ge(w_split, r * NU + (u - 2 + 1 + C_SPLIT))
                    sp.dma_start(WR[:, u % 2], w_in[r + UNITS[u]]).then_inc(raw_in[u % 2], 16)

                def rest_and_states(r):
                    for u in range(3, NU):
                        load(r, u)
                    sp.wait_ge(o_done, r * NT + 1)
                    sp.dma_start(S[:, 0, 2, :], a["state_hgrn"][0, 0, 0][r]).then_inc(s0_in, 16)
                    sp.dma_start(S[:, 1, NCH - 1, :], a["state_hgrn"][0, 0, 1][r]).then_inc(s0_in, 16)

                def store(r):
                    for d in range(2):
                        sp.wait_ge(st[d], r * 17 + 17)
                        sp.dma_start(out_state[0, 0, d][r], S[:, d, NCH, :]).then_inc(st_store, 16)
                    sp.wait_ge(rec_ready, r * NG + NG + 1)
                    sp.dma_start(rec_dram[r], OT[:, :]).then_inc(rec_store, 16)

                for u in range(3):
                    load(0, u)
                with sp.Fori(0, RH - 1) as r:
                    rest_and_states(r)
                    for u in range(3):
                        load(r + 1, u)
                    store(r)
                rest_and_states(RH - 1)
                for u in range(3):
                    sp.wait_ge(w_split, RH * NU + (u - 2 + 1 + C_SPLIT))
                    load_qkv(sp, WR, w_in, w_in64, 0, u, raw_in[u % 2])
                store(RH - 1)
                sp.wait_ge(rec_store, 16 * RH + 1)
                sp.wait_ge(st_store, 32 * RH + 1)

            @block.gpsimd
            def _(pool):
                pool.sem_inc(w_split, C_SPLIT)
                def split(u, n0, raw, used):
                    pool.wait_ge(raw_in[u % 2], raw)
                    pool.wait_ge(proj_done, used)
                    pool.sem_inc(w_go, 1)
                    nc.gpsimd.tensor_copy(WH[:, u % 3], WR[:, u % 2]).then_inc(w_hi, 1)
                    pool.wait_ge(w_hi, n0 + (u + 1))
                    nc.gpsimd.tensor_tensor(WL[:, u % 3], WR[:, u % 2], WH[:, u % 3].bitcast(F32), ALU.subtract).then_inc(w_split, 1)

                with pool.Fori(0, RH) as r:
                    for u in range(NU):
                        split(u, r * NU, r * 48 + 16 * (u // 2 + 1), r * PG + (NG * (u - 3) + NG + C_PROJ))
                for u in range(3):
                    split(u, RH * NU, RH * 48 + (16, 16, 48)[u], RH * PG + NG * (u - 3) + NG + C_PROJ)

            @block.tensor
            def _(pe):
                pe.sem_inc(proj_done, C_PROJ)
                pe.sem_inc(t_done, 1)
                pe.sem_inc(o_done, 1)
                pe.wait_ge(m_in, 16)
                pe.wait_ge(zero_ok, 3)
                with pe.Fori(0, RH) as r:
                    for u in range(NU):
                        pe.wait_ge(w_split, r * NU + (u + 1 + C_SPLIT))
                        for g in range(NG):
                            n = NG * u + g
                            pe.wait_ge(proj_out, r * PG + (n - 2 + 1 + C_OUT))
                            for k in range(KC):
                                m = three_pass(nc, proj[:, n % 2, 0:G], WH[:, u % 3, k], WL[:, u % 3, k],
                                               HH[:, k, g * G:(g + 1) * G], HL[:, k, g * G:(g + 1) * G], k, k == KC - 1)
                            m.then_inc(proj_done, 1)
                    pe.wait_ge(dir_ready, r * 2 + 3)
                    pe.wait_ge(proj_out, r * PG + (15 + C_OUT))
                    for j in range(NT):
                        if j >= 4:
                            if j % 2:
                                pe.wait_ge(t_out_v, r * 4 + j // 2 - 1)
                            else:
                                pe.wait_ge(t_out, r * 5 + j // 2 - 1)
                        cols = slice(j * P, (j + 1) * P)
                        nc.tensor.transpose(t_bank(j)[:, 0:P], SIG[:, 0, cols], ident[:, :])
                        nc.tensor.transpose(t_bank(j)[:, P:2 * P], SIG[:, 1, cols], ident[:, :])
                        nc.tensor.transpose(t_bank(j)[:, 2 * P:3 * P], RIT[:, cols], ident[:, :]).then_inc(t_done, 1)
                    pe.wait_ge(t_out, r * 5 + 5)
                    pe.wait_ge(t_out_v, r * 4 + 4)
                    for j in range(NT):
                        if j >= 2:
                            for d in range(2):
                                pe.wait_ge(st[d], r * 17 + links(d, j - 2))
                        for q in range(4):
                            c = FWD[2 * j + q][0] if q < 2 else BWD[2 * j + q - 2][0]
                            rows = slice((c % 2) * CH, (c % 2 + 1) * CH)
                            bank = (kvps, aps)[c % 2]
                            m = nc.tensor.matmul(bank[:, j % 2, q // 2 * P:(q // 2 + 1) * P], TK[rows, c // 2, q // 2, :], TK[rows, c // 2, 2, :],
                                                 start=True, stop=True)
                        m.then_inc(kv_done, 1)

                    def scores(j):
                        if j >= 2:
                            pe.wait_ge(a_out, r * NT + j - 1)
                        cols = slice(j * P, (j + 1) * P)
                        for d in range(2):
                            m = nc.tensor.matmul(aps[:, (j + 1) % 2, d * P:(d + 1) * P], KD[:, d, cols], QD[:, d, cols], start=True, stop=True)
                        m.then_inc(a_done, 1)

                    for d in range(2):
                        pe.wait_ge(st[d], r * 17 + links(d, NT - 2))
                    scores(0)
                    for s in st:
                        pe.wait_ge(s, r * 17 + 17)
                    pe.wait_ge(s0_in, r * 32 + 32)
                    for j in range(NT):
                        if j + 1 < NT:
                            scores(j + 1)
                        pe.wait_ge(a_out, r * NT + j + 1)
                        if j >= 2:
                            pe.wait_ge(o_out, r * 2 * NT + 2 * (j - 1))
                        o = tps[:, j % 2, 0:P]
                        for d in range(2):
                            nc.tensor.matmul(o, TK[:, j, 2, :], AM[:, j % 2, d * P:(d + 1) * P], start=(d == 0), stop=False)
                        for d in range(2):
                            for h in range(2):
                                c = 2 * j + h
                                m = nc.tensor.matmul(o[:, h * CH:(h + 1) * CH], S[:, d, c, :], QD[:, d, c * CH:(c + 1) * CH],
                                                     start=False, stop=(d == 1 and h == 1))
                        m.then_inc(o_done, 1)
                    for g in range(NG):
                        pe.wait_ge(o_out, r * 2 * NT + 6 * (g + 1))
                        if g == 2:
                            pe.wait_ge(ss_out, r * NG + 1)
                        nc.tensor.matmul(kvps[:, g % 2, 0:G], ones[:, :], BB[:, g * G:(g + 1) * G], start=True, stop=True).then_inc(ss_done, 1)

            @block.scalar
            def _(act):
                act.sem_inc(proj_out, C_OUT)
                act.wait_ge(zero_ok, 3)
                with act.Fori(0, RH) as r:
                    def evacuate(u, dst, func, groups=range(NG)):
                        for g in groups:
                            n = NG * u + g
                            act.wait_ge(proj_done, r * PG + (n + 1 + C_PROJ))
                            nc.scalar.activation(dst[:, g * G:(g + 1) * G], proj[:, n % 2, 0:G], func).then_inc(proj_out, 1)

                    def gate_logs(d):
                        act.wait_ge(proj_out, r * PG + (9 + 3 * d + C_OUT))
                        nc.scalar.activation(GB[:, d], SIG[:, d, :], ACT.Ln, bias=LBr[:, d:d + 1], scale=LB1r[:, d:d + 1]).then_inc(log_f, 1)

                    def gate_exps(d):
                        act.wait_ge(cum_f, r * 2 + d + 1)
                        nc.scalar.activation(GB[:, d], BB[:, :], ACT.Exp)
                        nc.scalar.activation(BB[:, :], BB[:, :], ACT.Exp, scale=-1.0).then_inc(exp_f, 1)

                    lbv = lb[:, :].rearrange("p (d h) -> p h d", d=2)
                    lb1v = lb1[:, :].rearrange("p (d h) -> p h d", d=2)
                    act.wait_ge(dir_ready, r * 2 + 1)
                    nc.scalar.activation(LBr[:, :], lbv[:, bass.ds(r, 1), :].rearrange("p a d -> p (a d)"), ACT.Copy)
                    nc.scalar.activation(LB1r[:, :], lb1v[:, bass.ds(r, 1), :].rearrange("p a d -> p (a d)"), ACT.Copy).then_inc(lb_ok, 1)
                    act.wait_ge(lb_ok, r + 1)
                    evacuate(0, RQ, ACT.Silu)
                    act.wait_ge(rec_ready, r * NG + 1)
                    evacuate(1, RG, ACT.Silu)
                    act.wait_ge(t_done, r * NT + 1)
                    evacuate(2, SIG[:, 0], ACT.Sigmoid)
                    evacuate(3, SIG[:, 1], ACT.Sigmoid)
                    act.wait_ge(ss_done, r * NG + 1)
                    for d in range(2):
                        gate_logs(d)
                    act.wait_ge(rec_store, r * 16 + 1)
                    evacuate(4, RIT, ACT.Copy, (0,))
                    gate_exps(0)
                    evacuate(4, RIT, ACT.Copy, (1,))
                    gate_exps(1)
                    evacuate(4, RIT, ACT.Copy, (2,))
                    evacuate(5, ZR, ACT.Sigmoid)
                    act.wait_ge(o_done, r * NT + 1)
                    for j in range(0, NT, 2):
                        act.wait_ge(t_done, r * NT + j + 2)
                        nc.scalar.activation(TK[:, j].rearrange("p a b -> p (a b)"), t_bank(j)[:, 0:3 * P], ACT.Copy).then_inc(t_out, 1)
                    for j in range(NT):
                        act.wait_ge(o_done, r * NT + j + 2)
                        nc.scalar.activation(OT[:, j * P:(j + 1) * P], tps[:, j % 2, 0:P], ACT.Copy).then_inc(o_out, 1)
                        nc.scalar.activation(BB[:, j * P:(j + 1) * P], tps[:, j % 2, 0:P], ACT.Square).then_inc(o_out, 1)
                    for g in range(NG):
                        act.wait_ge(ss_done, r * NG + g + 2)
                        cols = slice(g * G, (g + 1) * G)
                        nc.scalar.activation(RS[:, cols], kvps[:, g % 2, 0:G], ACT.Sqrt, scale=1.0 / P, bias=EPSB[:, 0:1]).then_inc(ss_out, 1)

            @block.vector
            def _(dve):
                dve.sem_inc(dir_ready, 1)
                dve.sem_inc(rec_ready, 1)
                dve.sem_inc(rec_store, 1)
                dve.sem_inc(st_store, 1)
                dve.sem_inc(ss_done, 1)
                nc.vector.memset(EPSB[:, :], EPS).then_inc(zero_ok, 1)
                nc.vector.memset(S[:, 0, 0, :], 0.0).then_inc(zero_ok, 1)
                nc.vector.memset(S[:, 1, 1, :], 0.0).then_inc(zero_ok, 1)
                nc.vector.memset(MK[:, :], 1.0).then_inc(mk_ok, 1)
                dve.wait_ge(mk_ok, 1)
                nc.vector.memset(MK[:, 0:T:CH], 0.0).then_inc(mk_ok, 1)
                dve.wait_ge(mk_ok, 2)
                dve.wait_ge(m_in, 16)
                with dve.Fori(0, RH) as r:
                    ch = Chain(dve, dve_ch, r * 8)
                    nc.vector.tensor_copy(LBk[:, :], lb1[:, :].rearrange("p (d h) -> p h d", d=2)[:, bass.ds(r, 1), :].rearrange("p a d -> p (a d)"))
                    ch.step(nc.vector.tensor_copy(LBn[:, :], lb1n[:, :].rearrange("p (d h) -> p h d", d=2)[:, bass.ds(r, 1), :].rearrange("p a d -> p (a d)")))
                    for d in range(2):
                        dve.wait_ge(dir_ready, r * 2 + d + 1)
                        dve.wait_ge(log_f, r * 2 + d + 1)
                        rev = slice(None, None, -1) if d else slice(None)
                        nc.vector.tensor_tensor_scan(BB[:, rev], MK[:, :], GB[:, d, rev], 0.0, ALU.mult, ALU.add).then_inc(cum_f, 1)
                        ch.wait()
                        ch.step(nc.vector.tensor_scalar(SIG[:, d, :], SIG[:, d, :], LBn[:, d:d + 1], LBk[:, d:d + 1], ALU.mult, ALU.add))
                        dve.wait_ge(exp_f, r * 2 + d + 1)
                        last = GB[:, d, CH - 1:T:CH] if d == 0 else GB[:, d, 0:T:CH]
                        ch.link(nc.vector.tensor_copy(EL[:, d, :], last))
                        ch.link(nc.vector.tensor_tensor(KD[:, d, :], SIG[:, d, :], BB[:, :], ALU.mult))
                        nc.vector.tensor_tensor(SIG[:, d, :].rearrange("p (c t) -> p c t", t=CH), KD[:, d, :].rearrange("p (c t) -> p c t", t=CH),
                                                EL[:, d, :].unsqueeze(2).broadcast_to((P, NCH, CH)), ALU.mult)
                        nc.vector.scalar_tensor_tensor(QD[:, d, :], RQ[:, :], float(P) ** -0.5, GB[:, d], ALU.mult, ALU.mult).then_inc(dir_ready, 1)
                    dve.wait_ge(proj_out, r * PG + (PG + C_OUT))
                    ch.step(nc.vector.tensor_tensor(RG[:, :], RG[:, :], ZR[:, :], ALU.mult))
                    dve.wait_ge(o_done, r * NT + 1)
                    for j in range(1, NT, 2):
                        dve.wait_ge(t_done, r * NT + j + 2)
                        nc.vector.tensor_copy(TK[:, j].rearrange("p a b -> p (a b)"), t_bank(j)[:, 0:3 * P]).then_inc(t_out_v, 1)
                    dve.wait_ge(s0_in, r * 32 + 32)
                    dve.wait_ge(st_store, r * 32 + 1)
                    count = [0, 0]
                    for j in range(NT):
                        dve.wait_ge(kv_done, r * NT + j + 1)
                        for half in range(2):
                            for d, order in enumerate((FWD, BWD)):
                                c, nxt = order[2 * j + half]
                                used = (kvps, aps)[c % 2][:, j % 2, d * P:(d + 1) * P]
                                if (d, c) in ((0, NCH - 1), (1, 2)):
                                    continue
                                if count[d]:
                                    dve.wait_ge(st[d], r * 17 + count[d])
                                ins = nc.vector.scalar_tensor_tensor(S[:, d, nxt, :], S[:, d, c, :], EL[:, d, c:c + 1], used, ALU.mult, ALU.add)
                                ins.then_inc(st[d], 1)
                                count[d] += 1
                        assert count == [links(0, j), links(1, j)]
                    for j in range(NT):
                        dve.wait_ge(a_done, r * NT + j + 1)
                        if j >= 2:
                            dve.wait_ge(o_done, r * NT + j)
                        nc.vector.tensor_tensor(AM[:, j % 2, :], aps[:, (j + 1) % 2, 0:2 * P], M2[:, :], ALU.mult).then_inc(a_out, 1)
                    ch.wait()
                    for g in range(NG):
                        dve.wait_ge(ss_out, r * NG + g + 1)
                        cols = slice(g * G, (g + 1) * G)
                        nc.vector.reciprocal(RS[:, cols], RS[:, cols]).then_inc(ss_inv, 1)
                        dve.wait_ge(ss_inv, r * NG + g + 1)
                        nc.vector.scalar_tensor_tensor(OT[:, cols], OT[:, cols], rgain[:, 0:1], RS[:, cols], ALU.mult, ALU.mult).then_inc(rec_t, 1)
                        dve.wait_ge(rec_t, r * NG + g + 1)
                        nc.vector.tensor_tensor(OT[:, cols], OT[:, cols], RG[:, cols], ALU.mult).then_inc(rec_ready, 1)
                    assert ch.n == 8, ch.n


def phase2(nc, a, sem, W, w_o, HH, HL, ident, w_in, w_in64, rec_dram, mix_dram, out_k, out_v):
    with ExitStack() as ctx:
        def sb(name, shape, dt=F32):
            return ctx.enter_context(nc.sbuf_tensor(name, shape, dt))

        WR, W_HI, W_LO = W
        WX_HI, WX_LO = sb("w2_hi", [P, KC, P], F32R), sb("w2_lo", [P, KC, P], F32R)
        WH = [W_HI[:, 0], W_HI[:, 1], W_HI[:, 2], WX_HI[:, :, :]]
        WL = [W_LO[:, 0], W_LO[:, 1], W_LO[:, 2], WX_LO[:, :, :]]
        QKV = sb("qkv", [P, NT, G])
        KH = sb("keys_hi2", [P, NKC * P], F32R)
        KL = sb("keys_lo1", [HEAD + 1, NKC * P], F32R)
        V1 = sb("values_hi1", [P, NKC, P], F32R)
        V2 = sb("values_lo", [P, NKC, HEAD], F32R)
        PE32 = sb("probs", [P, 2, 512])
        PH = sb("probs_hi", [P, 4, 512], F32R)
        PL = sb("probs_lo", [P, 4, 512], F32R)
        KS = PH[:, :, :].rearrange("p a b -> p (a b)")[:, 0:2 * 3 * 3 * HEAD].rearrange("p (s i c) -> p s i c", s=2, i=3)
        QT1 = sb("q_t_hilo", [P, 2, 512], F32R)
        QT2 = sb("q_t_max", [HEAD + 1, 2, 512], F32R)
        QS1 = sb("q_stage", [P, GQ, P], F32R)
        QS2 = sb("q_stage_max", [P, GQ, HEAD + 2], F32R)
        ATT = sb("attn_t", [P, 2, T])
        ZA = sb("za_gate", [P, 2, T])
        COS, SIN = sb("cos", [P, NT - 1, HEAD]), sb("sin", [P, NT - 1, HEAD])
        R1, R2 = (ATT[:, :, :].rearrange("p a t -> p (a t)")[:, i * 15 * HEAD:(i + 1) * 15 * HEAD].rearrange("p (t c) -> p t c", t=3)
                  for i in range(2))
        SS, RST = sb("qk_ss", [P, 15]), sb("qk_rstd", [P, 15])
        M4 = sb("row_max", [P, GQ])
        RR = sb("inv_sum", [HEAD, 512])
        RN = sb("inv_sum_check", [HEAD, 512])
        CK, CV = sb("cache_k_in", [P, 2, HEAD]), sb("cache_v_in", [P, 2, HEAD])
        GN = sb("qk_gain", [P, 2, HEAD])
        ps = ctx.enter_context(nc.psum_tensor("att_ps", [P, 8, 512], F32))
        B_S, B_QT, B_ST, B_PV, B_PROJ, B_GATE, B_KT = 0, 3, 4, 6, 4, 6, 0

        raw_in = [sem("a_raw_in0"), sem("a_raw_in1")]
        w_go, w_hi, w_split = sem("a_w_go"), sem("a_w_hi"), sem("a_w_split")
        proj_done, proj_out = sem("a_proj_done"), sem("a_proj_out")
        ss_ok, rst_ok, n_ch = sem("a_ss_ok"), sem("a_rst_ok"), sem("a_norm_chain")
        ks_ok, kt_done, kt_out, v_ok = sem("a_ks_ok"), sem("a_kt_done"), sem("a_kt_out"), sem("a_v_ok")
        qs1_ok, qs2_ok, qt_done, qt_out = sem("a_qs1_ok"), sem("a_qs2_ok"), sem("a_qt_done"), sem("a_qt_out")
        qs_hi = sem("a_qs_hi")
        s_done, m_done = sem("a_s_done"), sem("a_m_done")
        st_done, ex_done, lo_done, pv_done = sem("a_st_done"), sem("a_ex_done"), sem("a_lo_done"), sem("a_pv_done")
        r_ln, r_est, r_new, att_ok = sem("a_r_ln"), sem("a_r_est"), sem("a_r_new"), sem("a_att_ok")
        za_sig, za_mul, rec_in, mix_ok, mix_store = sem("a_za_sig"), sem("a_za_mul"), sem("a_rec_in"), sem("a_mix_ok"), sem("a_mix_store")
        ctx_in, kv_store, const_in, set_ok = sem("a_ctx_in"), sem("a_kv_store"), sem("a_const_in"), sem("a_set_ok")

        NU, PG, C_SPLIT, C_PROJ, C_OUT = 5, 15, 2, 7, 2
        NS = 9
        NC = 1 + 10 * (NS - 1)

        MAX_AT = (0, 2, 4, 6)

        def keys(n):
            return range(0, 1) if n == 0 else range(1, NKC)

        def idx(n, i):
            return 0 if n == 0 else 1 + 10 * (n - 1) + i

        def slot(n, i):
            return 1 if n == 0 else i % 2

        def split_slot(n, i):
            return (idx(n, i) - 1) % 4

        def after(n, i):
            nc_ = len(keys(n))
            if n == 0:
                return (1, 1)
            if i + 2 < nc_:
                return (n, i + 2)
            return (n + 1, i + 2 - nc_) if n + 1 < NS else None

        with nc.Block() as block:
            def all_steps(eng, kv, step):
                step(0, 0)
                with eng.Fori(0, 3) as p:
                    step(1, p * 2)
                    step(2, p * 2)
                step(7, 0)
                step(8, 0)

            @block.sync
            def _(sp):
                for dst, src in ((COS[:, :, :], a["c_cos"].rearrange("(t p) d -> p t d", p=P)),
                                 (SIN[:, :, :], a["c_sin"].rearrange("(t p) d -> p t d", p=P)),
                                 (GN[:, 0, :], a["q_norm"][0].partition_broadcast(P)),
                                 (GN[:, 1, :], a["k_norm"][0].partition_broadcast(P))):
                    sp.dma_start(dst, src).then_inc(const_in, 16)
                def load(kv, u):
                    before = (0, -1, 1, 2, 3)[u]
                    sp.wait_ge(w_split, kv * NU + (before + C_SPLIT))
                    if u < 3:
                        load_qkv(sp, WR, w_in, w_in64, kv, u, raw_in[u % 2])
                    else:
                        sp.dma_start(WR[:, u % 2], w_in[kv * 2 + (B_ZA + u - 3)]).then_inc(raw_in[u % 2], 16)

                def load_head(kv):
                    load(kv, 3)
                    load(kv, 4)
                    sp.wait_ge(v_ok, kv + 1)
                    sp.wait_ge(ks_ok, kv * 4 + 1)
                    sp.dma_start(CK[:, :, :], a["cache_k"][0, 0].rearrange("(b p) h d -> h p b d", p=P)[kv]).then_inc(ctx_in, 16)
                    sp.dma_start(CV[:, :, :], a["cache_v"][0, 0].rearrange("(b p) h d -> h p b d", p=P)[kv]).then_inc(ctx_in, 16)
                    sp.wait_ge(ks_ok, kv * 4 + 2)
                    sp.dma_start(out_k[0, 0].rearrange("t h d -> h t d")[kv], QKV[:, 0, 4 * HEAD:5 * HEAD]).then_inc(kv_store, 16)
                    sp.dma_start(out_v[0, 0].rearrange("t h d -> h t d")[kv], QKV[:, 0, 5 * HEAD:6 * HEAD]).then_inc(kv_store, 16)

                def merge(kv):
                    sp.wait_ge(za_mul, kv + 1)
                    for j in range(2):
                        sp.dma_start(ZA[:, j, :], rec_dram[kv * 2 + j]).then_inc(rec_in, 16)
                    for j in range(2):
                        sp.wait_ge(mix_ok, kv * 2 + j + 2)
                        sp.dma_start(mix_dram[kv * 2 + j], ATT[:, j, :]).then_inc(mix_store, 16)

                with sp.Fori(0, NKV - 1) as kv:
                    load_head(kv)
                    for u in range(3):
                        load(kv + 1, u)
                    merge(kv)
                load_head(NKV - 1)
                for u in range(2):
                    sp.wait_ge(w_split, (NKV - 1) * NU + (5 if u == 0 else 4) + C_SPLIT)
                    sp.dma_start(WR[:, u], w_o[u]).then_inc(raw_in[u], 16)
                merge(NKV - 1)
                sp.wait_ge(mix_store, 32 * NKV + 1)
                sp.wait_ge(kv_store, 32 * NKV + 1)

            @block.gpsimd
            def _(pool):
                pool.sem_inc(w_split, C_SPLIT + 3)
                pool.sem_inc(w_hi, 3)
                pool.sem_inc(raw_in[0], 48)
                pool.sem_inc(raw_in[1], 16)

                def split(u, n0, raw, used):
                    pool.wait_ge(raw_in[u % 2], raw)
                    pool.wait_ge(proj_done, used)
                    pool.sem_inc(w_go, 1)
                    nc.gpsimd.tensor_copy(WH[u % 4], WR[:, u % 2]).then_inc(w_hi, 1)
                    pool.wait_ge(w_hi, n0 + (u + 1))
                    nc.gpsimd.tensor_tensor(WL[u % 4], WR[:, u % 2], WH[u % 4].bitcast(F32), ALU.subtract).then_inc(w_split, 1)

                def split_unit(kv, u):
                    split(u, kv * NU, kv * (64, 32)[u % 2] + (16, 16, 48, 32, 64)[u], kv * PG + (7, 1, 1, 4, 16)[u])

                with pool.Fori(0, NKV - 1) as kv:
                    split_unit(kv, 3)
                    split_unit(kv, 4)
                    for u in range(3):
                        split_unit(kv + 1, u)
                split_unit(NKV - 1, 3)
                split_unit(NKV - 1, 4)
                for u in range(2):
                    split(u, NKV * NU, NKV * (64, 32)[u] + 16, NKV * PG + C_PROJ)

            def key_transposes(pe, kv, g):
                pe.wait_ge(ks_ok, kv * 4 + g + 2)
                pe.wait_ge(kt_out, kv * 8 + (2 * (g - 1) if g >= 2 else 0) + 2)
                n = 3 if g < 3 else 2
                for i in range(n):
                    m = nc.tensor.transpose(ps[:, B_KT + 2 * (g % 2), i * P:(i + 1) * P], KS[:, g % 2, i, 0:P].bitcast(F32), ident[:, :])
                for i in range(n):
                    m = nc.tensor.transpose(ps[0:HEAD, B_KT + 2 * (g % 2) + 1, i * P:(i + 1) * P], KS[:, g % 2, i, P:3 * HEAD].bitcast(F32), ident[:, :])
                m.then_inc(kt_done, 1)

            @block.tensor
            def _(pe):
                pe.sem_inc(proj_done, C_PROJ)
                pe.sem_inc(kt_done, 1)
                pe.wait_ge(set_ok, 2)
                with pe.Fori(0, NKV) as kv:
                    def gate_part(n, k0, k1):
                        u, g = 3 + (n - NT) // NG, (n - NT) % NG
                        bank = ps[:, B_GATE + n % 2, 0:G]
                        if k0 == 0:
                            if g == 0:
                                pe.wait_ge(w_split, kv * NU + (u + 1 + C_SPLIT))
                            pe.wait_ge(proj_out, kv * PG + (n - 1 + C_OUT))
                        for k in range(k0, k1):
                            m = three_pass(nc, bank, WH[u % 4][:, k], WL[u % 4][:, k],
                                           HH[:, k, g * G:(g + 1) * G], HL[:, k, g * G:(g + 1) * G], k, k == KC - 1)
                        if k1 == KC:
                            m.then_inc(proj_done, 1)

                    pe.wait_ge(w_split, kv * NU + (3 + C_SPLIT))
                    for n in range(NT):
                        pe.wait_ge(proj_out, kv * PG + (n - 1 if n else 0) + C_OUT)
                        bank = ps[:, B_PROJ + n % 2, 0:G]
                        cols = slice(n * P, (n + 1) * P)
                        for k in range(KC):
                            nc.tensor.matmul(bank, HH[:, k, cols], W_HI[:, :, k, :], start=(k == 0), stop=False)
                            nc.tensor.matmul(bank, HL[:, k, cols], W_HI[:, :, k, :], start=False, stop=False)
                            m = nc.tensor.matmul(bank, HH[:, k, cols], W_LO[:, :, k, :], start=False, stop=(k == KC - 1))
                        m.then_inc(proj_done, 1)
                    pe.wait_ge(att_ok, kv * NS + 1)
                    for g in range(3):
                        gate_part(NT + g, 0, KC)
                        key_transposes(pe, kv, g)
                    gate_part(NT + 3, 0, 3)
                    key_transposes(pe, kv, 3)

                    def wait_step(sem_, per_kv, count, o, per_step):
                        pe.wait_ge(sem_, kv * per_kv + o * per_step + count)

                    def q_part(n, o):
                        wait_step(qs1_ok, NS, n + 1, o, 1)
                        wait_step(qt_out, 2 * NS, 2 * n + 1, o, 2)
                        for h in range(GQ):
                            m = nc.tensor.transpose(ps[:, B_QT, h * P:(h + 1) * P], QS1[:, h, :].bitcast(F32), ident[:, :])
                        m.then_inc(qt_done, 1)

                    def max_scores(n, o, h):
                        if h == 0:
                            wait_step(qt_out, 2 * NS, 2 * n + 2, o, 2)
                        wait_step(m_done, 4 * NS, 4 * n + h + 1, o, 4)
                        k0, k1 = keys(n)[0] * P, (keys(n)[-1] + 1) * P
                        for i, c in enumerate(range(k0, k1, 512)):
                            w = min(512, k1 - c)
                            m = nc.tensor.matmul(ps[:, B_S + i, 0:w], QT1[:, n % 2, h * P:(h + 1) * P], KH[:, c:c + w], start=True, stop=True)
                        m.then_inc(s_done, 1)

                    def q_max_part(n, o):
                        wait_step(qs2_ok, NS, n + 2, o, 1)
                        for h in range(GQ):
                            m = nc.tensor.transpose(ps[0:HEAD + 1, B_QT, h * P:(h + 1) * P], QS2[:, h, 0:HEAD + 1].bitcast(F32), ident[:, :])
                        m.then_inc(qt_done, 1)

                    def scores_t(n, o, i):
                        g = idx(n, i)
                        if i == 0:
                            wait_step(qt_out, 2 * NS, 2 * n + 3, o, 2)
                        wait_step(ex_done, NC, max(g - 1, 0) + 1, o, 10)
                        c = keys(n)[i] * P
                        bank = ps[:, B_ST + slot(n, i), :]
                        nc.tensor.matmul(bank, KH[:, c:c + P], QT1[:, n % 2, :], start=True, stop=False)
                        nc.tensor.matmul(bank, KL[:, c:c + P], QT2[:, n % 2, :], start=False, stop=True).then_inc(st_done, 1)

                    def weighted(n, o, i):
                        if i == 0:
                            wait_step(att_ok, NS, max(n, 1), o, 1)
                        wait_step(lo_done, NC, idx(n, i) + 2, o, 10)
                        c, s = keys(n)[i], split_slot(n, i)
                        last = i == len(keys(n)) - 1
                        nc.tensor.matmul(ps[:, B_PV + n % 2, :], V1[:, c, :], PH[:, s, :], start=(i == 0), stop=False)
                        nc.tensor.matmul(ps[0:HEAD, B_PV + n % 2, :], V2[:, c, :], PH[:, s, :], start=False, stop=False)
                        nc.tensor.matmul(ps[:, B_PV + n % 2, :], V1[:, c, :], PL[:, s, :], start=False, stop=last).then_inc(pv_done, 1)

                    pe.wait_ge(kt_out, kv * 8 + 10)
                    q_part(0, 0)
                    gate_part(NT + 3, 3, 5)
                    for h in range(GQ):
                        max_scores(0, 0, h)
                    gate_part(NT + 3, 5, 6)
                    q_max_part(0, 0)
                    gate_part(NT + 3, 6, 7)
                    scores_t(0, 0, 0)

                    def step(n, o):
                        if n == 0:
                            q_part(1, o)
                            gate_part(NT + 3, 7, KC)
                            for h in range(GQ):
                                max_scores(1, o, h)
                                gate_part(NT + 4 + h // 2, h % 2 * 4, h % 2 * 4 + 4)
                            q_max_part(1, o)
                            scores_t(1, o, 0)
                            pe.wait_ge(v_ok, kv + 2)
                            pe.wait_ge(proj_out, kv * PG + PG + C_OUT)
                        for i in range(len(keys(n))):
                            ahead = n and n + 1 < NS
                            if i == 8:
                                weighted(n, o, i)
                            if after(n, i):
                                scores_t(after(n, i)[0], o, after(n, i)[1])
                            if ahead and i in MAX_AT[1:]:
                                max_scores(n + 1, o, MAX_AT.index(i))
                            if i != 8:
                                weighted(n, o, i)
                            if ahead and i == MAX_AT[0]:
                                max_scores(n + 1, o, 0)
                            if ahead and i == 7:
                                q_max_part(n + 1, o)
                        if n + 2 < NS:
                            q_part(n + 2, o)

                    all_steps(pe, kv, step)

            @block.scalar
            def _(act):
                act.sem_inc(proj_out, C_OUT)
                act.sem_inc(kt_out, 2)
                act.sem_inc(qt_out, 1)
                act.sem_inc(ex_done, 1)
                with act.Fori(0, NKV) as kv:
                    def wait_step(sem_, per_kv, count, o, per_step):
                        act.wait_ge(sem_, kv * per_kv + o * per_step + count)

                    act.wait_ge(kv_store, kv * 32 + 1)
                    def gate_out(n):
                        act.wait_ge(proj_done, kv * PG + (n + 1 + C_PROJ))
                        u, g = divmod(n - NT, NG)
                        nc.scalar.activation(ZA[:, u, g * G:(g + 1) * G], ps[:, B_GATE + n % 2, 0:G], ACT.Copy).then_inc(proj_out, 1)

                    def norms(g):
                        act.wait_ge(ss_ok, kv * 3 + g + 1)
                        nc.scalar.activation(RST[:, :], SS[:, :], ACT.Sqrt).then_inc(rst_ok, 1)

                    def keys_out(g):
                        w = (3 if g < 3 else 2) * P
                        act.wait_ge(kt_done, kv * 4 + g + 2)
                        nc.scalar.activation(KH[:, 3 * g * P:3 * g * P + w], ps[:, B_KT + 2 * (g % 2), 0:w], ACT.Copy).then_inc(kt_out, 1)
                        nc.scalar.activation(KL[0:HEAD, 3 * g * P:3 * g * P + w], ps[0:HEAD, B_KT + 2 * (g % 2) + 1, 0:w], ACT.Copy).then_inc(kt_out, 1)

                    for n in range(NT):
                        act.wait_ge(proj_done, kv * PG + (n + 1 + C_PROJ))
                        nc.scalar.activation(QKV[:, n, :], ps[:, B_PROJ + n % 2, 0:G], ACT.Copy).then_inc(proj_out, 1)
                        if n in (3, 6):
                            norms(n // 3 - 1)
                    act.wait_ge(mix_ok, kv * 2 + 1)
                    gate_out(NT)
                    norms(2)
                    keys_out(0)
                    for g in (1, 2):
                        gate_out(NT + g)
                        keys_out(g)
                    keys_out(3)

                    def q_out(n, o):
                        wait_step(qt_done, 2 * NS, 2 * n + 1, o, 2)
                        nc.scalar.activation(QT1[:, n % 2, :], ps[:, B_QT, :], ACT.Copy).then_inc(qt_out, 1)

                    def q_max_out(n, o):
                        wait_step(qt_done, 2 * NS, 2 * n + 2, o, 2)
                        nc.scalar.activation(QT2[:, n % 2, :], ps[0:HEAD + 1, B_QT, :], ACT.Copy).then_inc(qt_out, 1)

                    def exp(n, o, i):
                        g = idx(n, i)
                        wait_step(st_done, NC, g + 1, o, 10)
                        wait_step(lo_done, NC, max(g - 1, 0) + 1, o, 10)
                        nc.scalar.activation(PE32[:, slot(n, i), :], ps[:, B_ST + slot(n, i), :], ACT.Exp, scale=HEAD ** -0.5)
                        if g >= 4:
                            wait_step(pv_done, NC, g - 3, o, 10)
                        nc.scalar.activation(PH[:, split_slot(n, i), :], ps[:, B_ST + slot(n, i), :], ACT.Exp, scale=HEAD ** -0.5).then_inc(ex_done, 1)

                    nc.scalar.preload_act_table_set(LN_EXP)

                    def inverse_estimate(n, o):
                        wait_step(pv_done, NC, idx(n, len(keys(n)) - 1) + 1, o, 10)
                        wait_step(att_ok, NS, n + 1, o, 1)
                        nc.scalar.activation(RR[:, :], ps[HEAD:P, B_PV + n % 2, :], ACT.Ln).then_inc(r_ln, 1)
                        wait_step(r_ln, NS, n + 1, o, 1)
                        nc.scalar.activation(RR[:, :], RR[:, :], ACT.Exp, scale=-1.0).then_inc(r_est, 1)

                    q_out(0, 0)
                    q_max_out(0, 0)
                    exp(0, 0, 0)

                    def step(n, o):
                        if n == 0:
                            q_out(1, o)
                            for g in (3, 4, 5):
                                gate_out(NT + g)
                            q_max_out(1, o)
                            exp(1, o, 0)
                        for i in range(len(keys(n))):
                            if after(n, i):
                                exp(after(n, i)[0], o, after(n, i)[1])
                            if i == 0 and n:
                                inverse_estimate(n - 1, o)
                            if i == 7 and n and n + 1 < NS:
                                q_max_out(n + 1, o)
                        if n + 2 < NS:
                            q_out(n + 2, o)

                    all_steps(act, kv, step)
                    act.wait_ge(proj_out, kv * PG + PG + C_OUT)
                    nc.scalar.activation(ZA[:, :, :], ZA[:, :, :], ACT.Sigmoid).then_inc(za_sig, 1)
                    nc.scalar.preload_act_table_set(LN_EXP)
                    inverse_estimate(NS - 1, 0)

            @block.vector
            def _(dve):
                nc.vector.memset(KL[HEAD:HEAD + 1, :].bitcast(F32), 1.0).then_inc(set_ok, 1)
                nc.vector.memset(V1[:, :, HEAD:P].bitcast(F32), 1.0).then_inc(set_ok, 1)
                for s in (v_ok, ks_ok, kv_store, mix_store, mix_ok, m_done, lo_done, att_ok, qs2_ok):
                    dve.sem_inc(s, 1)
                dve.wait_ge(const_in, 64)
                with dve.Fori(0, NKV) as kv:
                    def wait_step(sem_, per_kv, count, o, per_step):
                        dve.wait_ge(sem_, kv * per_kv + o * per_step + count)

                    ch = Chain(dve, n_ch, kv * CHAIN2)

                    def stage_keys(g, src, n):
                        dve.wait_ge(kt_done, kv * 4 + (g - 1 if g >= 2 else 0) + 1)
                        ch.wait()
                        st = KS[:, g % 2, 0:n, :]
                        nc.vector.tensor_copy(st[:, :, 0:HEAD], src)
                        ch.link(nc.vector.tensor_copy(st[:, :, HEAD:P], src))
                        nc.vector.tensor_tensor(st[:, :, P:3 * HEAD], src, st[:, :, 0:HEAD].bitcast(F32), ALU.subtract).then_inc(ks_ok, 1)

                    dve.wait_ge(mix_store, kv * 32 + 1)
                    for g in range(3):
                        dve.wait_ge(proj_out, kv * PG + (3 * g + 3 + C_OUT))
                        if g:
                            ch.wait()
                        x = QKV[:, 3 * g:3 * g + 3, 0:5 * HEAD]
                        x4 = x.rearrange("p t (h d) -> p t h d", d=HEAD)
                        ch.link(nc.vector.tensor_tensor(R1[:, :, :], x, x, ALU.mult))
                        ch.link(nc.vector.tensor_reduce(SS[:, :], R1[:, :, :].rearrange("p t (h d) -> p (t h) d", d=HEAD), AX_X, ALU.add))
                        nc.vector.tensor_scalar(SS[:, :], SS[:, :], 1.0 / HEAD, EPS, ALU.mult, ALU.add).then_inc(ss_ok, 1)
                        dve.wait_ge(rst_ok, kv * 3 + g + 1)
                        ch.link(nc.vector.reciprocal(RST[:, :], RST[:, :]))
                        ch.link(nc.vector.tensor_tensor(x4, x4, RST[:, :].rearrange("p (t h) -> p t h", t=3).unsqueeze(3).broadcast_to((P, 3, 5, HEAD)), ALU.mult))
                        ch.step(nc.vector.tensor_tensor(x4[:, :, 0:4, :], x4[:, :, 0:4, :], GN[:, 0, :].unsqueeze(1).unsqueeze(1).broadcast_to((P, 3, 4, HEAD)), ALU.mult))
                        ch.link(nc.vector.tensor_tensor(x4[:, :, 4, :], x4[:, :, 4, :], GN[:, 1, :].unsqueeze(1).broadcast_to((P, 3, HEAD)), ALU.mult))
                        tiles = [t for t in range(3 * g, 3 * g + 3) if t]
                        for t in tiles:
                            i = t - 3 * g
                            xt = QKV[:, t, 0:5 * HEAD].rearrange("p (h d) -> p h d", d=HEAD)
                            nc.vector.tensor_tensor(R1[:, i, :].rearrange("p (h d) -> p h d", d=HEAD), xt,
                                                    COS[:, t - 1, :].unsqueeze(1).broadcast_to((P, 5, HEAD)), ALU.mult)
                            for half in range(2):
                                v = lambda z: z.rearrange("p h (s b e) -> p h s b e", s=2, b=2)
                                m = nc.vector.tensor_tensor(v(R2[:, i, :].rearrange("p (h d) -> p h d", d=HEAD))[:, :, :, half, :],
                                                            v(xt)[:, :, :, 1 - half, :],
                                                            SIN[:, t - 1, :].rearrange("p (s b e) -> p s b e", s=2, b=2)[:, :, half, :].unsqueeze(1).broadcast_to((P, 5, 2, 16)), ALU.mult)
                        ch.link(m)
                        i0 = tiles[0] - 3 * g
                        ch.link(nc.vector.tensor_tensor(QKV[:, tiles[0]:3 * g + 3, 0:5 * HEAD], R1[:, i0:3, :], R2[:, i0:3, :], ALU.add))
                        stage_keys(g, QKV[:, 3 * g:3 * g + 3, 4 * HEAD:5 * HEAD], 3)
                    dve.wait_ge(ctx_in, kv * 32 + 32)
                    stage_keys(3, CK[:, :, :], 2)
                    def stage_q(n, o):
                        if n:
                            wait_step(qt_done, 2 * NS, 2 * n, o, 2)
                        q = (QKV[:, n, 0:4 * HEAD] if isinstance(o, int) else QKV[:, bass.ds(o + n, 1), 0:4 * HEAD].rearrange("p a d -> p (a d)"))
                        q = q.rearrange("p (h d) -> p h d", d=HEAD)
                        nc.vector.tensor_copy(QS2[:, :, 0:HEAD], q)
                        nc.vector.tensor_copy(QS1[:, :, 0:HEAD], q).then_inc(qs_hi, 1)
                        wait_step(qs_hi, NS, n + 1, o, 1)
                        nc.vector.tensor_tensor(QS1[:, :, HEAD:P], q, QS1[:, :, 0:HEAD].bitcast(F32), ALU.subtract).then_inc(qs1_ok, 1)

                    def row_max(n, o, h):
                        wait_step(s_done, 4 * NS, 4 * n + h + 1, o, 4)
                        if h == 0:
                            wait_step(qs2_ok, NS, n + 1, o, 1)
                        w = len(keys(n)) * P
                        s = ps[:, B_S:B_S + 3, :].rearrange("p a b -> p (a b)")[:, 0:w]
                        nc.vector.tensor_reduce(M4[:, h:h + 1], s, AX_X, ALU.max).then_inc(m_done, 1)

                    def put_max(n, o):
                        wait_step(m_done, 4 * NS, 4 * n + 5, o, 4)
                        nc.vector.tensor_scalar(QS2[:, :, HEAD], M4[:, :], -1.0, None, ALU.mult).then_inc(qs2_ok, 1)

                    def low(n, o, i):
                        g = idx(n, i)
                        wait_step(ex_done, NC, g + 2, o, 10)
                        if g >= 4:
                            wait_step(pv_done, NC, g - 3, o, 10)
                        s = split_slot(n, i)
                        nc.vector.tensor_tensor(PL[:, s, :], PE32[:, slot(n, i), :], PH[:, s, :].bitcast(F32), ALU.subtract).then_inc(lo_done, 1)

                    def check_inverse(n, o):
                        wait_step(r_est, NS, n + 1, o, 1)
                        nc.vector.tensor_tensor(RN[:, :], ps[HEAD:P, B_PV + n % 2, :], RR[:, :], ALU.mult).then_inc(r_new, 1)

                    def refine_inverse(n, o):
                        wait_step(r_new, 2 * NS, 2 * n + 1, o, 2)
                        nc.vector.scalar_tensor_tensor(RR[:, :], RN[:, :], 2.0, RR[:, :], ALU.subtract, ALU.mult).then_inc(r_new, 1)

                    def normalise(n, o):
                        wait_step(r_new, 2 * NS, 2 * n + 2, o, 2)
                        for par in range(2):
                            out = ATT[par * HEAD:(par + 1) * HEAD, :, :]
                            out = out[:, :, n * P:(n + 1) * P] if isinstance(o, int) else out[:, :, bass.ds(o * P + n * P, P)]
                            m = nc.vector.scalar_tensor_tensor(out, ps[0:HEAD, B_PV + n % 2, :].rearrange("p (j b q) -> p b j q", j=2, b=2)[:, par], -1.0,
                                                               RR[:, :].rearrange("p (j b q) -> p b j q", j=2, b=2)[:, par], ALU.mult, ALU.mult)
                        m.then_inc(att_ok, 1)

                    stage_q(0, 0)
                    val = QKV[:, :, 5 * HEAD:6 * HEAD]
                    ch.step(nc.vector.tensor_copy(V1[:, 0:NT, 0:HEAD], val))
                    ch.link(nc.vector.tensor_copy(V1[:, NT:NKC, 0:HEAD], CV[:, :, :]))
                    ch.link(nc.vector.tensor_tensor(V2[:, 0:NT, :], val, V1[:, 0:NT, 0:HEAD].bitcast(F32), ALU.subtract))
                    nc.vector.tensor_tensor(V2[:, NT:NKC, :], CV[:, :, :], V1[:, NT:NKC, 0:HEAD].bitcast(F32), ALU.subtract).then_inc(v_ok, 1)
                    for h in range(GQ):
                        row_max(0, 0, h)
                    put_max(0, 0)
                    stage_q(1, 0)
                    low(0, 0, 0)

                    def step(n, o):
                        if n == 0:
                            for h in range(GQ):
                                row_max(1, o, h)
                            put_max(1, o)
                            stage_q(2, o)
                            low(1, o, 0)
                        for i in range(len(keys(n))):
                            if n and n + 1 < NS and i in MAX_AT:
                                row_max(n + 1, o, MAX_AT.index(i))
                                if i == MAX_AT[-1]:
                                    put_max(n + 1, o)
                            if i == 8 and n and n + 2 < NS:
                                stage_q(n + 2, o)
                            if after(n, i):
                                low(after(n, i)[0], o, after(n, i)[1])
                            if n and i in (1, 3, 5):
                                {1: check_inverse, 3: refine_inverse, 5: normalise}[i](n - 1, o)

                    all_steps(dve, kv, step)
                    check_inverse(NS - 1, 0)
                    refine_inverse(NS - 1, 0)
                    normalise(NS - 1, 0)
                    dve.wait_ge(att_ok, kv * NS + NS + 1)
                    dve.wait_ge(za_sig, kv + 1)
                    nc.vector.tensor_tensor(ATT[:, :, :], ATT[:, :, :], ZA[:, :, :], ALU.mult).then_inc(za_mul, 1)
                    dve.wait_ge(za_mul, kv + 1)
                    dve.wait_ge(rec_in, kv * 32 + 32)
                    for j in range(2):
                        nc.vector.tensor_tensor(ATT[:, j, :], ATT[:, j, :], ZA[:, j, :], ALU.add).then_inc(mix_ok, 1)
                    assert ch.n == CHAIN2, ch.n



def phase3(nc, a, sem, W, w_up, HH, HL, ident, ones, MOD, A2, X1, w_o, mix_dram):
    with ExitStack() as ctx:
        def sb(name, shape, dt=F32):
            return ctx.enter_context(nc.sbuf_tensor(name, shape, dt))

        WR, WH, WL = W
        X = sb("x3", [P, 2, D])
        MS = sb("mix_in", [P, 2, T])
        RS = sb("rs3", [P, T])
        PRE = sb("pre3", [P, 2, T])
        SQ = PRE
        EPSB = sb("eps3", [P, 1])
        ps = ctx.enter_context(nc.psum_tensor("out_ps", [P, 8, 512], F32))

        raw_in = [sem("o_raw_in0"), sem("o_raw_in1")]
        w_go, w_hi, w_split = sem("o_w_go"), sem("o_w_hi"), sem("o_w_split")
        x_in = [sem("o_x_in0"), sem("o_x_in1")]
        mix_in = [sem("o_mix_in0"), sem("o_mix_in1")]
        xt_done, xt_out = sem("o_xt_done"), sem("o_xt_out")
        mh, ml = sem("o_mix_hi"), sem("o_mix_lo")
        proj_done, res_ok = sem("o_proj_done"), sem("o_res_ok")
        sq_ok, ss_done, ss_sqrt, rs_ok = sem("o_sq_ok"), sem("o_ss_done"), sem("o_ss_sqrt"), sem("o_rs_ok")
        pre_ok, hi_ok, lo_ok, set_ok = sem("o_pre_ok"), sem("o_hi_ok"), sem("o_lo_ok"), sem("o_set_ok")
        C_SPLIT, C_PROJ = 2, 6

        def x_rows(t):
            return a["x_prompt"][0] if t == 0 else a["x_sample"][0, (t - 1) * P:t * P, :]

        with nc.Block() as block:
            @block.sync
            def _(sp):
                for t in range(NT):
                    if t >= 2:
                        sp.wait_ge(xt_done, 2 * (t - 1))
                    sp.dma_start(X[:, t % 2, :], x_rows(t)).then_inc(x_in[t % 2], 16)
                    if t < KC:
                        if t >= 2:
                            sp.wait_ge(ml, t - 1)
                        sp.dma_start(MS[:, t % 2, :], mix_dram[t]).then_inc(mix_in[t % 2], 16)
                with sp.Fori(1, KC // 2) as i:
                    for u in range(2):
                        sp.wait_ge(w_split, i * 2 + u + 1)
                        sp.dma_start(WR[:, u], w_o[i * 2 + u]).then_inc(raw_in[u], 16)
                for u in range(2):
                    sp.wait_ge(w_split, KC + u + 1)
                    sp.dma_start(WR[:, u], w_up[u * FB]).then_inc(raw_in[u], 16)

            @block.gpsimd
            def _(pool):
                pool.sem_inc(w_split, C_SPLIT + 2)
                pool.sem_inc(w_hi, 2)
                for s in raw_in:
                    pool.sem_inc(s, 16)

                def split(i, u):
                    pool.wait_ge(raw_in[u], i * 16 + 16)
                    pool.wait_ge(proj_done, i * 6 + (NG * (u - 2) + NG + C_PROJ))
                    pool.sem_inc(w_go, 1)
                    nc.gpsimd.tensor_copy(WH[:, u], WR[:, u]).then_inc(w_hi, 1)
                    pool.wait_ge(w_hi, i * 2 + u + 1)
                    nc.gpsimd.tensor_tensor(WL[:, u], WR[:, u], WH[:, u].bitcast(F32), ALU.subtract).then_inc(w_split, 1)

                with pool.Fori(1, KC // 2) as i:
                    for u in range(2):
                        split(i, u)
                for u in range(2):
                    split(KC // 2, u)

            @block.tensor
            def _(pe):
                pe.sem_inc(proj_done, C_PROJ)
                for t in range(NT):
                    pe.wait_ge(x_in[t % 2], 16 * (t // 2 + 1))
                    for q in range(2):
                        n = 2 * t + q
                        if n >= 4:
                            pe.wait_ge(xt_out, n - 3)
                        for i in range(4):
                            m = nc.tensor.transpose(ps[:, n % 4, i * P:(i + 1) * P], X[:, t % 2, (4 * q + i) * P:(4 * q + i + 1) * P], ident[:, :])
                        m.then_inc(xt_done, 1)
                pe.wait_ge(ml, KC)
                pe.wait_ge(xt_out, 2 * NT)
                with pe.Fori(0, KC // 2) as i:
                    for u in range(2):
                        pe.wait_ge(w_split, i * 2 + u + 1 + C_SPLIT)
                        for g in range(NG):
                            n = NG * u + g
                            pe.wait_ge(res_ok, i * 6 + n + 1)
                            for k in range(KC):
                                m = three_pass(nc, ps[:, n, 0:G], WH[:, u, k], WL[:, u, k],
                                               HH[:, k, g * G:(g + 1) * G], HL[:, k, g * G:(g + 1) * G], k, k == KC - 1)
                            m.then_inc(proj_done, 1)
                pe.wait_ge(res_ok, 6 * (KC // 2) + 6)
                for j in range(KC):
                    pe.wait_ge(sq_ok, j + 1)
                    for g in range(NG):
                        m = nc.tensor.matmul(ps[:, g, 0:G], ones[:, :], SQ[:, j % 2, g * G:(g + 1) * G], start=(j == 0), stop=(j == KC - 1))
                    m.then_inc(ss_done, 1)

            @block.scalar
            def _(act):
                for t in range(NT):
                    for q in range(2):
                        n = 2 * t + q
                        act.wait_ge(xt_done, n + 1)
                        nc.scalar.activation(X1[:, 4 * q:4 * q + 4, t * P:(t + 1) * P], ps[:, n % 4, :].rearrange("p (j c) -> p j c", j=4), ACT.Copy).then_inc(xt_out, 1)
                    if t < KC:
                        act.wait_ge(mix_in[t % 2], 16 * (t // 2 + 1))
                        nc.scalar.activation(HH[:, t, :], MS[:, t % 2, :], ACT.Copy).then_inc(mh, 1)
                act.wait_ge(res_ok, 6 * (KC // 2) + 6)
                act.wait_ge(set_ok, 1)
                for j in range(KC):
                    if j >= 2:
                        act.wait_ge(ss_done, j - 1)
                    nc.scalar.activation(SQ[:, j % 2], X1[:, j, :], ACT.Square).then_inc(sq_ok, 1)
                act.wait_ge(ss_done, KC)
                for g in range(NG):
                    nc.scalar.activation(RS[:, g * G:(g + 1) * G], ps[:, g, 0:G], ACT.Sqrt, scale=1.0 / D, bias=EPSB[:, 0:1]).then_inc(ss_sqrt, 1)
                for j in range(KC):
                    act.wait_ge(pre_ok, 2 * j + 2)
                    for grp, (t0, t1) in enumerate(RANGES):
                        nc.scalar.activation(HH[:, j, t0:t1], PRE[:, j % 2, t0:t1], ACT.Identity, bias=MOD[:, 24 + j, grp:grp + 1]).then_inc(hi_ok, 1)

            @block.vector
            def _(dve):
                nc.vector.memset(EPSB[:, :], EPS).then_inc(set_ok, 1)
                dve.sem_inc(res_ok, 6)
                for k in range(KC):
                    dve.wait_ge(mh, k + 1)
                    nc.vector.tensor_tensor(HL[:, k, :], MS[:, k % 2, :], HH[:, k, :].bitcast(F32), ALU.subtract).then_inc(ml, 1)
                dve.wait_ge(xt_out, 2 * NT)
                with dve.Fori(0, KC // 2) as i:
                    for u in range(2):
                        for g in range(NG):
                            n = NG * u + g
                            dve.wait_ge(proj_done, i * 6 + n + 1 + C_PROJ)
                            for t0, t1, grp in split_groups(g):
                                x = X1[:, bass.ds(i * 2 + u, 1), t0:t1].rearrange("p a t -> p (a t)")
                                gate = MOD[:, bass.ds(i * 2 + (16 + u), 1), grp:grp + 1].rearrange("p a t -> p (a t)")
                                m = nc.vector.scalar_tensor_tensor(x, ps[:, n, t0 - g * G:t1 - g * G], gate, x, ALU.mult, ALU.add)
                            m.then_inc(res_ok, 1)
                for g in range(NG):
                    dve.wait_ge(ss_sqrt, g + 1)
                    nc.vector.reciprocal(RS[:, g * G:(g + 1) * G], RS[:, g * G:(g + 1) * G]).then_inc(rs_ok, 1)
                dve.wait_ge(rs_ok, NG)

                def low(j):
                    for grp, (t0, t1) in enumerate(RANGES):
                        dve.wait_ge(hi_ok, 2 * j + grp + 1)
                        nc.vector.scalar_tensor_tensor(HL[:, j, t0:t1], PRE[:, j % 2, t0:t1], MOD[:, 24 + j, grp:grp + 1],
                                                       HH[:, j, t0:t1].bitcast(F32), ALU.add, ALU.subtract).then_inc(lo_ok, 1)
                for j in range(KC):
                    if j >= 2:
                        dve.wait_ge(lo_ok, 2 * (j - 1))
                    for grp, (t0, t1) in enumerate(RANGES):
                        nc.vector.scalar_tensor_tensor(PRE[:, j % 2, t0:t1], X1[:, j, t0:t1], A2[:, j, grp:grp + 1], RS[:, t0:t1],
                                                       ALU.mult, ALU.mult).then_inc(pre_ok, 1)
                    if j:
                        low(j - 1)
                low(KC - 1)


def phase4(nc, a, sem, W, HH, HL, MOD, CW, X1, w_up, w_down):
    with ExitStack() as ctx:
        def sb(name, shape, dt=F32):
            return ctx.enter_context(nc.sbuf_tensor(name, shape, dt))

        W_RAW, WH, WL = W
        WX_RAW = sb("w4_raw", [P, KC, P])
        WR = [W_RAW[:, 0], W_RAW[:, 1], WX_RAW[:, :, :]]
        U = sb("up", [P, 2, T])
        C = sb("conv", [P, 2, T])
        GF = sb("gated", [P, T])
        GH = sb("gated_hi", [P, T], F32R)
        GL = sb("gated_lo", [P, T], F32R)
        RING_UP, RING = 3, 5
        up = ctx.enter_context(nc.psum_tensor("up_ps", [P, RING_UP, 512], F32))
        dn = ctx.enter_context(nc.psum_tensor("down_ps", [P, RING, 512], F32))

        raw_in = [sem(f"f_raw_in{i}") for i in range(3)]
        w_go, w_hi = sem("f_w_go"), sem("f_w_hi")
        w_split = [sem(f"f_w_split{i}") for i in range(3)]
        up_done, up_out, taps = sem("f_up_done"), sem("f_up_out"), sem("f_taps")
        silu_ok, g_ok, gh_ok, gl_ok = sem("f_silu_ok"), sem("f_g_ok"), sem("f_gh_ok"), sem("f_gl_ok")
        dn_done, dn_out = sem("f_dn_done"), sem("f_dn_out")
        ND = KC * NG
        C_UP, C_UO, C_DN = 6, RING_UP, RING

        with nc.Block() as block:
            @block.sync
            def _(sp):
                def load(s, f):
                    sp.wait_ge(w_split[s], f + 1)
                    sp.dma_start(WR[s], (w_up[f], w_up[f + FB], w_down[f])[s]).then_inc(raw_in[s], 16)

                with sp.Fori(0, FB - 1) as f:
                    load(0, f + 1)
                    load(1, f + 1)
                    load(2, f)
                load(2, FB - 1)

            @block.gpsimd
            def _(pool):
                for s, credit in zip(w_split, (2, 2, 1)):
                    pool.sem_inc(s, credit)
                pool.sem_inc(w_hi, 2)
                pool.sem_inc(raw_in[0], 16)
                pool.sem_inc(raw_in[1], 16)

                def split(s, f, n):
                    pool.wait_ge(raw_in[s], f * 16 + 16)
                    if s < 2:
                        pool.wait_ge(up_done, f * 6 + (3 * s - 3 + C_UP))
                    else:
                        pool.wait_ge(dn_done, f * ND + 1)
                    pool.sem_inc(w_go, 1)
                    nc.gpsimd.tensor_copy(WH[:, s], WR[s]).then_inc(w_hi, 1)
                    pool.wait_ge(w_hi, n)
                    nc.gpsimd.tensor_tensor(WL[:, s], WR[s], WH[:, s].bitcast(F32), ALU.subtract).then_inc(w_split[s], 1)

                with pool.Fori(0, FB - 1) as f:
                    split(0, f + 1, f * 3 + 3)
                    split(1, f + 1, f * 3 + 4)
                    split(2, f, f * 3 + 5)
                split(2, FB - 1, 3 * FB)

            @block.tensor
            def _(pe):
                pe.sem_inc(up_done, C_UP)
                pe.sem_inc(dn_done, 1)

                def up_part(f):
                    for s in range(2):
                        pe.wait_ge(w_split[s], f + 2)
                        for g in range(NG):
                            n = NG * s + g
                            pe.wait_ge(up_out, f * 6 + (n - RING_UP + 1 + C_UO))
                            for k in range(KC):
                                m = three_pass(nc, up[:, n % RING_UP, 0:G], WH[:, s, k], WL[:, s, k],
                                               HH[:, k, g * G:(g + 1) * G], HL[:, k, g * G:(g + 1) * G], k, k == KC - 1)
                            m.then_inc(up_done, 1)

                def down_part(f):
                    pe.wait_ge(w_split[2], f + 2)
                    pe.wait_ge(gl_ok, f + 2)
                    for j in range(KC):
                        for g in range(NG):
                            n = NG * j + g
                            before = n - RING if n >= RING else max(m for m in range(ND) if m % RING == n) - ND
                            pe.wait_ge(dn_out, f * ND + (before + 1 + C_DN))
                            three_pass(nc, dn[:, n % RING, 0:G], WH[:, 2, j], WL[:, 2, j],
                                       GH[:, g * G:(g + 1) * G], GL[:, g * G:(g + 1) * G], 0, True).then_inc(dn_done, 1)

                up_part(0)
                with pe.Fori(0, FB - 1) as f:
                    up_part(f + 1)
                    down_part(f)
                down_part(FB - 1)

            @block.scalar
            def _(act):
                act.sem_inc(up_out, C_UO)
                with act.Fori(0, FB) as f:
                    for s in range(2):
                        act.wait_ge(g_ok, f + 1)
                        for g in range(NG):
                            n = NG * s + g
                            act.wait_ge(up_done, f * 6 + n + 1 + C_UP)
                            cols = slice(g * G, (g + 1) * G)
                            tap = CW[:, 1, bass.ds(f + s * FB, 1)]
                            bias = CW[:, 3, bass.ds(f + s * FB, 1)]
                            nc.scalar.activation(U[:, s, cols], up[:, n % RING_UP, 0:G], ACT.Copy)
                            nc.scalar.activation(C[:, s, cols], up[:, n % RING_UP, 0:G], ACT.Identity, scale=tap, bias=bias).then_inc(up_out, 1)
                        if s == 0:
                            act.wait_ge(taps, f * 8 + 4)
                            nc.scalar.activation(C[:, 0, :], C[:, 0, :], ACT.Silu).then_inc(silu_ok, 1)
                    act.wait_ge(g_ok, f + 2)
                    act.wait_ge(dn_done, f * ND + 1)
                    nc.scalar.activation(GH[:, :], GF[:, :], ACT.Copy).then_inc(gh_ok, 1)

            @block.vector
            def _(dve):
                dve.sem_inc(g_ok, 1)
                dve.sem_inc(gl_ok, 1)
                dve.sem_inc(dn_out, C_DN)

                def conv(s, f):
                    dve.wait_ge(up_out, f * 6 + (NG * (s + 1) + C_UO))
                    n = 0
                    for tap, src, dst in ((0, 0, 1), (2, 1, 0)):
                        for t0, t1 in RANGES:
                            w = t1 - t0 - 1
                            if n >= 2:
                                dve.wait_ge(taps, f * 8 + 4 * s + n - 1)
                            c = C[:, s, t0 + dst:t0 + dst + w]
                            nc.vector.scalar_tensor_tensor(c, U[:, s, t0 + src:t0 + src + w], CW[:, tap, bass.ds(f + s * FB, 1)],
                                                           c, ALU.mult, ALU.add).then_inc(taps, 1)
                            n += 1

                def gate(f):
                    dve.wait_ge(silu_ok, f + 1)
                    dve.wait_ge(taps, f * 8 + 8)
                    dve.wait_ge(gl_ok, f + 1)
                    nc.vector.tensor_tensor(GF[:, :], C[:, 0, :], C[:, 1, :], ALU.mult).then_inc(g_ok, 1)

                def low(f):
                    dve.wait_ge(gh_ok, f + 1)
                    nc.vector.tensor_tensor(GL[:, :], GF[:, :], GH[:, :].bitcast(F32), ALU.subtract).then_inc(gl_ok, 1)

                def add_down(f):
                    dve.wait_ge(dn_out, f * ND + C_DN)
                    for j in range(KC):
                        for g in range(NG):
                            n = NG * j + g
                            dve.wait_ge(dn_done, f * ND + n + 2)
                            for t0, t1, grp in split_groups(g):
                                x = X1[:, j, t0:t1]
                                m = nc.vector.scalar_tensor_tensor(x, dn[:, n % RING, t0 - g * G:t1 - g * G], MOD[:, 40 + j, grp:grp + 1], x, ALU.mult, ALU.add)
                            m.then_inc(dn_out, 1)

                conv(0, 0)
                conv(1, 0)
                gate(0)
                low(0)
                with dve.Fori(0, FB - 1) as f:
                    conv(0, f + 1)
                    add_down(f)
                    conv(1, f + 1)
                    gate(f + 1)
                    low(f + 1)
                add_down(FB - 1)


def phase5(nc, a, sem, ident, X1, y_prompt, y_sample):
    with ExitStack() as ctx:
        def sb(name, shape, dt=F32):
            return ctx.enter_context(nc.sbuf_tensor(name, shape, dt))

        Y = sb("y", [P, NT, D])
        junk = sb("junk5", [P, 2, D])
        FN = sb("final_gain", [P, D])
        SS, RS = sb("ss5", [P, NT]), sb("rs5", [P, NT])
        EPSB = sb("eps5", [P, 1])
        ps = ctx.enter_context(nc.psum_tensor("y_ps", [P, 4, 1024], F32))
        fn_in, yt, sq, yc, root, rs, st = (sem("y_gain_in"), sem("y_t"), sem("y_sq"), sem("y_copy"), sem("y_root"),
                                                   sem("y_rs"), sem("y_store"))
        set_ok = sem("y_set_ok")
        with nc.Block() as block:
            @block.sync
            def _(sp):
                sp.dma_start(FN[:, :], a["final_norm"].partition_broadcast(P)).then_inc(fn_in, 16)
                for t in range(NT):
                    sp.wait_ge(yc, t + 1)
                    sp.dma_start(y_prompt[0] if t == 0 else y_sample[0, (t - 1) * P:t * P, :], Y[:, t, :]).then_inc(st, 16)
                sp.wait_ge(st, 16 * NT)

            @block.tensor
            def _(pe):
                for t in range(NT):
                    if t >= 4:
                        pe.wait_ge(yc, t - 3)
                    for j in range(KC):
                        m = nc.tensor.transpose(ps[:, t % 4, j * P:(j + 1) * P], X1[:, j, t * P:(t + 1) * P], ident[:, :])
                    m.then_inc(yt, 1)

            @block.scalar
            def _(act):
                act.wait_ge(set_ok, 1)
                for t in range(NT):
                    act.wait_ge(yt, t + 1)
                    if t >= 2:
                        act.wait_ge(sq, t - 1)
                    nc.scalar.activation(junk[:, t % 2, :], ps[:, t % 4, :], ACT.Square, accum_out=SS[:, t:t + 1]).then_inc(sq, 1)
                    act.wait_ge(sq, t + 1)
                    nc.scalar.activation(RS[:, t:t + 1], SS[:, t:t + 1], ACT.Sqrt, scale=1.0 / D, bias=EPSB[:, 0:1]).then_inc(root, 1)

            @block.vector
            def _(dve):
                nc.vector.memset(EPSB[:, :], EPS).then_inc(set_ok, 1)
                dve.wait_ge(fn_in, 16)
                for t in range(NT):
                    dve.wait_ge(root, t + 1)
                    nc.vector.reciprocal(RS[:, t:t + 1], RS[:, t:t + 1]).then_inc(rs, 1)
                    dve.wait_ge(rs, t + 1)
                    nc.vector.scalar_tensor_tensor(Y[:, t, :], ps[:, t % 4, :], RS[:, t:t + 1], FN[:, :], ALU.mult, ALU.mult).then_inc(yc, 1)



_INS = ["x_prompt", "x_sample", "c", "cache_k", "cache_v", "state_hgrn", "c_ctx", "ada_w", "ada_b", "norm1", "norm2",
        "w_in", "q_norm", "k_norm", "hgrn_lb_logits", "hgrn_norm", "w_o", "w_up", "conv_w", "conv_b", "w_down", "final_norm"]
_OUTS = [(1, T_CTX, D), (1, T_LAT, D), (1, 1, T_CTX, NKV, HEAD), (1, 1, T_CTX, NKV, HEAD), (1, 1, 2, RH, P, P)]


def shape_constants():
    import numpy as np
    s, t = np.arange(P)[:, None], np.arange(P)[None, :]
    same = s // CH == t // CH
    mask = np.concatenate([same & (s <= t), same & (s >= t)], axis=1).astype(np.float32)
    half, grid_w = HEAD // 2, 64
    inv = (1.0 / (10000.0 ** (np.arange(0, half, 2, dtype=np.float32) / np.float32(half)))).astype(np.float32)
    n = np.arange(T_LAT)
    row, col = (n // grid_w).astype(np.float32)[:, None] * inv, (n % grid_w).astype(np.float32)[:, None] * inv
    cos = np.concatenate([np.cos(row), np.cos(row), np.cos(col), np.cos(col)], axis=1).astype(np.float32)
    sin = np.concatenate([-np.sin(row), np.sin(row), -np.sin(col), np.sin(col)], axis=1).astype(np.float32)
    return {"c_ident": np.eye(P, dtype=np.float32), "c_mask": mask, "c_cos": cos, "c_sin": sin}


def kernel(**inputs):
    import numpy as np
    import concourse.bacc as bacc
    from concourse.bass_utils import run_bass_kernel_spmd

    nc = bacc.Bacc("TRN2", target_bir_lowering=False, num_devices=1)
    arrays, aps = {}, {}
    given = {n: np.ascontiguousarray(inputs[n]) for n in _INS}
    given.update(shape_constants())
    for n, v in given.items():
        arrays["in_" + n] = v
        aps[n] = nc.dram_tensor("in_" + n, v.shape, F32, kind="ExternalInput").ap()
    outs = [nc.dram_tensor(f"out_{i}", s, F32, kind="ExternalOutput").ap() for i, s in enumerate(_OUTS)]
    build(nc, aps, outs)
    r = run_bass_kernel_spmd(nc, [arrays], core_ids=[0])
    return tuple(r.results[0][f"out_{i}"] for i in range(len(_OUTS)))
```
